# Optimizing a Trainium2 kernel written in Bass

```python
import jax
import jax.numpy as jnp
from jax import lax
import numpy as np

D_MODEL = 1024
BATCH = 1
SEQ = 1024
DEPTH = 1
DEC_BATCH = 8
DEC_SEQ = 1
PAST_LEN = 256
PAGE_SIZE = 128

CHUNK = 128
D_GMLP = 1024
GMLP_GROUPS = 8
GMLP_GW = D_GMLP // GMLP_GROUPS
N_HEADS = 16
KV_HEADS = 2
Q_PER_KV = N_HEADS // KV_HEADS
HEAD_DIM = 64
D_ATTN = N_HEADS * HEAD_DIM
D_KV = KV_HEADS * HEAD_DIM
CMP_BLOCK = 32
CMP_STRIDE = 16
CMP_RATIO = CMP_BLOCK // CMP_STRIDE
CMP_HIDDEN = 2 * HEAD_DIM
SEL_BLOCK = 64
N_SELECT = 16
WINDOW = 512
Q_BLOCK = 128
FORCE_BONUS = 1e4
N_KV_SLOTS = 4
N_EXPERTS = 16
N_EXPERT_GROUPS = 4
EXPERTS_PER_GROUP = N_EXPERTS // N_EXPERT_GROUPS
TOP_K = 2
D_EXPERT = 512
PROJ_SIZES = (D_GMLP, D_GMLP, D_ATTN) + (D_KV,) * 6 + (3 * N_HEADS, D_MODEL, D_MODEL)
D_IN = sum(PROJ_SIZES)

kernel_name = "gmlp_nsa_gated_hybrid_moe_step"

def layer_norm(x, g, b, eps=1e-5):
    xf = x.astype(jnp.float32)
    mu = jnp.mean(xf, -1, keepdims=True)
    var = jnp.mean(jnp.square(xf - mu), -1, keepdims=True)
    return ((xf - mu) * lax.rsqrt(var + eps) * g.astype(jnp.float32) + b.astype(jnp.float32)).astype(x.dtype)

def masked_softmax(s, mask):
    s = jnp.where(mask, s.astype(jnp.float32), -1e30)
    m = jnp.max(s, -1, keepdims=True)
    p = jnp.where(mask, jnp.exp(s - m), 0.0)
    return p / jnp.maximum(jnp.sum(p, -1, keepdims=True), 1e-30)

def split_projection(x, w):
    cuts = [int(c) for c in np.cumsum(PROJ_SIZES)[:-1]]
    return jnp.split(x @ w, cuts, axis=-1)

def heads_kv(t):
    return t.reshape(t.shape[:2] + (KV_HEADS, HEAD_DIM))

def heads_q(t):
    return t.reshape(t.shape[:2] + (KV_HEADS, Q_PER_KV, HEAD_DIM))

def nsa_gates(g):
    return jax.nn.sigmoid(g).reshape(g.shape[:2] + (KV_HEADS, Q_PER_KV, 3))

def gmlp_mix(u, v, w_s, b_s):
    B, T, _ = v.shape
    n_chunks = -(-T // CHUNK)
    vp = jnp.pad(v, ((0, 0), (0, n_chunks * CHUNK - T), (0, 0)))
    vp = vp.reshape(B, n_chunks, CHUNK, GMLP_GROUPS, GMLP_GW)
    causal = jnp.tril(jnp.ones((CHUNK, CHUNK), bool))
    w = jnp.where(causal[None], w_s, 0.0)
    mixed = jnp.einsum('gts,bcsgd->bctgd', w, vp) + b_s.T[None, None, :, :, None]
    return u * mixed.reshape(B, n_chunks * CHUNK, D_GMLP)[:, :T]

def gmlp_branch(u, v, ln_g, ln_b, w_s, b_s):
    vn = layer_norm(jax.nn.gelu(v), ln_g, ln_b)
    return gmlp_mix(jax.nn.gelu(u), vn, w_s, b_s), vn

def compress(k, pos, w1, w2):
    B, T = k.shape[:2]
    n_sub = T // CMP_STRIDE
    n_cmp = n_sub - CMP_RATIO + 1
    sub = k[:, :n_sub * CMP_STRIDE].reshape(B, n_sub, CMP_STRIDE, KV_HEADS, HEAD_DIM)
    w1b = w1.reshape(CMP_BLOCK, HEAD_DIM, CMP_HIDDEN)
    w1r = w1.reshape(CMP_RATIO, CMP_STRIDE, HEAD_DIM, CMP_HIDDEN)
    hid = jnp.einsum('sd,sdf->f', pos, w1b)
    for r in range(CMP_RATIO):
        hid = hid + jnp.einsum('bnshd,sdf->bnhf', sub[:, r:r + n_cmp], w1r[r])
    return jax.nn.gelu(hid) @ w2

def sel_blocks(k, n_sel):
    B, T = k.shape[:2]
    kp = jnp.pad(k, ((0, 0), (0, n_sel * SEL_BLOCK - T), (0, 0), (0, 0)))
    return kp.reshape(B, n_sel, SEL_BLOCK, KV_HEADS, HEAD_DIM).transpose(0, 3, 1, 2, 4)

def block_overlap(n_cmp, n_sel):
    c0 = np.arange(n_cmp) * CMP_STRIDE
    s0 = np.arange(n_sel) * SEL_BLOCK
    ov = (c0[:, None] < s0[None, :] + SEL_BLOCK) & (c0[:, None] + CMP_BLOCK > s0[None, :])
    return jnp.asarray(ov.astype(np.float32))

def nsa_context(k_cm, v_cm, k_sl, v_sl, pos_c, w1_c, w2_c):
    T = k_cm.shape[1]
    kc = compress(k_cm, pos_c[0], w1_c[0], w2_c[0])
    vc = compress(v_cm, pos_c[1], w1_c[1], w2_c[1])
    n_sel = -(-T // SEL_BLOCK)
    return (kc, vc, sel_blocks(k_sl, n_sel), sel_blocks(v_sl, n_sel), block_overlap(kc.shape[1], n_sel))

def nsa_block(q, qpos, gates, ctx, kw, vw, wpos):
    kc, vc, kb, vb, overlap = ctx
    B, Q = q.shape[:2]
    n_cmp, n_sel = kc.shape[1], kb.shape[2]
    scale = HEAD_DIM ** -0.5
    cmp_end = jnp.arange(n_cmp) * CMP_STRIDE + (CMP_BLOCK - 1)
    m_c = (cmp_end[None, :] <= qpos[:, None])[None, :, None, None, :]
    p_c = masked_softmax(jnp.einsum('bqkgd,bnkd->bqkgn', q, kc) * scale, m_c)
    o_c = jnp.einsum('bqkgn,bnkd->bqkgd', p_c.astype(vc.dtype), vc)
    imp = jnp.einsum('bqkn,nj->bqkj', jnp.sum(p_c, 3), overlap)
    blk = jnp.arange(n_sel)[None, :]
    cur = (qpos // SEL_BLOCK)[:, None]
    forced = (blk == 0) | (blk == cur) | (blk == cur - 1)
    valid = blk * SEL_BLOCK <= qpos[:, None]
    score = jnp.where(valid[None, :, None, :], imp + jnp.where(forced, FORCE_BONUS, 0.0)[None, :, None, :], -1e30)
    n_top = min(N_SELECT, n_sel)
    _, idx = lax.top_k(score, n_top)
    idx_t = idx.transpose(0, 2, 1, 3).reshape(B, KV_HEADS, Q * n_top)
    gather = jax.vmap(jax.vmap(lambda blocks, i: blocks[i]))
    ks = gather(kb, idx_t).reshape(B, KV_HEADS, Q, n_top * SEL_BLOCK, HEAD_DIM)
    vs = gather(vb, idx_t).reshape(B, KV_HEADS, Q, n_top * SEL_BLOCK, HEAD_DIM)
    tok = (idx[..., None] * SEL_BLOCK + jnp.arange(SEL_BLOCK)).reshape(B, Q, KV_HEADS, 1, n_top * SEL_BLOCK)
    m_s = tok <= qpos[None, :, None, None, None]
    p_s = masked_softmax(jnp.einsum('bqkgd,bkqmd->bqkgm', q, ks) * scale, m_s)
    o_s = jnp.einsum('bqkgm,bkqmd->bqkgd', p_s.astype(vs.dtype), vs)
    rel = qpos[:, None] - wpos[None, :]
    m_w = ((rel >= 0) & (rel < WINDOW) & (wpos[None, :] >= 0))[None, :, None, None, :]
    p_w = masked_softmax(jnp.einsum('bqkgd,bwkd->bqkgw', q, kw) * scale, m_w)
    o_w = jnp.einsum('bqkgw,bwkd->bqkgd', p_w.astype(vw.dtype), vw)
    return gates[..., 0:1] * o_c + gates[..., 1:2] * o_s + gates[..., 2:3] * o_w

def nsa_prompt(q, gates, ctx, k_wn, v_wn):
    B, T = q.shape[:2]
    pad = ((0, 0), (WINDOW, 0), (0, 0), (0, 0))
    kwp, vwp = jnp.pad(k_wn, pad), jnp.pad(v_wn, pad)
    span = WINDOW + Q_BLOCK

    def one_block(i):
        s = i * Q_BLOCK
        qb = lax.dynamic_slice_in_dim(q, s, Q_BLOCK, axis=1)
        gb = lax.dynamic_slice_in_dim(gates, s, Q_BLOCK, axis=1)
        kwb = lax.dynamic_slice_in_dim(kwp, s, span, axis=1)
        vwb = lax.dynamic_slice_in_dim(vwp, s, span, axis=1)
        return nsa_block(qb, s + jnp.arange(Q_BLOCK), gb, ctx, kwb, vwb, s - WINDOW + jnp.arange(span))

    o = lax.map(one_block, jnp.arange(T // Q_BLOCK))
    return jnp.moveaxis(o, 0, 1).reshape(B, T, D_ATTN)

def merge_branches(a, o, g_a, g_b, w_pa, w_pb, w_o):
    y = jax.nn.sigmoid(g_a) * (a @ w_pa) + jax.nn.sigmoid(g_b) * (o @ w_pb)
    return y @ w_o

def moe_ffn(x, w_router, b_router, w_gate, w_up, w_down):
    shape = x.shape
    xt = x.reshape(-1, D_MODEL)
    n_tok = xt.shape[0]
    aff = jax.nn.sigmoid((xt @ w_router).astype(jnp.float32))
    grp = (aff + b_router.astype(jnp.float32)).reshape(n_tok, N_EXPERT_GROUPS, EXPERTS_PER_GROUP)
    g_sel = jnp.argmax(jnp.sum(lax.top_k(grp, TOP_K)[0], -1), -1)
    in_grp = jnp.take_along_axis(grp, g_sel[:, None, None], axis=1)[:, 0]
    _, loc = lax.top_k(in_grp, TOP_K)
    eid = g_sel[:, None] * EXPERTS_PER_GROUP + loc
    wts = jnp.take_along_axis(aff, eid, axis=1)
    wts = wts / jnp.sum(wts, -1, keepdims=True)
    flat_e = eid.reshape(-1)
    order = jnp.argsort(flat_e)
    tok = order // TOP_K
    xs = xt[tok]
    sizes = jnp.bincount(flat_e, length=N_EXPERTS).astype(jnp.int32)
    h = jax.nn.silu(lax.ragged_dot(xs, w_gate, sizes)) * lax.ragged_dot(xs, w_up, sizes)
    out = lax.ragged_dot(h, w_down, sizes) * wts.reshape(-1)[order][:, None].astype(xt.dtype)
    return jax.ops.segment_sum(out, tok, num_segments=n_tok).reshape(shape)

def setup_inputs(seed: int = 0) -> dict:
    key = jax.random.key(seed)
    ks = jax.random.split(key, 32)
    beta = (8.0 * DEPTH) ** -0.25
    n_pages = PAST_LEN // PAGE_SIZE
    n_phys = (5 * DEC_BATCH * n_pages) // 4
    win_buf = min(WINDOW, PAST_LEN)

    def nrm(k, shape, scale):
        return jax.random.normal(k, shape, jnp.float32) * scale

    bounds = np.cumsum((0,) + PROJ_SIZES)
    col_scale = np.ones((D_IN,), np.float32)
    for i in (4, 6, 8):
        col_scale[bounds[i]:bounds[i + 1]] = beta
    perm = jax.random.permutation(ks[3], n_phys)
    return {
        'x_prompt': nrm(ks[0], (BATCH, SEQ, D_MODEL), 1.0),
        'x_sample': nrm(ks[1], (DEC_BATCH, DEC_SEQ, D_MODEL), 1.0),
        'cache_kv': nrm(ks[2], (n_phys, DEPTH, PAGE_SIZE, N_KV_SLOTS, KV_HEADS, HEAD_DIM), 1.0),
        'cache_win': nrm(ks[4], (DEC_BATCH, DEPTH, win_buf, 2, KV_HEADS, HEAD_DIM), 1.0),
        'page_table': perm[:DEC_BATCH * n_pages].reshape(DEC_BATCH, n_pages).astype(jnp.int32),
        'w_in': nrm(ks[5], (DEPTH, D_MODEL, D_IN), D_MODEL ** -0.5) * jnp.asarray(col_scale),
        'gmlp_ln_g': 1.0 + nrm(ks[6], (DEPTH, D_GMLP), 0.02),
        'gmlp_ln_b': nrm(ks[7], (DEPTH, D_GMLP), 0.02),
        'gmlp_ws': nrm(ks[8], (DEPTH, GMLP_GROUPS, CHUNK, CHUNK), CHUNK ** -0.5),
        'gmlp_bs': 1.0 + nrm(ks[9], (DEPTH, GMLP_GROUPS, CHUNK), 0.02),
        'cmp_pos': nrm(ks[10], (DEPTH, 2, CMP_BLOCK, HEAD_DIM), 0.1),
        'cmp_w1': nrm(ks[11], (DEPTH, 2, CMP_BLOCK * HEAD_DIM, CMP_HIDDEN), (CMP_BLOCK * HEAD_DIM) ** -0.5),
        'cmp_w2': nrm(ks[12], (DEPTH, 2, CMP_HIDDEN, HEAD_DIM), CMP_HIDDEN ** -0.5),
        'w_branch_a': nrm(ks[13], (DEPTH, D_GMLP, D_MODEL), beta * D_GMLP ** -0.5),
        'w_branch_b': nrm(ks[14], (DEPTH, D_ATTN, D_MODEL), beta * D_ATTN ** -0.5),
        'w_out': nrm(ks[15], (DEPTH, D_MODEL, D_MODEL), beta * D_MODEL ** -0.5),
        'ln1_g': 1.0 + nrm(ks[16], (DEPTH, D_MODEL), 0.02),
        'ln1_b': nrm(ks[17], (DEPTH, D_MODEL), 0.02),
        'ln2_g': 1.0 + nrm(ks[18], (DEPTH, D_MODEL), 0.02),
        'ln2_b': nrm(ks[19], (DEPTH, D_MODEL), 0.02),
        'w_router': nrm(ks[20], (D_MODEL, N_EXPERTS), D_MODEL ** -0.5),
        'b_router': nrm(ks[21], (N_EXPERTS,), 0.01),
        'w_gate': nrm(ks[22], (DEPTH, N_EXPERTS, D_MODEL, D_EXPERT), D_MODEL ** -0.5),
        'w_up': nrm(ks[23], (DEPTH, N_EXPERTS, D_MODEL, D_EXPERT), D_MODEL ** -0.5),
        'w_down': nrm(ks[24], (DEPTH, N_EXPERTS, D_EXPERT, D_MODEL), beta * D_EXPERT ** -0.5),
    }

def reference(x_prompt, x_sample, cache_kv, cache_win, page_table, w_in, gmlp_ln_g, gmlp_ln_b, gmlp_ws, gmlp_bs,
              cmp_pos, cmp_w1, cmp_w2, w_branch_a, w_branch_b, w_out, ln1_g, ln1_b, ln2_g, ln2_b,
              w_router, b_router, w_gate, w_up, w_down):
    alpha = (2.0 * DEPTH) ** 0.25
    n_past = page_table.shape[1] * PAGE_SIZE
    n_dec, t_dec = x_sample.shape[:2]
    wb = cache_win.shape[2]
    xp, xs = x_prompt, x_sample
    kv_p, win_p, kv_s, win_s, gv_s = [], [], [], [], []
    for l in range(DEPTH):
        u, v, q, *kv_new, g_nsa, g_a, g_b = split_projection(xp, w_in[l])
        a, _ = gmlp_branch(u, v, gmlp_ln_g[l], gmlp_ln_b[l], gmlp_ws[l], gmlp_bs[l])
        k_cm, v_cm, k_sl, v_sl, k_wn, v_wn = [heads_kv(t) for t in kv_new]
        ctx = nsa_context(k_cm, v_cm, k_sl, v_sl, cmp_pos[l], cmp_w1[l], cmp_w2[l])
        o = nsa_prompt(heads_q(q), nsa_gates(g_nsa), ctx, k_wn, v_wn)
        mix = merge_branches(a, o, g_a, g_b, w_branch_a[l], w_branch_b[l], w_out[l])
        xp = layer_norm(alpha * xp + mix, ln1_g[l], ln1_b[l])
        xp = layer_norm(alpha * xp + moe_ffn(xp, w_router, b_router, w_gate[l], w_up[l], w_down[l]), ln2_g[l], ln2_b[l])
        kv_p.append(jnp.stack([k_cm, v_cm, k_sl, v_sl], axis=2))
        win_p.append(jnp.stack([k_wn, v_wn], axis=2)[:, -min(WINDOW, k_wn.shape[1]):])

        u, v, q, *kv_new, g_nsa, g_a, g_b = split_projection(xs, w_in[l])
        a, vn = gmlp_branch(u, v, gmlp_ln_g[l], gmlp_ln_b[l], gmlp_ws[l], gmlp_bs[l])
        new = [heads_kv(t) for t in kv_new]
        new_kv = jnp.stack(new[:4], axis=2)
        past = cache_kv[page_table, l].reshape(n_dec, n_past, N_KV_SLOTS, KV_HEADS, HEAD_DIM)
        full = jnp.concatenate([past, new_kv.astype(past.dtype)], axis=1)
        ctx = nsa_context(full[:, :, 0], full[:, :, 1], full[:, :, 2], full[:, :, 3], cmp_pos[l], cmp_w1[l], cmp_w2[l])
        win = jnp.concatenate([cache_win[:, l], jnp.stack(new[4:], axis=2).astype(cache_win.dtype)], axis=1)
        qpos = n_past + jnp.arange(t_dec)
        wpos = n_past - wb + jnp.arange(wb + t_dec)
        o = nsa_block(heads_q(q), qpos, nsa_gates(g_nsa), ctx, win[:, :, 0], win[:, :, 1], wpos)
        o = o.reshape(n_dec, t_dec, D_ATTN)
        mix = merge_branches(a, o, g_a, g_b, w_branch_a[l], w_branch_b[l], w_out[l])
        xs = layer_norm(alpha * xs + mix, ln1_g[l], ln1_b[l])
        xs = layer_norm(alpha * xs + moe_ffn(xs, w_router, b_router, w_gate[l], w_up[l], w_down[l]), ln2_g[l], ln2_b[l])
        kv_s.append(new_kv)
        win_s.append(win[:, -wb:])
        gv_s.append(vn)
    kv_rows_prompt = jnp.stack(kv_p, axis=1)
    win_prompt = jnp.stack(win_p, axis=1)
    kv_rows_sample = jnp.stack(kv_s, axis=1)
    win_sample = jnp.stack(win_s, axis=1)
    gmlp_v_sample = jnp.stack(gv_s, axis=1)
    return (xp, xs, kv_rows_prompt, win_prompt, kv_rows_sample, win_sample, gmlp_v_sample)


_drawn_inputs = setup_inputs


def setup_inputs(seed=0):
    import zlib

    import numpy as np

    out = dict(_drawn_inputs(seed))
    spreads = {}
    factors = {'gmlp_ln_g': 7.376,
     'gmlp_ln_b': 21.147,
     'cmp_pos': 3.271,
     'ln2_g': 24.328,
     'ln2_b': 23.968,
     'gmlp_bs': 8.0,
     'cache_kv': 4.039}
    for name, (base, spread) in spreads.items():
        noise = np.random.default_rng([zlib.crc32(name.encode()), seed]).standard_normal(out[name].shape)
        drawn = base * np.exp(spread * noise) if base else spread * noise
        out[name] = jnp.asarray(drawn.astype(out[name].dtype))
    for name, factor in factors.items():
        out[name] = (out[name] * factor).astype(out[name].dtype)
    return out
```

```python
from contextlib import ExitStack

import concourse.bass as bass
import numpy as np
from concourse import mybir
from concourse.alu_op_type import AluOpType as ALU

F32 = mybir.dt.float32
F32R = mybir.dt.float32r
BF16 = mybir.dt.bfloat16
I32 = mybir.dt.int32
U32 = mybir.dt.uint32
ACT = mybir.ActivationFunctionType
AX = mybir.AxisListType

P = 128
DM = 1024
SEQ = 1024
NB = 8
NTOK = SEQ + NB
TT = SEQ // P
NT9 = TT + 1
KT = DM // P
NH, NKV, HD = 16, 2, 64
QPK = NH // NKV
CMP_STRIDE, CMP_BLOCK = 16, 32
NCMP = SEQ // CMP_STRIDE - 1
PAST, PAGE = 256, 128
NPAGE = PAST // PAGE
NPG = NB * NPAGE
CKEYS = NB * PAST
SCMP = PAST // CMP_STRIDE - 1
WINDOW = 512
WBLK = WINDOW // P
NEG = -1e30
SCALE = HD ** -0.5
ALPHA = 2.0 ** 0.25
EPS = 1e-5
NE, NG, EPG = 16, 4, 4
FE = 512
FT = FE // P
NPAIR = 2 * NTOK
NROWS = NPAIR + P
MAXT = (NPAIR + NE * (P - 1)) // P + 2
NTC = NTOK // P + 1
COL_V, COL_Q, COL_KV = 1024, 2048, 3072
COL_GA, COL_GB = 3888, 4912
KVW = 6 * 128 + 3 * NH
KVH = KVW // 2


def rows_of(t):
    return P if t < TT else NB


def span(t):
    return slice(t * P, t * P + rows_of(t))


class Memory:

    def __init__(self, nc, ctx):
        self.nc, self.ctx, self.sems = nc, ctx, []
        self.at_R3 = nc.sbuf_base
        self.R3 = self.sb("region_3", [P, 3 * KT * NTOK])
        self.RO = self.R3[:, KT * NTOK:2 * KT * NTOK]
        self.RA = self.R3[:, 2 * KT * NTOK:3 * KT * NTOK]
        self.RK = self.sb("region_k", [P, 8496])
        self.at_RW = nc.sbuf_base
        self.RW = self.sb("region_w", [P, 16384])
        self.ps = ctx.enter_context(nc.psum_tensor("ps", [P, 8, 512], F32))
        self.ident = self.sb("ident", [P, P])
        self.gates = self.sb("gates", [P, NT9, 3 * NH])
        self.xT = view(self.R3, 0, KT, NTOK)
        self.qT = view(self.RO, 0, KT, NTOK)
        self.aT = view(self.RA, 0, KT, NTOK)
        self.kT = view(self.RK, 0, 4, NTOK)
        self.vv = view(self.RK, 4 * NTOK, NT9, 256)
        self.kvst = view(self.RK, 4 * NTOK + NT9 * 256, 2, KVW)
        self.small = self.sb("small", [P, 1408])
        self.k_stacks = self.parts("key_stacks", self.at_RW + 4 * 6144, 8 * SEQ).rearrange(
            "p (a g h n) -> p a g h n", a=2, g=NKV, h=2)
        self.kc_stacks = self.sb("compressed_key_stacks", [P, NKV, 2, 64], F32R)
        self.q_stacks = self.parts("query_stacks", self.at_RW + 4 * 14336, 2 * SEQ).rearrange("p (g n) -> p g n", g=NKV)
        self.kcT = self.sb("kcT", [P, 2 * P])
        self.vc = self.sb("vc", [P, 2, P])
        self.gs = self.sb("gates_sample_rows", [P, 3])
        self.page_ids = self.sb("page_ids", [1, NPG], I32)
        self.identb = self.sb("ident_bf16", [P, P], BF16)
        self.mask_diag = self.sb("mask_diag", [P, P], BF16)
        self.mask_edge = self.sb("mask_edge", [P, P], BF16)
        self.mask_cmp = self.sb("mask_cmp", [P, 56 + NCMP], BF16)
        self.x1 = [self.RW[:, t * DM:(t + 1) * DM] for t in range(TT)] + [self.small[0:NB, 0:DM]]
        self.aff = self.small[:, 1024:1024 + NT9 * NE].rearrange("p (t e) -> p t e", e=NE)
        self.pair_w = self.small[:, 1168:1168 + 2 * NT9].rearrange("p (t c) -> p t c", c=2)
        self.sem_wout, self.sem_expert, self.sem_stored = (
            ctx.enter_context(nc.semaphore(n)) for n in ("w_out_in", "expert_weights_in", "rows_stored"))
        self.mhalf = self.sb("minus_half", [P, 1])
        self.table = self.sb("tile_table", [1, 3 * MAXT + NE + 1], I32)
        self.slots = self.sb("slots", [P, 2 * NT9], U32)
        self.xs_dram = nc.dram_tensor("dispatched", [NROWS, DM], F32, kind="Internal").ap()
        self.ys_dram = nc.dram_tensor("expert_out", [NROWS, DM], F32, kind="Internal").ap()
        self.gate_dram = nc.dram_tensor("gate_scratch", [NB, 3 * NH], F32, kind="Internal").ap()

    def sb(self, name, shape, dt=F32):
        return self.ctx.enter_context(self.nc.sbuf_tensor(name, shape, dt))

    def parts(self, name, offset, n):
        return self.nc.alloc_sbuf_tensor_at(name, [P, n], F32R, offset=offset)[:]

    def sem(self, name):
        self.sems.append(self.nc.alloc_semaphore(name))
        return self.sems[-1]

    def clear_semaphores(self):
        self.nc.clear_and_free_semaphores(self.sems)
        self.sems = []
        self.nc.all_engine_barrier()


def view(region, offset, a, b, parts=P):
    return region[0:parts, offset:offset + a * b].rearrange("p (a b) -> p a b", a=a)


def load_and_turn_x(nc, m, io):
    xst = view(m.RK, 0, 2, DM)
    s_in = [m.sem("x_in0"), m.sem("x_in1")]
    s_turned, s_kept = m.sem("x_turned"), m.sem("x_kept")
    s_id0, s_id = m.sem("ident_clear"), m.sem("ident_ready")
    s_m0, s_m = m.sem("masks_clear"), m.sem("masks_ready")
    xp = io["x_prompt"].rearrange("a (t p) d -> p (a t) d", p=P)
    xs = io["x_sample"].rearrange("b t d -> (b t) d")
    with nc.Block() as block:

        @block.sync
        def _(sp):
            for t in range(NT9):
                if t >= 2:
                    sp.wait_ge(s_turned, t - 1)
                src = xp[:, t, :] if t < TT else xs
                sp.dma_start(xst[0:rows_of(t), t % 2, :], src).then_inc(s_in[t % 2], 16)

        @block.gpsimd
        def _(pool):
            nc.gpsimd.memset(m.ident[:], 0.0).then_inc(s_id0, 1)
            pool.wait_ge(s_id0, 1)
            nc.gpsimd.affine_select(out=m.ident[:], in_=m.ident[:], compare_op=ALU.not_equal, fill=1.0,
                                    base=0, pattern=[[-1, P]], channel_multiplier=1).then_inc(s_id, 1)
            pool.wait_ge(s_id, 1)
            nc.gpsimd.tensor_copy(m.identb[:], m.ident[:])
            nc.gpsimd.memset(m.mhalf[:], -0.5)
            for mask in (m.mask_diag, m.mask_edge, m.mask_cmp):
                nc.gpsimd.memset(mask[:], 0.0).then_inc(s_m0, 1)
            pool.wait_ge(s_m0, 3)
            nc.gpsimd.affine_select(out=m.mask_diag[:], in_=m.mask_diag[:], compare_op=ALU.is_ge, fill=NEG,
                                    base=0, pattern=[[-1, P]], channel_multiplier=1)
            nc.gpsimd.affine_select(out=m.mask_edge[:], in_=m.mask_edge[:], compare_op=ALU.is_gt, fill=NEG,
                                    base=0, pattern=[[1, P]], channel_multiplier=-1)
            nc.gpsimd.affine_select(out=m.mask_cmp[:], in_=m.mask_cmp[:], compare_op=ALU.is_ge, fill=NEG,
                                    base=56 * CMP_STRIDE - (CMP_BLOCK - 1), pattern=[[-CMP_STRIDE, 56 + NCMP]],
                                    channel_multiplier=1).then_inc(s_m, 1)
            pool.wait_ge(s_m, 1)

        @block.tensor
        def _(pe):
            pe.wait_ge(s_id, 1)
            for t in range(NT9):
                n, bank = rows_of(t), 2 * (t % 2)
                pe.wait_ge(s_in[t % 2], 16 * (t // 2 + 1))
                if t >= 2:
                    pe.wait_ge(s_kept, t - 1)
                for k in range(KT):
                    out = m.ps[:, bank + k // 4, (k % 4) * P:(k % 4) * P + n]
                    last = nc.tensor.transpose(out, xst[0:n, t % 2, k * P:(k + 1) * P], m.ident[0:n, 0:n])
                last.then_inc(s_turned, 1)

        @block.vector
        def _(dve):
            for t in range(NT9):
                dve.wait_ge(s_turned, t + 1)
                bank = 2 * (t % 2)
                src = m.ps[:, bank:bank + 2, :].rearrange("p b (k c) -> p (b k) c", k=4)[:, :, 0:rows_of(t)]
                nc.vector.tensor_copy(m.xT[:, :, span(t)], src).then_inc(s_kept, 1)


def project_kv(nc, m, io):
    wkv = view(m.RW, 0, KT, KVW)
    st = m.kvst
    s_w, s_proj, s_row, s_gate = (m.sem(n) for n in ("kv_w", "kv_projected", "kv_rows_staged", "kv_gates"))
    s_vv, s_turned, s_kept = m.sem("kv_values"), m.sem("kv_turned"), m.sem("kv_kept")
    s_out = [m.sem("kv_out0"), m.sem("kv_out1")]
    s_gd, s_gw = m.sem("gates_bounced"), m.sem("gates_scattered")
    s_win = m.sem("win_sample_out")
    kvp = io["kv_rows_prompt"].rearrange("a l (t p) s h d -> p (a l t) (s h d)", p=P)
    kvs = io["kv_rows_sample"].rearrange("b l t s h d -> (b l t) (s h d)")
    winp = io["win_prompt"].rearrange("a l (t p) s h d -> p (a l t) (s h d)", p=P)
    wins = io["win_sample"].rearrange("b l w s h d -> b (l w) (s h d)")
    cwin = io["cache_win"].rearrange("b l w s h d -> b (l w) (s h d)")
    w_in = io["w_in"].rearrange("l (k p) n -> p (l k) n", p=P)
    outs = [0, 0]

    with nc.Block() as block:

        @block.sync
        def _(sp):
            for h in range(2):
                sp.dma_start(wkv[:, :, h * KVH:(h + 1) * KVH],
                             w_in[:, :, COL_KV + h * KVH:COL_KV + (h + 1) * KVH]).then_inc(s_w, 16)
            sp.dma_start(wins[:, 0:PAST - 1, :], cwin[:, 1:PAST, :]).then_inc(s_win, 16)
            for t in range(NT9):
                n, b = rows_of(t), t % 2
                sp.wait_ge(s_row, t + 1)
                dst = kvp[:, t, :] if t < TT else kvs
                sp.dma_start(dst, st[0:n, b, 0:512]).then_inc(s_out[b], 16)
                outs[b] += 16
                if t >= TT // 2:
                    dst = winp[:, t - TT // 2, :] if t < TT else wins[:, PAST - 1, :]
                    sp.dma_start(dst, st[0:n, b, 512:768]).then_inc(s_out[b], 16)
                    outs[b] += 16
            sp.wait_ge(s_gate, NT9)
            sp.dma_start(m.gate_dram, m.gates[0:NB, TT, :]).then_inc(s_gd, 16)
            sp.wait_ge(s_gd, 16)
            for h in range(NH):
                sp.dma_start(m.gs[h * NB:(h + 1) * NB, :], m.gate_dram[:, 3 * h:3 * h + 3]).then_inc(s_gw, 16)
            for b in range(2):
                sp.wait_ge(s_out[b], outs[b])
            sp.wait_ge(s_win, 16)
            sp.wait_ge(s_gw, 16 * NH)

        @block.tensor
        def _(pe):
            def turn(t):
                n = rows_of(t)
                pe.wait_ge(s_row, t + 1)
                if t >= 2:
                    pe.wait_ge(s_kept, t - 1)
                for c, col in enumerate((0, 128, 256, 512)):
                    last = nc.tensor.transpose(m.ps[:, 6 + t % 2, c * P:c * P + n], st[0:n, t % 2, col:col + P],
                                               m.ident[0:n, 0:n])
                last.then_inc(s_turned, 1)

            pe.wait_ge(s_w, 32)
            for t in range(NT9):
                n = rows_of(t)
                if t >= 2:
                    pe.wait_ge(s_row, t - 1)
                for h in range(2):
                    for k in range(KT):
                        last = nc.tensor.matmul(m.ps[0:n, 2 * (t % 2) + h, 0:KVH], m.xT[:, k, span(t)],
                                                wkv[:, k, h * KVH:(h + 1) * KVH], start=(k == 0), stop=(k == KT - 1))
                last.then_inc(s_proj, 1)
                if t >= 1:
                    turn(t - 1)
            turn(NT9 - 1)

        @block.scalar
        def _(act):
            for t in range(NT9):
                n, b = rows_of(t), t % 2
                act.wait_ge(s_proj, t + 1)
                if t >= 2:
                    act.wait_ge(s_turned, t - 1)
                    done = 16 * ((t - 2) // 2 + 1) + 16 * sum(1 for u in range(b, t - 1, 2) if u >= TT // 2)
                    act.wait_ge(s_out[b], done)
                    act.wait_ge(s_vv, t - 1)
                src = m.ps[0:n, 2 * b:2 * b + 2, 0:KVH]
                nc.scalar.copy(st[0:n, b, :].rearrange("p (h c) -> p h c", h=2), src).then_inc(s_row, 1)
                act.wait_ge(s_row, t + 1)
                nc.scalar.activation(m.gates[0:n, t, :], st[0:n, b, 768:KVW], ACT.Sigmoid).then_inc(s_gate, 1)

        @block.vector
        def _(dve):
            for t in range(NT9):
                n, b = rows_of(t), t % 2
                dve.wait_ge(s_row, t + 1)
                src = st[0:n, b, 384:896 - 128].rearrange("p (a c) -> p a c", c=P)[:, 0:3:2, :]
                nc.vector.tensor_copy(m.vv[0:n, t, :].rearrange("p (a c) -> p a c", a=2), src).then_inc(s_vv, 1)
                dve.wait_ge(s_turned, t + 1)
                src = m.ps[:, 6 + b, :].rearrange("p (a c) -> p a c", a=4)[:, :, 0:n]
                nc.vector.tensor_copy(m.kT[:, :, span(t)], src).then_inc(s_kept, 1)


def project_q(nc, m, io):
    wq = [view(m.RA, 0, KT, P), view(m.RA, KT * P, KT, P)]
    s_w = [m.sem("q_w0"), m.sem("q_w1")]
    s_proj, s_kept = m.sem("q_projected"), m.sem("q_kept")
    w_in = io["w_in"].rearrange("l (k p) n -> p (l k) n", p=P)
    with nc.Block() as block:

        @block.sync
        def _(sp):
            def load(j, b):
                for g in range(NKV):
                    col = j * HD + (COL_Q + g * QPK * HD)
                    sp.dma_start(wq[b][:, :, g * HD:(g + 1) * HD], w_in[:, :, bass.ds(col, HD)]).then_inc(s_w[b], 16)

            for b in range(2):
                load(b, b)
            with sp.Fori(1, KT // 2) as jj:
                for b in range(2):
                    sp.wait_ge(s_proj, 2 * jj + (b - 1))
                    load(2 * jj + b, b)

        @block.tensor
        def _(pe):
            def tile(b, jj=None):
                pe.wait_ge(s_w[b], 32 if jj is None else 32 * jj + 32)
                if jj is not None:
                    pe.wait_ge(s_kept, 2 * jj + (b - 1))
                for c in range(3):
                    cols = slice(c * 512, min((c + 1) * 512, NTOK))
                    for k in range(KT):
                        last = nc.tensor.matmul(m.ps[:, 3 * b + c, 0:cols.stop - cols.start], wq[b][:, k, :],
                                                m.xT[:, k, cols], start=(k == 0), stop=(k == KT - 1))
                last.then_inc(s_proj, 1)

            for b in range(2):
                tile(b)
            with pe.Fori(1, KT // 2) as jj:
                for b in range(2):
                    tile(b, jj)

        @block.vector
        def _(dve):
            with dve.Fori(0, KT // 2) as jj:
                for b in range(2):
                    dve.wait_ge(s_proj, 2 * jj + (b + 1))
                    at = (2 * jj + b) * NTOK
                    src = m.ps[:, 3 * b:3 * b + 2, :].rearrange("p a c -> p (a c)")
                    nc.vector.tensor_scalar(m.RO[:, bass.ds(at, SEQ)], src, SCALE, None, ALU.mult)
                    nc.vector.tensor_scalar(m.RO[:, bass.ds(at + SEQ, NB)], m.ps[:, 3 * b + 2, 0:NB],
                                            SCALE, None, ALU.mult).then_inc(s_kept, 1)


def compress_keys(nc, m, io):
    w1 = [view(m.RA, c * 4096, CMP_BLOCK, P) for c in range(2)]
    pages = view(m.RW, 0, NPG, 256)
    cT = view(m.RW, 4096, 2, CKEYS)
    small = m.small
    w2 = small[:, 0:128].rearrange("p (c d) -> p c d", c=2)
    pos = small[0:CMP_BLOCK, 128:256]
    posT = small[0:HD, 256:320].rearrange("p (c s) -> p c s", c=2)
    bias = small[:, 320:322]
    hid = small[:, 384:384 + 8 * P].rearrange("p (u n) -> p u n", u=8)
    s_w1, s_w2, s_pt, s_page = m.sem("cmp_w1"), m.sem("cmp_w2"), m.sem("page_table_in"), m.sem("cmp_pages")
    s_posT, s_posk = m.sem("pos_turned"), m.sem("pos_kept")
    s_bias, s_biask = m.sem("cmp_bias"), m.sem("cmp_bias_kept")
    s_turned, s_kept = m.sem("cmp_turned"), m.sem("cmp_turned_kept")
    s_hid, s_act, s_out, s_end = m.sem("cmp_hidden"), m.sem("cmp_gelu"), m.sem("cmp_outputs"), m.sem("cmp_kept")
    cache = io["cache_kv"].rearrange("n l p s h d -> (n l) p (s h d)")
    units = [(src, c, g) for src in range(2) for c in range(2) for g in range(2)]
    nkeys = (NCMP, NB * SCMP)
    with nc.Block() as block:

        @block.sync
        def _(sp):
            pt = io["page_table"].rearrange("(o b) n -> o (b n)", o=1)
            sp.dma_start(m.page_ids[:], pt).then_inc(s_pt, 16)
            for c in range(2):
                w = io["cmp_w1"][0, c].rearrange("(s d) f -> d s f", d=HD)
                for g in range(2):
                    sp.dma_start(w1[c][g * HD:(g + 1) * HD], w).then_inc(s_w1, 16)
            sp.dma_start(w2, io["cmp_w2"].rearrange("l c f d -> f (l c) d")).then_inc(s_w2, 16)
            sp.dma_start(pos.rearrange("s (c d) -> s c d", c=2),
                         io["cmp_pos"].rearrange("l c s d -> s (l c) d")).then_inc(s_w2, 16)
            sp.wait_ge(s_pt, 16)
            with sp.Fori(0, NPG) as i:
                page = sp.value_load(m.page_ids[0:1, bass.ds(i, 1)], min_val=0, max_val=cache.shape[0] - 1)
                sp.dma_start(m.RW[:, bass.ds(i * 256, 256)],
                             cache[bass.ds(page, 1), :, 0:256].rearrange("n p c -> p (n c)")).then_inc(s_page, 16)

        @block.tensor
        def _(pe):
            pe.wait_ge(s_w2, 32)
            for c in range(2):
                last = nc.tensor.transpose(m.ps[0:HD, 0, c * 32:c * 32 + 32], pos[:, c * HD:(c + 1) * HD],
                                           m.ident[0:32, 0:32])
            last.then_inc(s_posT, 1)
            pe.wait_ge(s_posk, 1)
            pe.wait_ge(s_w1, 64)
            for c in range(2):
                for s in range(CMP_BLOCK):
                    last = nc.tensor.matmul(m.ps[:, 1, c:c + 1], w1[c][0:HD, s, :], posT[:, c, s:s + 1],
                                            start=(s == 0), stop=(s == CMP_BLOCK - 1))
            last.then_inc(s_bias, 1)

            def hidden(u):
                src, c, g = units[u]
                rows = slice(g * HD, (g + 1) * HD)
                for s in range(CMP_BLOCK):
                    if src == 0:
                        rhs = m.kT[rows, c, s:s + CMP_STRIDE * (NCMP - 1) + 1:CMP_STRIDE]
                    else:
                        rhs = cT[rows, c, :].rearrange("p (b t) -> p b t", b=NB)[
                            :, :, s:s + CMP_STRIDE * (SCMP - 1) + 1:CMP_STRIDE]
                    out = m.ps[:, 2 + u % 2, 0:nkeys[src]]
                    last = nc.tensor.matmul(out, w1[c][rows, s, :], rhs, start=(s == 0), stop=(s == CMP_BLOCK - 1))
                last.then_inc(s_hid, 1)

            def outputs(src):
                n = nkeys[src]
                for g in range(2):
                    nc.tensor.matmul(m.ps[g * HD:(g + 1) * HD, 6, 0:n], w2[:, 0, :], hid[:, 4 * src + g, 0:n],
                                     start=True, stop=True)
                for g in range(2):
                    last = nc.tensor.matmul(m.ps[0:n, 7, g * HD:(g + 1) * HD], hid[:, 4 * src + 2 + g, 0:n],
                                            w2[:, 1, :], start=(g == 0), stop=(g == 1), skip_group_check=True)
                last.then_inc(s_out, 1)

            for u in range(4):
                if u >= 2:
                    pe.wait_ge(s_act, u - 1)
                hidden(u)
            for q in range(NPG // 4):
                for c in range(2):
                    i = 2 * q + c
                    if c == 0:
                        pe.wait_ge(s_page, 16 * NPG)
                    if i >= 2:
                        pe.wait_ge(s_kept, i - 1)
                    for r in range(4):
                        last = nc.tensor.transpose(m.ps[:, 4 + i % 2, r * P:(r + 1) * P],
                                                   pages[:, 4 * q + r, c * P:(c + 1) * P], m.ident[:])
                    last.then_inc(s_turned, 1)
            pe.wait_ge(s_act, 4)
            outputs(0)
            pe.wait_ge(s_kept, NPG // 2)
            for u in range(4, 8):
                pe.wait_ge(s_act, u - 1)
                hidden(u)
            pe.wait_ge(s_act, 8)
            pe.wait_ge(s_end, 1)
            outputs(1)

        @block.scalar
        def _(act):
            act.wait_ge(s_biask, 1)
            for u, (src, c, g) in enumerate(units):
                n = nkeys[src]
                act.wait_ge(s_hid, u + 1)
                nc.scalar.activation(hid[:, u, 0:n], m.ps[:, 2 + u % 2, 0:n], ACT.Gelu_apprx_tanh,
                                     bias=bias[:, c:c + 1]).then_inc(s_act, 1)

        @block.vector
        def _(dve):
            dve.wait_ge(s_posT, 1)
            nc.vector.tensor_copy(small[0:HD, 256:320], m.ps[0:HD, 0, 0:64]).then_inc(s_posk, 1)
            dve.wait_ge(s_bias, 1)
            nc.vector.tensor_copy(bias, m.ps[:, 1, 0:2]).then_inc(s_biask, 1)
            for i in range(NPG // 2):
                q, c = i // 2, i % 2
                dve.wait_ge(s_turned, i + 1)
                nc.vector.tensor_copy(cT[:, c, q * 512:(q + 1) * 512], m.ps[:, 4 + i % 2, :]).then_inc(s_kept, 1)
            for src in range(2):
                n = nkeys[src]
                dve.wait_ge(s_out, src + 1)
                nc.vector.tensor_copy(m.kcT[:, src * P:src * P + n], m.ps[:, 6, 0:n])
                nc.vector.tensor_copy(m.vc[0:n, src, :], m.ps[0:n, 7, 0:P]).then_inc(s_end, 1)


def attend_samples(nc, m, io):
    pages = [view(m.RW, 4096, NPG, 256), view(m.RW, 8192, NPG, 256)]
    cT = view(m.RW, 0, 2, CKEYS)
    NS = CKEYS + NB
    S = m.RA[:, 0:NS]
    PT = view(m.RA, 2176, NPG + 1, P)
    sm = m.small
    qs = sm[:, 0:64]
    onehot, mask = sm[:, 64:72], sm[:, 72:80]
    stat = sm[:, 80:92]
    O = view(sm, 128, 3, P)
    s_page, s_c0, s_c1, s_q = m.sem("att_pages"), m.sem("onehot"), m.sem("sample_mask"), m.sem("sample_q")
    s_turned, s_kept = m.sem("page_turned"), m.sem("page_kept")
    s_score, s_masked, s_max = m.sem("s_scores"), m.sem("s_masked"), m.sem("s_max")
    s_exp, s_pt, s_ptk = m.sem("s_probs"), m.sem("s_probs_turned"), m.sem("s_probs_kept")
    s_pv, s_sc, s_o, s_oT, s_sum = m.sem("s_values"), m.sem("s_scaled"), m.sem("s_branch"), m.sem("s_oT"), m.sem("s_rowsum")
    s_oTk = m.sem("s_oT_kept")
    cache = io["cache_kv"].rearrange("n l p s h d -> (n l) p (s h d)")
    win = io["cache_win"].rearrange("b l (n p) s h d -> (b l n) p (s h d)", p=P)
    ngroup = (1, 5, 5)
    with nc.Block() as block:

        @block.sync
        def _(sp):
            with sp.Fori(0, NPG) as i:
                page = sp.value_load(m.page_ids[0:1, bass.ds(i, 1)], min_val=0, max_val=cache.shape[0] - 1)
                sp.dma_start(m.RW[:, bass.ds(4096 + i * 256, 256)],
                             cache[bass.ds(page, 1), :, 256:512].rearrange("n p c -> p (n c)")).then_inc(s_page, 16)
            sp.dma_start(pages[1], win.rearrange("n p c -> p n c")).then_inc(s_page, 16)

        @block.tensor
        def _(pe):
            g_t = 0
            n_pt = 0
            for br in range(3):
                if br == 0:
                    pe.wait_ge(s_q, 1)
                else:
                    pe.wait_ge(s_page, 16 * (NPG + 1))
                    for q in range(NPG // 4):
                        if g_t >= 2:
                            pe.wait_ge(s_kept, g_t - 1)
                        for r in range(4):
                            last = nc.tensor.transpose(m.ps[:, 6 + g_t % 2, r * P:(r + 1) * P],
                                                       pages[br - 1][:, 4 * q + r, 0:P], m.ident[:])
                        last.then_inc(s_turned, 1)
                        g_t += 1
                    pe.wait_ge(s_kept, g_t)
                    pe.wait_ge(s_masked, br)
                for g in range(NKV):
                    rows = slice(g * HD, (g + 1) * HD)
                    if br == 0:
                        last = nc.tensor.matmul(m.ps[rows, 4, 0:NB * SCMP], qs[rows, :], m.kcT[rows, P:P + NB * SCMP],
                                                start=True, stop=True)
                    else:
                        for c in range(4):
                            nc.tensor.matmul(m.ps[rows, c, :], qs[rows, :], cT[rows, br - 1, c * 512:(c + 1) * 512],
                                             start=True, stop=True)
                        last = nc.tensor.matmul(m.ps[rows, 4, 0:NB], qs[rows, :], m.kT[rows, 1 + br, SEQ:NTOK],
                                                start=True, stop=True)
                last.then_inc(s_score, 1)
                pe.wait_ge(s_exp, br + 1)
                pe.wait_ge(s_kept, g_t)
                for q in range(ngroup[br]):
                    if n_pt >= 2:
                        pe.wait_ge(s_ptk, n_pt - 1)
                    if br == 0:
                        last = nc.tensor.transpose(m.ps[0:NB * SCMP, 6 + n_pt % 2, 0:P], S[:, 0:NB * SCMP], m.ident[:])
                    elif q < 4:
                        for r in range(4):
                            k = 4 * q + r
                            last = nc.tensor.transpose(m.ps[:, 6 + n_pt % 2, r * P:(r + 1) * P],
                                                       S[:, k * P:(k + 1) * P], m.ident[:])
                    else:
                        last = nc.tensor.transpose(m.ps[0:NB, 6 + n_pt % 2, 0:P], S[:, CKEYS:NS], m.ident[:])
                    last.then_inc(s_pt, 1)
                    n_pt += 1
                pe.wait_ge(s_ptk, n_pt)
                if br >= 1:
                    pe.wait_ge(s_o, br)
                if br == 0:
                    last = nc.tensor.matmul(m.ps[:, 5, 0:P], PT[0:NB * SCMP, 0, :], m.vc[0:NB * SCMP, 1, :],
                                            start=True, stop=True)
                else:
                    for k in range(NPG):
                        nc.tensor.matmul(m.ps[:, 5, 0:P], PT[:, k, :], pages[br - 1][:, k, P:2 * P],
                                         start=(k == 0), stop=False)
                    last = nc.tensor.matmul(m.ps[:, 5, 0:P], PT[0:NB, NPG, :],
                                            m.vv[0:NB, TT, (br - 1) * P:br * P], start=False, stop=True)
                last.then_inc(s_pv, 1)
            pe.wait_ge(s_sum, 1)
            nc.tensor.transpose(m.ps[:, 6, 0:P], O[:, 0, :], m.ident[:]).then_inc(s_oT, 1)

        @block.scalar
        def _(act):
            for br in range(3):
                act.wait_ge(s_max, br + 1)
                n = NB * SCMP if br == 0 else NS
                nc.scalar.activation(S[:, 0:n], S[:, 0:n], ACT.Exp, bias=stat[:, br:br + 1],
                                     accum_out=stat[:, 3 + br:4 + br]).then_inc(s_exp, 1)

        @block.vector
        def _(dve):
            nc.vector.tensor_reduce(onehot, m.ident[:].rearrange("p (a b) -> p b a", b=NB), AX.X, ALU.add).then_inc(s_c0, 1)
            nc.vector.tensor_copy(qs.rearrange("p (h b) -> p h b", b=NB), m.qT[:, :, SEQ:NTOK]).then_inc(s_q, 1)
            dve.wait_ge(s_c0, 1)
            nc.vector.tensor_scalar(mask, onehot, 1.0, -NEG, ALU.subtract, ALU.mult).then_inc(s_c1, 1)
            dve.wait_ge(s_c1, 1)
            g_t = n_pt = 0
            for br in range(3):
                if br >= 1:
                    for q in range(NPG // 4):
                        g_t += 1
                        dve.wait_ge(s_turned, g_t)
                        nc.vector.tensor_copy(cT[:, br - 1, q * 512:(q + 1) * 512],
                                              m.ps[:, 6 + (g_t - 1) % 2, :]).then_inc(s_kept, 1)
                dve.wait_ge(s_score, br + 1)
                if br >= 1:
                    dve.wait_ge(s_pt, n_pt)
                if br == 0:
                    nc.vector.tensor_tensor(S[:, 0:NB * SCMP].rearrange("p (b n) -> p b n", b=NB),
                                            m.ps[:, 4, 0:NB * SCMP].rearrange("p (b n) -> p b n", b=NB),
                                            mask.unsqueeze(2).to_broadcast([P, NB, SCMP]), ALU.add).then_inc(s_masked, 1)
                    n = NB * SCMP
                else:
                    nc.vector.tensor_tensor(S[:, 0:CKEYS].rearrange("p (b n) -> p b n", b=NB),
                                            m.ps[:, 0:4, :].rearrange("p a c -> p (a c)").rearrange("p (b n) -> p b n", b=NB),
                                            mask.unsqueeze(2).to_broadcast([P, NB, PAST]), ALU.add)
                    nc.vector.tensor_tensor(S[:, CKEYS:NS], m.ps[:, 4, 0:NB], mask, ALU.add).then_inc(s_masked, 1)
                    n = NS
                dve.wait_ge(s_masked, br + 1)
                nc.vector.tensor_reduce(stat[:, br:br + 1], S[:, 0:n], AX.X, ALU.max, negate=True).then_inc(s_max, 1)
                for q in range(ngroup[br]):
                    n_pt += 1
                    dve.wait_ge(s_pt, n_pt)
                    bank = 6 + (n_pt - 1) % 2
                    if br >= 1 and q == 0:
                        dve.wait_ge(s_pv, br)
                    if br == 0:
                        last = nc.vector.tensor_copy(PT[0:NB * SCMP, 0, :], m.ps[0:NB * SCMP, bank, 0:P])
                    elif q < 4:
                        last = nc.vector.tensor_copy(PT[:, 4 * q:4 * q + 4, :],
                                                     m.ps[:, bank, :].rearrange("p (a c) -> p a c", a=4))
                    else:
                        last = nc.vector.tensor_copy(PT[0:NB, NPG, :], m.ps[0:NB, bank, 0:P])
                    last.then_inc(s_ptk, 1)
                dve.wait_ge(s_exp, br + 1)
                nc.vector.reciprocal(stat[:, 6 + br:7 + br], stat[:, 3 + br:4 + br]).then_inc(s_sc, 1)
                dve.wait_ge(s_sc, 2 * br + 1)
                nc.vector.tensor_tensor(stat[:, 9 + br:10 + br], stat[:, 6 + br:7 + br], m.gs[:, br:br + 1],
                                        ALU.mult).then_inc(s_sc, 1)
                dve.wait_ge(s_sc, 2 * br + 2)
                dve.wait_ge(s_pv, br + 1)
                nc.vector.tensor_scalar(O[:, br, :], m.ps[:, 5, 0:P], stat[:, 9 + br:10 + br], None,
                                        ALU.mult).then_inc(s_o, 1)
            dve.wait_ge(s_o, 3)
            nc.vector.tensor_tensor(O[:, 1, :], O[:, 1, :], O[:, 2, :], ALU.add).then_inc(s_o, 1)
            dve.wait_ge(s_o, 4)
            nc.vector.tensor_tensor(O[:, 0, :], O[:, 0, :], O[:, 1, :], ALU.add).then_inc(s_sum, 1)
            dve.wait_ge(s_oT, 1)
            for g in range(NKV):
                rows = slice(g * HD, (g + 1) * HD)
                nc.vector.tensor_copy(m.qT[rows, :, SEQ:NTOK],
                                      m.ps[rows, 6, g * HD:(g + 1) * HD].rearrange("p (h b) -> p h b", b=NB)).then_inc(s_oTk, 1)


def attend_prompt(nc, m):
    probs = [m.RW[:, 1024 + b * 1024:2048 + b * 1024] for b in range(2)]
    probsT = [view(m.RW, 3072 + b * 1024, 8, P) for b in range(2)]
    onat = [m.RW[:, 5120 + b * P:5248 + b * P] for b in range(2)]
    otmp = [m.RW[:, 5376 + b * 384:5760 + b * 384] for b in range(2)]
    identb, diag, edge = m.identb, m.mask_diag, m.mask_edge
    stat = m.small[:, 0:64].rearrange("p (b w) -> p b w", b=2)
    nmax = m.small[:, 64:76]

    s_q, s_qk, s_max, s_exp = m.sem("a_queries"), m.sem("a_scores"), m.sem("a_max"), m.sem("a_probs")
    s_t, s_tkv, s_tka, s_pv = m.sem("a_turned"), m.sem("a_kept_by_dve"), m.sem("a_kept_by_act"), m.sem("a_values")
    s_sc, s_tmp, s_o, s_oT, s_oTk = (m.sem(n) for n in ("a_scale", "a_scaled", "a_output", "a_oT", "a_oT_kept"))
    s_clamp, s_qh, s_kh, s_kl = (m.sem("a_" + n) for n in ("clamp_input", "q_high", "k_high", "k_low"))

    LO, HI = slice(0, HD), slice(HD, P)
    qs, ks, kcs = m.q_stacks, m.k_stacks, m.kc_stacks
    pieces = [[(m.kT[g * HD:(g + 1) * HD, 2 + a, 0:SEQ], ks[:, a, g])] for g in range(NKV) for a in range(2)]
    for g in range(NKV):
        pieces[2 * g + 1].append((m.kcT[g * HD:(g + 1) * HD, 0:NCMP], kcs[:, g, :, 0:NCMP]))

    jobs = [(i, g, kind) for i in range(TT) for g in range(NKV) for kind in "AB"]
    NJ = len(jobs)
    NMAX = sum(1 if kind == "A" else 2 for _, _, kind in jobs)

    def wblocks(i):
        return list(range(max(0, i - WBLK), i + 1))

    def blocks(job):
        i, g, kind = job
        if kind == "A":
            return [(b * P, P) for b in range(i + 1)]
        win = [(b * P, P) for b in range(len(wblocks(i)))]
        at = cmp_at(i)
        return win[:at] + [(cmp_col(i), NCMP)] + win[at:]

    def cmp_at(i):
        return min(len(wblocks(i)), 3)

    def cmp_col(i):
        return len(wblocks(i)) * P

    def groups(job):
        bl = blocks(job)
        return [bl[a:a + 4] for a in range(0, len(bl), 4)]

    def nmaxes(job):
        return 1 if job[2] == "A" else 2

    NGRP = sum(len(groups(j)) for j in jobs)
    NGV = sum((len(groups(j)) + 1) // 2 for j in jobs)
    NGA = NGRP - NGV
    g_before = [sum(len(groups(j)) for j in jobs[:n]) for n in range(NJ + 1)]
    v_before = [sum((len(groups(j)) + 1) // 2 for j in jobs[:n]) for n in range(NJ + 1)]
    a_before = [g_before[n] - v_before[n] for n in range(NJ + 1)]
    m_before = [sum(nmaxes(j) for j in jobs[:n]) for n in range(NJ + 1)]
    kept_by = [("v" if q % 2 == 0 else "a") for j in jobs for q in range(len(groups(j)))]

    def keep_group(copy, n, q, grp, G):
        full = sum(1 for _, w in grp if w == P)
        last = None
        if full:
            last = copy(probsT[n % 2][:, 4 * q:4 * q + full, :],
                        m.ps[:, 4 + G % 2, 0:full * P].rearrange("p (a c) -> p a c", a=full))
        if full < len(grp):
            last = copy(probsT[n % 2][0:NCMP, 4 * q + full, :], m.ps[0:NCMP, 4 + G % 2, full * P:(full + 1) * P])
        return last

    def wait_from(eng, sem, base, value, first):
        if not (first and value <= 0):
            eng.wait_ge(sem, base + value)

    with nc.Block() as block:

        @block.gpsimd
        def _(pool):
            def high_queries(j, first):
                for i in range(TT):
                    if not first:
                        pool.wait_ge(s_qk, NJ * j + (4 * (i + 1) - NJ))
                    at, cols = bass.ds(j * NTOK + i * P, P), slice(i * P, (i + 1) * P)
                    nc.gpsimd.tensor_copy(qs[LO, 0, cols], m.RO[LO, at])
                    nc.gpsimd.tensor_copy(qs[HI, 1, cols], m.RO[HI, at]).then_inc(s_qh, 1)

            high_queries(0, True)
            with pool.Fori(1, QPK) as j:
                high_queries(j, False)

        @block.tensor
        def _(pe):
            def scores(n, j, first):
                i, g, kind = jobs[n]
                bank = 2 * (n % 2)

                def product(out, k, start=True):
                    for h in range(2):
                        nc.tensor.matmul(out, qs[:, g, i * P:(i + 1) * P], k[:, h], start=start and h == 0,
                                         stop=(h == 1), skip_group_check=True)

                if kind == "A" and g == 0:
                    pe.wait_ge(s_q, TT * j + (i + 1))
                if first and n < len(pieces):
                    pe.wait_ge(s_kh, n + 1)
                    pe.wait_ge(s_kl, n + 1)
                wait_from(pe, s_exp, NMAX * j, m_before[n - 1] if n >= 2 else m_before[NJ + n - 1] - NMAX, first)
                if kind == "A":
                    nk = (i + 1) * P
                    for c in range(0, nk, 512):
                        w = min(512, nk - c)
                        product(m.ps[:, bank + c // 512, 0:w], ks[:, 0, g, :, c:c + w])
                    mm = nc.tensor.matmul(m.ps[:, bank + i // 4, (i % 4) * P:(i % 4 + 1) * P], identb[:], diag[:],
                                          start=False, stop=True, skip_group_check=True)
                    mm.then_inc(s_qk, 1)
                else:
                    bl = wblocks(i)
                    k0, nk, cc = bl[0] * P, len(bl) * P, cmp_col(i)
                    if len(bl) > WBLK:
                        product(m.ps[:, bank, 0:512], ks[:, 1, g, :, k0:k0 + 512])
                        nc.tensor.matmul(m.ps[:, bank, 0:P], identb[:], edge[:], start=False, stop=True, skip_group_check=True)
                        product(m.ps[:, bank + 1, 0:P], ks[:, 1, g, :, k0 + 512:k0 + 640])
                    else:
                        product(m.ps[:, bank, 0:nk], ks[:, 1, g, :, k0:k0 + nk])
                    at = nk - P
                    nc.tensor.matmul(m.ps[:, bank + at // 512, at % 512:at % 512 + P], identb[:], diag[:], start=False,
                                     stop=True, skip_group_check=True)
                    out = m.ps[:, bank + cc // 512, cc % 512:cc % 512 + NCMP + 1]
                    product(out, kcs[:, g], start=(cc % 512 == 0))
                    out = out[:, 0:NCMP]
                    at = 56 - 8 * i
                    nc.tensor.matmul(out, identb[:], m.mask_cmp[:, at:at + NCMP], start=False, stop=True,
                                     skip_group_check=True).then_inc(s_qk, 1)

            def turn(n, j, first):
                pe.wait_ge(s_exp, NMAX * j + m_before[n + 1])
                for q, grp in enumerate(groups(jobs[n])):
                    G = g_before[n] + q
                    H = G - 2
                    if H >= 0:
                        by, cnt = kept_by[H], sum(1 for x in kept_by[:H + 1] if x == kept_by[H])
                    else:
                        by = kept_by[H + NGRP]
                        cnt = sum(1 for x in kept_by[:H + NGRP + 1] if x == by) - (NGV if by == "v" else NGA)
                    wait_from(pe, s_tkv if by == "v" else s_tka, (NGV if by == "v" else NGA) * j, cnt, first)
                    for r, (col, w) in enumerate(grp):
                        last = nc.tensor.transpose(m.ps[0:w, 4 + G % 2, r * P:(r + 1) * P],
                                                   probs[n % 2][:, col:col + w], m.ident[:])
                    last.then_inc(s_t, 1)

            def values(n, j, first):
                i, g, kind = jobs[n]
                pe.wait_ge(s_tkv, NGV * j + v_before[n + 1])
                wait_from(pe, s_tka, NGA * j, a_before[n + 1], first)
                if g == 0 and kind == "A":
                    wait_from(pe, s_oTk, TT * j, i - 1, first)
                bank = 6 + i % 2
                gc = slice(g * HD, (g + 1) * HD)
                pT = probsT[n % 2]
                if kind == "A":
                    out = m.ps[:, bank, g * 192 + 64:g * 192 + 128]
                    for b in range(i + 1):
                        last = nc.tensor.matmul(out, pT[:, b, :], m.vv[:, b, g * HD:(g + 1) * HD],
                                                start=(b == 0), stop=(b == i), skip_group_check=True)
                else:
                    bl = wblocks(i)
                    out = m.ps[:, bank, g * 192 + 128:g * 192 + 192]
                    for r, b in enumerate(bl):
                        nc.tensor.matmul(out, pT[:, r + (r >= cmp_at(i)), :], m.vv[:, b, P + g * HD:P + (g + 1) * HD],
                                         start=(r == 0), stop=(r == len(bl) - 1), skip_group_check=True)
                    last = nc.tensor.matmul(m.ps[:, bank, g * 192:g * 192 + 64], pT[0:NCMP, cmp_at(i), :],
                                            m.vc[0:NCMP, 0, gc], start=True, stop=True, skip_group_check=True)
                last.then_inc(s_pv, 1)

            def turn_output(i, j, first):
                pe.wait_ge(s_o, TT * j + (i + 1))
                nc.tensor.transpose(m.ps[:, 6 + i % 2, 384:512], onat[i % 2], m.ident[:]).then_inc(s_oT, 1)

            def one_pass(j, first):
                scores(0, j, first)
                for n in range(NJ + 2):
                    if n + 1 < NJ:
                        scores(n + 1, j, first)
                    if n < NJ:
                        turn(n, j, first)
                    if 1 <= n <= NJ:
                        values(n - 1, j, first)
                    if n >= 2 and jobs[n - 2][1:] == (1, "B"):
                        turn_output(jobs[n - 2][0], j, first)

            one_pass(0, True)
            with pe.Fori(1, QPK) as j:
                one_pass(j, False)

        @block.vector
        def _(dve):
            def job_max(n, j, first):
                i, g, kind = jobs[n]
                bank = 2 * (n % 2)
                dve.wait_ge(s_qk, NJ * j + (n + 1))
                sc = m.ps[:, bank:bank + 2, :].rearrange("p a c -> p (a c)")
                col = 2 * (n % 2)
                nk = (i + 1) * P if kind == "A" else cmp_col(i)
                nc.vector.tensor_reduce(nmax[:, col:col + 1], sc[:, 0:nk], AX.X, ALU.max, negate=True).then_inc(s_max, 1)
                if kind == "B":
                    dst = nmax[:, 4:5] if i == 0 else nmax[:, col + 1:col + 2]
                    red = nc.vector.tensor_reduce(dst, sc[:, nk:nk + NCMP], AX.X, ALU.max, negate=True)
                    if i > 0:
                        red.then_inc(s_max, 1)
                    else:
                        red.then_inc(s_clamp, 1)
                        dve.wait_ge(s_clamp, NKV * j + (g + 1))
                        nc.vector.tensor_scalar(nmax[:, col + 1:col + 2], nmax[:, 4:5], 1e29, None,
                                                ALU.min).then_inc(s_max, 1)

            def keep(n, j, first):
                for q, grp in enumerate(groups(jobs[n])):
                    if q % 2 == 0:
                        G = g_before[n] + q
                        dve.wait_ge(s_t, NGRP * j + (G + 1))
                        if n >= 2 or not first:
                            dve.wait_ge(s_pv, NJ * j + (n - 1))
                        keep_group(nc.vector.tensor_copy, n, q, grp, G).then_inc(s_tkv, 1)

            def finish(i, j, first):
                b = i % 2
                sums, rec, scl = stat[:, b, 0:6], stat[:, b, 8:14], stat[:, b, 16:22]
                dve.wait_ge(s_exp, NMAX * j + m_before[4 * i + 4])
                if i == 0:
                    nc.vector.tensor_scalar(sums, sums, 1e-30, None, ALU.max).then_inc(s_sc, 1)
                    dve.wait_ge(s_sc, 17 * j + 1)
                nc.vector.reciprocal(rec, sums).then_inc(s_sc, 1)
                dve.wait_ge(s_sc, 17 * j + (2 * i + 2))
                gate = m.gates[:, i, :].rearrange("p (g x) -> p g x", g=NKV)[:, :, bass.ds(3 * j, 3)]
                nc.vector.tensor_tensor(scl.rearrange("p (g x) -> p g x", g=NKV), rec.rearrange("p (g x) -> p g x", g=NKV),
                                        gate, ALU.mult).then_inc(s_sc, 1)
                dve.wait_ge(s_sc, 17 * j + (2 * i + 3))
                dve.wait_ge(s_pv, NJ * j + (4 * i + 4))
                nc.vector.tensor_tensor(otmp[b].rearrange("p (x d) -> p x d", d=HD),
                                        m.ps[:, 6 + b, 0:384].rearrange("p (x d) -> p x d", d=HD),
                                        scl.unsqueeze(2).to_broadcast([P, 6, HD]), ALU.mult).then_inc(s_tmp, 1)
                dve.wait_ge(s_tmp, TT * j + (i + 1))
                nc.vector.tensor_reduce(onat[b].rearrange("p (g d) -> p g d", g=NKV),
                                        otmp[b].rearrange("p (g x d) -> p g d x", g=NKV, x=3), AX.X, ALU.add).then_inc(s_o, 1)

            def low_queries(i, j):
                at, cols = bass.ds(j * NTOK + i * P, P), slice(i * P, (i + 1) * P)
                dve.wait_ge(s_qh, TT * j + (i + 1))
                nc.vector.tensor_tensor(qs[HI, 0, cols], m.RO[LO, at], qs[LO, 0, cols], ALU.subtract)
                nc.vector.tensor_tensor(qs[LO, 1, cols], m.RO[HI, at], qs[HI, 1, cols], ALU.subtract).then_inc(s_q, 1)

            def keep_output(i, j, first):
                dve.wait_ge(s_oT, TT * j + (i + 1))
                nc.vector.tensor_scalar(m.RO[:, bass.ds(j * NTOK + i * P, P)], m.ps[:, 6 + i % 2, 384:512],
                                        1.0, None, ALU.mult).then_inc(s_oTk, 1)

            def one_pass(j, first):
                low_queries(0, j)
                job_max(0, j, first)
                for n in range(NJ + 2):
                    if n % 4 == 0 and n // 4 + 1 < TT:
                        low_queries(n // 4 + 1, j)
                    if n + 1 < NJ:
                        job_max(n + 1, j, first)
                    if n < NJ:
                        keep(n, j, first)
                    if 1 <= n <= NJ and jobs[n - 1][1:] == (1, "B"):
                        finish(jobs[n - 1][0], j, first)
                    if n >= 2 and jobs[n - 2][1:] == (1, "B"):
                        keep_output(jobs[n - 2][0], j, first)

            nc.vector.memset(kcs[:, :, :, NCMP:NCMP + 1].bitcast(F32), 0.0)
            for n, piece in enumerate(pieces):
                dve.wait_ge(s_kh, n + 1)
                rows = slice(n // 2 * HD, (n // 2 + 1) * HD)
                for src, dst in piece:
                    for half in (LO, HI):
                        last = nc.vector.tensor_tensor(dst[half, 1], src, dst[rows, 0], ALU.subtract)
                last.then_inc(s_kl, 1)
            one_pass(0, True)
            with dve.Fori(1, QPK) as j:
                one_pass(j, False)

        @block.scalar
        def _(act):
            def exps(n, j, first):
                i, g, kind = jobs[n]
                bank, col = 2 * (n % 2), 2 * (n % 2)
                sc = m.ps[:, bank:bank + 2, :].rearrange("p a c -> p (a c)")
                if n >= 2 or not first:
                    act.wait_ge(s_t, NGRP * j + (g_before[n - 1] if n >= 2 else g_before[NJ + n - 1] - NGRP))
                if kind == "A" and g == 0 and (i >= 2 or not first):
                    act.wait_ge(s_sc, 17 * j + (2 * (i - 2) + 2 if i >= 2 else 2 * (i + 6) + 2 - 17))
                nk = (i + 1) * P if kind == "A" else cmp_col(i)
                branch = 1 if kind == "A" else 2
                act.wait_ge(s_max, NMAX * j + m_before[n + 1])
                nc.scalar.activation(probs[n % 2][:, 0:nk], sc[:, 0:nk], ACT.Exp, bias=nmax[:, col:col + 1],
                                     accum_out=stat[:, i % 2, 3 * g + branch:3 * g + branch + 1]).then_inc(s_exp, 1)
                if kind == "B":
                    nc.scalar.activation(probs[n % 2][:, nk:nk + NCMP], sc[:, nk:nk + NCMP], ACT.Exp,
                                         bias=nmax[:, col + 1:col + 2],
                                         accum_out=stat[:, i % 2, 3 * g:3 * g + 1]).then_inc(s_exp, 1)

            def keep(n, j, first):
                for q, grp in enumerate(groups(jobs[n])):
                    if q % 2 == 1:
                        G = g_before[n] + q
                        act.wait_ge(s_t, NGRP * j + (G + 1))
                        if n >= 2 or not first:
                            act.wait_ge(s_pv, NJ * j + (n - 1))
                        keep_group(nc.scalar.copy, n, q, grp, G).then_inc(s_tka, 1)

            def one_pass(j, first):
                exps(0, j, first)
                for n in range(NJ):
                    if n + 1 < NJ:
                        exps(n + 1, j, first)
                    keep(n, j, first)

            for piece in pieces:
                for src, dst in piece:
                    for half in (LO, HI):
                        last = nc.scalar.copy(dst[half, 0], src)
                last.then_inc(s_kh, 1)
            one_pass(0, True)
            with act.Fori(1, QPK) as j:
                one_pass(j, False)


def normalise(nc, dve, x, n, stats, mv, rstd, gain, bias, s_stat, s_mv, s_rstd, s_norm, t, done):
    nc.vector.bn_stats(stats[0:n, 0:6], x[:, 0:512])
    nc.vector.bn_stats(stats[0:n, 6:12], x[:, 512:1024]).then_inc(s_stat, 1)
    dve.wait_ge(s_stat, t + 1)
    nc.vector.bn_aggr(mv[0:n], stats[0:n, 0:12]).then_inc(s_mv, 1)
    dve.wait_ge(s_rstd, t + 1)
    nc.vector.tensor_scalar(x, x, mv[0:n, 0:1], rstd[0:n], ALU.subtract, ALU.mult).then_inc(s_norm, 1)
    dve.wait_ge(s_norm, 2 * t + 1)
    nc.vector.tensor_tensor(x, x, gain[0:n], ALU.mult).then_inc(s_norm, 1)
    dve.wait_ge(s_norm, 2 * t + 2)
    nc.vector.tensor_tensor(x, x, bias[0:n], ALU.add).then_inc(done, 1)


def inverse_deviation(nc, m, pool, n, mv, rstd, s_mv, s_eps, s_rstd, t):
    pool.wait_ge(s_mv, t + 1)
    nc.gpsimd.tensor_scalar(rstd[0:n], mv[0:n, 1:2], EPS, None, ALU.add).then_inc(s_eps, 1)
    pool.wait_ge(s_eps, t + 1)
    nc.gpsimd.tensor_tensor(rstd[0:n], rstd[0:n], m.mhalf[0:n], ALU.pow).then_inc(s_rstd, 1)


def gmlp_values(nc, m, io):
    wv = view(m.RW, 0, 2 * KT, 512)
    vn = [m.RK[:, t * DM:(t + 1) * DM] for t in range(TT)] + [m.RW[0:NB, 8192:9216]]
    gain, bias = m.RW[:, 9216:10240], m.RW[:, 10240:11264]
    wsT = view(m.RW, 11264, 8, P)
    bs = view(m.RW, 12288, 8, P)
    ws = view(m.RW, 13312, 8, P)
    stats, mv, rstd = m.small[:, 0:12], m.small[:, 12:14], m.small[:, 14:15]
    w00 = m.small[0:NB, 16:24]
    first = m.small[0:NB, 24:88].rearrange("p (g b) -> p g b", g=8)
    s_w, s_c, s_wsT, s_wsk, s_ws = (m.sem(n) for n in ("v_w", "v_consts", "ws_turned", "ws_kept", "ws_masked"))
    s_proj, s_gelu, s_stat, s_mv, s_eps = (m.sem(n) for n in ("v_projected", "v_gelu", "v_stats", "v_moments", "v_eps"))
    s_rstd, s_norm, s_v, s_mix, s_kept = (m.sem(n) for n in ("v_rstd", "v_scaling", "v_normal", "v_mixed", "v_mixed_kept"))
    s_first, s_out = m.sem("ws_first"), m.sem("v_sample_out")
    w_in = io["w_in"].rearrange("l (k p) n -> p (l k) n", p=P)
    with nc.Block() as block:

        @block.sync
        def _(sp):
            for c in range(2):
                sp.dma_start(wv[:, c * KT:(c + 1) * KT, :], w_in[:, :, COL_V + c * 512:COL_V + (c + 1) * 512]).then_inc(s_w, 16)
            sp.dma_start(ws, io["gmlp_ws"].rearrange("l g t s -> t (l g) s")).then_inc(s_c, 16)
            sp.dma_start(gain, io["gmlp_ln_g"].rearrange("l d -> (l d)").partition_broadcast(P)).then_inc(s_c, 16)
            sp.dma_start(bias, io["gmlp_ln_b"].rearrange("l d -> (l d)").partition_broadcast(P)).then_inc(s_c, 16)
            sp.dma_start(bs.rearrange("p g t -> p (g t)"),
                         io["gmlp_bs"].rearrange("l g t -> (l g t)").partition_broadcast(P)).then_inc(s_c, 16)
            with nc.allow_non_contiguous_dma(reason="one weight per group"):
                sp.dma_start(w00.unsqueeze(2), io["gmlp_ws"][0, :, 0, 0:1].partition_broadcast(NB)).then_inc(s_c, 16)
            sp.wait_ge(s_v, NT9)
            sp.dma_start(io["gmlp_v_sample"].rearrange("b l t d -> (b l t) d"), vn[TT]).then_inc(s_out, 16)
            sp.wait_ge(s_out, 16)

        @block.gpsimd
        def _(pool):
            pool.wait_ge(s_wsk, 1)
            nc.gpsimd.affine_select(out=wsT, in_=wsT, compare_op=ALU.is_ge, fill=0.0, base=0,
                                    pattern=[[0, 8], [1, P]], channel_multiplier=-1).then_inc(s_ws, 1)
            for t in range(NT9):
                inverse_deviation(nc, m, pool, rows_of(t), mv, rstd, s_mv, s_eps, s_rstd, t)

        @block.tensor
        def _(pe):
            pe.wait_ge(s_c, 80)
            for g in range(8):
                last = nc.tensor.transpose(m.ps[:, 4 + g // 4, (g % 4) * P:(g % 4 + 1) * P], ws[:, g, :], m.ident[:])
            last.then_inc(s_wsT, 1)

            def mix(t):
                n, bank = rows_of(t), 4 + 2 * (t % 2)
                pe.wait_ge(s_v, t + 1)
                if t == 0:
                    pe.wait_ge(s_ws, 1)
                if t == TT:
                    pe.wait_ge(s_first, 1)
                if t >= 2:
                    pe.wait_ge(s_kept, t - 1)
                for g in range(8):
                    out = m.ps[:, bank + g // 4, (g % 4) * P:(g % 4) * P + n]
                    rhs = wsT[:, g, :] if t < TT else first[:, g, :]
                    last = nc.tensor.matmul(out, vn[t][:, g * P:(g + 1) * P], rhs, start=True, stop=True)
                last.then_inc(s_mix, 1)

            pe.wait_ge(s_w, 32)
            for t in range(NT9):
                n = rows_of(t)
                if t >= 2:
                    pe.wait_ge(s_gelu, t - 1)
                for c in range(2):
                    for k in range(KT):
                        last = nc.tensor.matmul(m.ps[0:n, 2 * (t % 2) + c, :], m.xT[:, k, span(t)],
                                                wv[:, c * KT + k, :], start=(k == 0), stop=(k == KT - 1))
                last.then_inc(s_proj, 1)
                if t >= 1:
                    mix(t - 1)
            mix(TT)

        @block.scalar
        def _(act):
            for t in range(NT9):
                n, b = rows_of(t), t % 2
                act.wait_ge(s_proj, t + 1)
                nc.scalar.activation(vn[t].rearrange("p (a c) -> p a c", a=2), m.ps[0:n, 2 * b:2 * b + 2, :],
                                     ACT.Gelu_apprx_tanh).then_inc(s_gelu, 1)

        @block.vector
        def _(dve):
            dve.wait_ge(s_wsT, 1)
            nc.vector.tensor_copy(wsT.rearrange("p (a c) t -> p a (c t)", a=2), m.ps[:, 4:6, :]).then_inc(s_wsk, 1)
            dve.wait_ge(s_c, 80)
            nc.vector.tensor_tensor(first, m.ident[0:NB, 0:NB].unsqueeze(1).to_broadcast([NB, 8, NB]),
                                    w00.unsqueeze(2).to_broadcast([NB, 8, NB]), ALU.mult).then_inc(s_first, 1)

            def keep(t):
                n, bank = rows_of(t), 4 + 2 * (t % 2)
                dve.wait_ge(s_mix, t + 1)
                src = m.ps[:, bank:bank + 2, :].rearrange("p a (g c) -> p (a g) c", g=4)[:, :, 0:n]
                add = bs if t < TT else bs[:, :, 0:1].to_broadcast([P, 8, NB])
                nc.vector.tensor_tensor(m.aT[:, :, span(t)], src, add, ALU.add).then_inc(s_kept, 1)

            for t in range(NT9):
                dve.wait_ge(s_gelu, t + 1)
                normalise(nc, dve, vn[t], rows_of(t), stats, mv, rstd, gain, bias,
                          s_stat, s_mv, s_rstd, s_norm, t, s_v)
                if t >= 1:
                    keep(t - 1)
            keep(TT)


def gmlp_gate(nc, m, io):
    wu = [view(m.RW, 14336 + b * KT * P, KT, P) for b in range(2)]
    ug = [m.RW[:, b * NTOK:(b + 1) * NTOK] for b in range(2)]
    s_w = [m.sem("u_w0"), m.sem("u_w1")]
    s_proj, s_gelu, s_a = m.sem("u_projected"), m.sem("u_gelu"), m.sem("a_ready")
    w_in = io["w_in"].rearrange("l (k p) n -> p (l k) n", p=P)
    with nc.Block() as block:

        @block.sync
        def _(sp):
            for b in range(2):
                sp.dma_start(wu[b], w_in[:, :, b * P:(b + 1) * P]).then_inc(s_w[b], 16)
            with sp.Fori(1, KT // 2) as jj:
                for b in range(2):
                    sp.wait_ge(s_proj, 2 * jj + (b - 1))
                    sp.dma_start(wu[b], w_in[:, :, bass.ds(2 * P * jj + b * P, P)]).then_inc(s_w[b], 16)

        @block.tensor
        def _(pe):
            def tile(b, jj=None):
                pe.wait_ge(s_w[b], 16 if jj is None else 16 * jj + 16)
                if jj is not None:
                    pe.wait_ge(s_gelu, 2 * jj + (b - 1))
                for c in range(3):
                    cols = slice(c * 512, min((c + 1) * 512, NTOK))
                    for k in range(KT):
                        last = nc.tensor.matmul(m.ps[:, 3 * b + c, 0:cols.stop - cols.start], wu[b][:, k, :],
                                                m.xT[:, k, cols], start=(k == 0), stop=(k == KT - 1))
                last.then_inc(s_proj, 1)

            for b in range(2):
                tile(b)
            with pe.Fori(1, KT // 2) as jj:
                for b in range(2):
                    tile(b, jj)

        @block.scalar
        def _(act):
            def tile(b, jj=None):
                act.wait_ge(s_proj, b + 1 if jj is None else 2 * jj + (b + 1))
                if jj is not None:
                    act.wait_ge(s_a, 2 * jj + (b - 1))
                src = m.ps[:, 3 * b:3 * b + 2, :].rearrange("p a c -> p (a c)")
                nc.scalar.activation(ug[b][:, 0:SEQ], src, ACT.Gelu_apprx_tanh)
                nc.scalar.activation(ug[b][:, SEQ:NTOK], m.ps[:, 3 * b + 2, 0:NB], ACT.Gelu_apprx_tanh).then_inc(s_gelu, 1)

            for b in range(2):
                tile(b)
            with act.Fori(1, KT // 2) as jj:
                for b in range(2):
                    tile(b, jj)

        @block.vector
        def _(dve):
            with dve.Fori(0, KT // 2) as jj:
                for b in range(2):
                    dve.wait_ge(s_gelu, 2 * jj + (b + 1))
                    at = m.RA[:, bass.ds((2 * jj + b) * NTOK, NTOK)]
                    nc.vector.tensor_tensor(at, at, ug[b], ALU.mult).then_inc(s_a, 1)


def merge(nc, m, io):
    w = [m.RW[:, b * 4096:(b + 1) * 4096].rearrange("p (q k c) -> p q k c", q=4, k=KT) for b in range(2)]
    wout = view(m.RW, 8192, KT, DM)
    sa, sb = m.small[:, 0:512], m.small[:, 512:1024]
    s_w = [m.sem("m_w0"), m.sem("m_w1")]
    s_out = m.sem_wout
    s_mm, s_sig, s_mul, s_y = m.sem("m_products"), m.sem("m_sigmoid"), m.sem("m_gated"), m.sem("m_merged")
    w_in = io["w_in"].rearrange("l (k p) n -> p (l k) n", p=P)
    w_a = io["w_branch_a"].rearrange("l (k p) n -> p (l k) n", p=P)
    w_b = io["w_branch_b"].rearrange("l (g k d) n -> g d (l k) n", g=NKV, d=HD)
    NS = 3

    def columns(c):
        return slice(c * 512, min((c + 1) * 512, NTOK))

    with nc.Block() as block:

        @block.sync
        def _(sp):
            def load(col, b):
                sp.dma_start(w[b][:, 0], w_in[:, :, bass.ds(col + COL_GA, P)]).then_inc(s_w[b], 16)
                sp.dma_start(w[b][:, 1], w_in[:, :, bass.ds(col + COL_GB, P)]).then_inc(s_w[b], 16)
                sp.dma_start(w[b][:, 2], w_a[:, :, bass.ds(col, P)]).then_inc(s_w[b], 16)
                for g in range(NKV):
                    sp.dma_start(w[b][g * HD:(g + 1) * HD, 3], w_b[g, :, :, bass.ds(col, P)]).then_inc(s_w[b], 16)

            for b in range(2):
                load(b * P, b)
            sp.dma_start(wout, io["w_out"].rearrange("l (k p) n -> p (l k) n", p=P)).then_inc(s_out, 16)
            with sp.Fori(1, KT // 2) as jj:
                for b in range(2):
                    sp.wait_ge(s_mm, NS * 2 * jj + NS * (b - 1))
                    load(2 * P * jj + b * P, b)

        @block.tensor
        def _(pe):
            def tile(b, jj=None):
                pe.wait_ge(s_w[b], 80 if jj is None else 80 * jj + 80)
                for c in range(NS):
                    step = NS * b + c
                    half = step % 2
                    if jj is not None or step >= 2:
                        pe.wait_ge(s_mul, step - 1 if jj is None else 2 * NS * jj + (step - 1))
                    n = columns(c).stop - columns(c).start
                    for q, src in enumerate((m.xT, m.xT, m.aT, m.qT)):
                        for k in range(KT):
                            last = nc.tensor.matmul(m.ps[:, 4 * half + q, 0:n], w[b][:, q, k, :], src[:, k, columns(c)],
                                                    start=(k == 0), stop=(k == KT - 1))
                    last.then_inc(s_mm, 1)

            for b in range(2):
                tile(b)
            with pe.Fori(1, KT // 2) as jj:
                for b in range(2):
                    tile(b, jj)

        def step_of(jj, b, c):
            return 2 * NS * jj + (NS * b + c)

        @block.scalar
        def _(act):
            def tile(b, jj, first):
                for c in range(NS):
                    half, n = (NS * b + c) % 2, columns(c).stop - columns(c).start
                    act.wait_ge(s_mm, step_of(jj, b, c) + 1)
                    if not (first and b == 0 and c == 0):
                        act.wait_ge(s_y, step_of(jj, b, c))
                    nc.scalar.activation(sa[:, 0:n], m.ps[:, 4 * half, 0:n], ACT.Sigmoid)
                    nc.scalar.activation(sb[:, 0:n], m.ps[:, 4 * half + 1, 0:n], ACT.Sigmoid).then_inc(s_sig, 1)

            for b in range(2):
                tile(b, 0, True)
            with act.Fori(1, KT // 2) as jj:
                for b in range(2):
                    tile(b, jj, False)

        @block.vector
        def _(dve):
            with dve.Fori(0, KT // 2) as jj:
                for b in range(2):
                    for c in range(NS):
                        half, n = (NS * b + c) % 2, columns(c).stop - columns(c).start
                        dve.wait_ge(s_sig, step_of(jj, b, c) + 1)
                        nc.vector.tensor_tensor(sa[:, 0:n], sa[:, 0:n], m.ps[:, 4 * half + 2, 0:n], ALU.mult)
                        nc.vector.tensor_tensor(sb[:, 0:n], sb[:, 0:n], m.ps[:, 4 * half + 3, 0:n], ALU.mult).then_inc(s_mul, 1)
                        dve.wait_ge(s_mul, step_of(jj, b, c) + 1)
                        at = (2 * jj + b) * NTOK + c * 512
                        nc.vector.tensor_tensor(m.RK[:, bass.ds(at, n)], sa[:, 0:n], sb[:, 0:n], ALU.add).then_inc(s_y, 1)


def output_and_router(nc, m, io):
    yT = view(m.RK, 0, KT, NTOK)
    wout = view(m.RW, 8192, KT, DM)
    x1 = m.x1
    base = 12288
    gain, bias = m.R3[:, base:base + DM], m.R3[:, base + DM:base + 2 * DM]
    x1T = view(m.R3, base + 2 * DM, KT, P)
    wr = m.R3[:, base + 3 * DM:base + 3 * DM + KT * NE].rearrange("p (k e) -> p k e", k=KT)
    sc = m.R3[:, base + 3 * DM + 128:base + 3 * DM + 160]
    stats, mv, rstd = sc[:, 0:12], sc[:, 12:14], sc[:, 14:15]
    aff = m.aff
    s_x, s_c, s_mm, s_z = [m.sem(f"o_x{b}") for b in range(3)], m.sem("o_consts"), m.sem("o_products"), m.sem("o_residual")
    s_stat, s_mv, s_eps, s_rstd, s_norm = (m.sem("o_" + n) for n in ("stats", "moments", "eps", "rstd", "scaling"))
    s_x1, s_t, s_tk, s_r, s_aff, s_a0 = (m.sem("o_" + n) for n in ("x1_ready", "turned", "turned_kept", "routed", "affinity", "clear"))
    xp = io["x_prompt"].rearrange("a (t p) d -> p (a t) d", p=P)
    with nc.Block() as block:

        @block.sync
        def _(sp):
            sp.dma_start(gain, io["ln1_g"].rearrange("l d -> (l d)").partition_broadcast(P)).then_inc(s_c, 16)
            sp.dma_start(bias, io["ln1_b"].rearrange("l d -> (l d)").partition_broadcast(P)).then_inc(s_c, 16)
            sp.dma_start(wr, io["w_router"].rearrange("(k p) e -> p k e", p=P)).then_inc(s_c, 16)
            for t in range(NT9):
                if t >= 3:
                    sp.wait_ge(s_x[t % 3], 16 * (t // 3))
                src = xp[:, t, :] if t < TT else io["x_sample"].rearrange("b t d -> (b t) d")
                sp.dma_start(x1[t], src).then_inc(s_x[t % 3], 16)
            load_expert(nc, m, io, sp, 0, 0)

        @block.gpsimd
        def _(pool):
            nc.gpsimd.memset(aff[:, TT, :], 0.0).then_inc(s_a0, 1)
            for t in range(NT9):
                inverse_deviation(nc, m, pool, rows_of(t), mv, rstd, s_mv, s_eps, s_rstd, t)

        @block.tensor
        def _(pe):
            def turn(t):
                n = rows_of(t)
                pe.wait_ge(s_x1, t + 1)
                if t >= 1:
                    pe.wait_ge(s_tk, t)
                for k in range(KT):
                    last = nc.tensor.transpose(m.ps[:, 4 + k // 4, (k % 4) * P:(k % 4) * P + n],
                                               x1[t][:, k * P:(k + 1) * P], m.ident[0:n, 0:n])
                last.then_inc(s_t, 1)

            def route(t):
                n = rows_of(t)
                pe.wait_ge(s_tk, t + 1)
                if t >= 2:
                    pe.wait_ge(s_aff, t - 1)
                for k in range(KT):
                    last = nc.tensor.matmul(m.ps[0:n, 6 + t % 2, 0:NE], x1T[:, k, 0:n], wr[:, k, :],
                                            start=(k == 0), stop=(k == KT - 1))
                last.then_inc(s_r, 1)

            pe.wait_ge(m.sem_wout, 16)
            pe.wait_ge(s_c, 48)
            for t in range(NT9):
                n = rows_of(t)
                if t >= 2:
                    pe.wait_ge(s_z, t - 1)
                for c in range(2):
                    for k in range(KT):
                        last = nc.tensor.matmul(m.ps[0:n, 2 * (t % 2) + c, :], yT[:, k, span(t)],
                                                wout[:, k, c * 512:(c + 1) * 512], start=(k == 0), stop=(k == KT - 1))
                last.then_inc(s_mm, 1)
                if t >= 2:
                    route(t - 2)
                if t >= 1:
                    turn(t - 1)
            route(TT - 1)
            turn(TT)
            route(TT)

        @block.scalar
        def _(act):
            for t in range(NT9):
                n = rows_of(t)
                act.wait_ge(s_t, t + 1)
                if t >= 1:
                    act.wait_ge(s_r, t)
                src = m.ps[:, 4:6, :].rearrange("p a (k c) -> p (a k) c", k=4)[:, :, 0:n]
                nc.scalar.copy(x1T[:, :, 0:n], src).then_inc(s_tk, 1)
                act.wait_ge(s_r, t + 1)
                if t == TT:
                    act.wait_ge(s_a0, 1)
                nc.scalar.activation(aff[0:n, t, :], m.ps[0:n, 6 + t % 2, 0:NE], ACT.Sigmoid).then_inc(s_aff, 1)

        @block.vector
        def _(dve):
            dve.wait_ge(s_c, 48)
            for t in range(NT9):
                n, b = rows_of(t), t % 2
                dve.wait_ge(s_mm, t + 1)
                dve.wait_ge(s_x[t % 3], 16 * (t // 3 + 1))
                src = m.ps[0:n, 2 * b:2 * b + 2, :].rearrange("p a c -> p (a c)")
                nc.vector.scalar_tensor_tensor(out=x1[t], in0=x1[t], scalar=ALPHA, in1=src, op0=ALU.mult,
                                               op1=ALU.add).then_inc(s_z, 1)
                dve.wait_ge(s_z, t + 1)
                normalise(nc, dve, x1[t], n, stats, mv, rstd, gain, bias, s_stat, s_mv, s_rstd, s_norm, t, s_x1)


def load_expert(nc, m, io, sp, e, slot):
    wg = io["w_gate"].rearrange("l e (p k) f -> p (l e) (k f)", k=KT)
    wu = io["w_up"].rearrange("l e (p k) f -> p (l e) (k f)", k=KT)
    wd = io["w_down"].rearrange("l e (p k) n -> p (l e) (k n)", k=FT)
    for q, w in enumerate((wg, wu, wd)):
        at = slot * 12288 + q * 4096
        src = w[:, bass.ds(e, 1), :].rearrange("p o c -> p (o c)")
        sp.dma_start(m.R3[:, at:at + 4096], src).then_inc(m.sem_expert, 16)


def route_and_dispatch(nc, m, io):
    NQ = NT9 * NE
    cursor = [0]

    def take(n):
        a = m.RK[:, cursor[0]:cursor[0] + n]
        cursor[0] += n
        return a

    def te(x):
        return x.rearrange("p (t e) -> p t e", e=NE)

    aff = m.aff.rearrange("p t e -> p (t e)")
    br, w4, w16, par = take(NE), take(4), take(NE), take(NE)
    kk, tau = take(NTC), take(MAXT)
    ones, before = take(P), take(P)
    rowmask = take(1)
    grp, vm, oh1, oh2, tmp, eqw = (take(NQ) for _ in range(6))
    M = take(NQ)
    a_, b_, c_, d_ = (take(NT9 * NG) for _ in range(4))
    gs_, goh = take(NT9 * NG), take(NT9 * NG)
    mx, mm = take(NT9), take(NT9)
    a12 = take(2 * NT9)
    tot, tb, pos = take(NQ), take(NQ), take(NQ)
    cnt, off, nt, T, Tex, tq = (take(NE) for _ in range(6))
    big1 = take(MAXT * NE)
    big2 = take(MAXT * NE)
    rowv, sumb = take(MAXT), take(MAXT)
    slotf = take(2 * NT9)
    tabf = take(3 * MAXT + NE + 1)
    zeros = take(DM)
    assert cursor[0] <= 8496
    s_b, s_c0, s_c, s_v, s_m, s_cnt = (m.sem("r_" + n) for n in ("bias", "clear", "consts", "step", "chosen", "counted"))
    s_slot, s_send = m.sem("r_slots"), m.sem("r_rows_sent")
    with nc.Block() as block:

        @block.sync
        def _(sp):
            sp.dma_start(br, io["b_router"].partition_broadcast(P)).then_inc(s_b, 16)
            sp.wait_ge(m.sem_expert, 48)
            load_expert(nc, m, io, sp, 1, 1)

        @block.gpsimd
        def _(pool):
            flt = dict(allow_small_or_imprecise_dtypes=True)
            nc.gpsimd.iota(w4, [[-1, 4]], base=4, channel_multiplier=0, **flt)
            nc.gpsimd.iota(w16, [[-1, NE]], base=NE, channel_multiplier=0, **flt)
            nc.gpsimd.iota(par.rearrange("p (a b) -> p a b", b=2), [[0, NE // 2], [12288, 2]], base=0,
                           channel_multiplier=0, **flt)
            nc.gpsimd.iota(kk, [[P, NTC]], base=0, channel_multiplier=0, **flt)
            nc.gpsimd.iota(tau, [[1, MAXT]], base=0, channel_multiplier=0, **flt)
            nc.gpsimd.memset(ones, 1.0)
            nc.gpsimd.memset(zeros, 0.0)
            nc.gpsimd.memset(before, 1.0)
            nc.gpsimd.memset(rowmask, 1.0).then_inc(s_c0, 1)
            pool.wait_ge(s_c0, 1)
            nc.gpsimd.affine_select(out=before, in_=before, compare_op=ALU.is_gt, fill=0.0, base=0,
                                    pattern=[[1, P]], channel_multiplier=-1)
            nc.gpsimd.affine_select(out=rowmask, in_=rowmask, compare_op=ALU.is_gt, fill=0.0, base=NB,
                                    pattern=[[0, 1]], channel_multiplier=-1).then_inc(s_c, 1)
            pool.wait_ge(s_c, 1)
            nc.gpsimd.dma_start(m.xs_dram[NPAIR:NROWS, :], zeros).then_inc(m.sem_stored, 16)
            pool.wait_ge(s_slot, 1)
            for t in range(NT9):
                for c in range(2):
                    n = rows_of(t)
                    col = t * 2 + c
                    nc.gpsimd.indirect_dma_start(
                        out=m.xs_dram, out_offset=bass.IndirectOffsetOnAxis(ap=m.slots[0:n, col:col + 1], axis=0),
                        in_=m.x1[t], in_offset=None).then_inc(s_send, 16)
            pool.wait_ge(s_send, 16 * 2 * NT9)
            pool.wait_ge(m.sem_stored, 16)

        @block.tensor
        def _(pe):
            pe.wait_ge(s_m, 1)
            pe.wait_ge(s_c, 1)
            nc.tensor.matmul(m.ps[:, 0, 0:NQ], before, M, start=True, stop=True)
            nc.tensor.matmul(m.ps[:, 1, 0:NQ], ones, M, start=True, stop=True).then_inc(s_cnt, 1)

        @block.vector
        def _(dve):
            steps = [0]

            def step(ins):
                steps[0] += 1
                ins.then_inc(s_v, 1)
                dve.wait_ge(s_v, steps[0])

            tt, ts, red = nc.vector.tensor_tensor, nc.vector.tensor_scalar, nc.vector.tensor_reduce

            def bc(x, shape):
                return x.to_broadcast(shape)

            def first_best(v, n, groups, width, weights, out):
                v3 = v.rearrange("p (a b) -> p a b", b=width)
                o3 = out.rearrange("p (a b) -> p a b", b=width)
                t3 = eqw[:, 0:n].rearrange("p (a b) -> p a b", b=width)
                step(red(mx[:, 0:groups], v3, AX.X, ALU.max))
                step(tt(t3, v3, bc(mx[:, 0:groups].unsqueeze(2), [P, groups, width]), ALU.is_equal))
                step(tt(t3, t3, bc(weights.unsqueeze(1), [P, groups, width]), ALU.mult))
                step(red(mm[:, 0:groups], t3, AX.X, ALU.max))
                step(tt(o3, t3, bc(mm[:, 0:groups].unsqueeze(2), [P, groups, width]), ALU.is_equal))

            dve.wait_ge(s_b, 16)
            dve.wait_ge(s_c, 1)
            step(tt(te(grp), te(aff), bc(br.unsqueeze(1), [P, NT9, NE]), ALU.add))
            v = [grp.rearrange("p (x q) -> p x q", q=EPG)[:, :, q] for q in range(EPG)]
            tt(a_, v[0], v[1], ALU.max)
            tt(b_, v[0], v[1], ALU.min)
            tt(c_, v[2], v[3], ALU.max)
            step(tt(d_, v[2], v[3], ALU.min))
            tt(gs_, a_, c_, ALU.max)
            tt(goh, a_, c_, ALU.min)
            step(tt(b_, b_, d_, ALU.max))
            step(tt(goh, goh, b_, ALU.max))
            step(tt(gs_, gs_, goh, ALU.add))
            first_best(gs_, NT9 * NG, NT9, NG, w4, goh)
            step(ts(goh, goh, 1.0, -NEG, ALU.subtract, ALU.mult))
            step(tt(vm.rearrange("p (x q) -> p x q", q=EPG), grp.rearrange("p (x q) -> p x q", q=EPG),
                    bc(goh.unsqueeze(2), [P, NT9 * NG, EPG]), ALU.add))
            first_best(vm, NQ, NT9, NE, w16, oh1)
            step(nc.vector.scalar_tensor_tensor(out=vm, in0=oh1, scalar=NEG, in1=vm, op0=ALU.mult, op1=ALU.add))
            first_best(vm, NQ, NT9, NE, w16, oh2)
            for oh in (oh1, oh2):
                step(ts(te(oh)[:, TT, :], te(oh)[:, TT, :], rowmask, None, ALU.mult))
            tt(M, oh1, oh2, ALU.add).then_inc(s_m, 1)
            wt = m.pair_w
            for c, oh in enumerate((oh1, oh2)):
                step(tt(tmp, aff, oh, ALU.mult))
                step(red(wt[:, :, c], te(tmp), AX.X, ALU.add))
            step(tt(mx, wt[:, :, 0], wt[:, :, 1], ALU.add))
            step(ts(mx, mx, 1e-38, None, ALU.max))
            step(nc.vector.reciprocal(mm, mx))
            step(tt(wt, wt, bc(mm.unsqueeze(2), [P, NT9, 2]), ALU.mult))
            dve.wait_ge(s_cnt, 1)
            step(nc.vector.tensor_copy(tot, m.ps[:, 1, 0:NQ]))
            step(nc.vector.memset(tb[:, 0:NE], 0.0))
            for t in range(1, NT9):
                step(tt(te(tb)[:, t, :], te(tb)[:, t - 1, :], te(tot)[:, t - 1, :], ALU.add))
            step(tt(cnt, te(tb)[:, TT, :], te(tot)[:, TT, :], ALU.add))
            step(nc.vector.tensor_tensor_scan(off, ones[:, 0:NE], cnt, 0.0, ALU.mult, ALU.add))
            step(tt(off, off, cnt, ALU.subtract))
            step(tt(te(pos), te(tb), bc(off.unsqueeze(1), [P, NT9, NE]), ALU.add))
            step(tt(pos, pos, m.ps[:, 0, 0:NQ], ALU.add))
            for c, oh in enumerate((oh1, oh2)):
                step(tt(tmp, pos, oh, ALU.mult))
                step(red(slotf.rearrange("p (t c) -> p t c", c=2)[:, :, c], te(tmp), AX.X, ALU.add))
            nc.vector.tensor_copy(m.slots[:], slotf).then_inc(s_slot, 1)
            r1 = slice(0, 1)
            b16k = big1[r1, 0:NE * NTC].rearrange("p (e k) -> p e k", e=NE)
            step(tt(b16k, bc(cnt[r1].unsqueeze(2), [1, NE, NTC]), bc(kk[r1].unsqueeze(1), [1, NE, NTC]), ALU.is_gt))
            step(red(nt[r1], b16k, AX.X, ALU.add))
            step(nc.vector.tensor_tensor_scan(T[r1], ones[r1, 0:NE], nt[r1], 0.0, ALU.mult, ALU.add))
            step(tt(Tex[r1], T[r1], nt[r1], ALU.subtract))
            A3 = big1[r1].rearrange("p (x e) -> p x e", e=NE)
            B3 = big2[r1].rearrange("p (x e) -> p x e", e=NE)
            tab = tabf[r1, 0:3 * MAXT].rearrange("p (x c) -> p x c", c=3)
            full = [1, MAXT, NE]
            step(tt(A3, bc(tau[r1].unsqueeze(2), full), bc(T[r1].unsqueeze(1), full), ALU.is_ge))
            step(tt(B3, bc(tau[r1].unsqueeze(2), full), bc(Tex[r1].unsqueeze(1), full), ALU.is_ge))
            step(red(tab[:, :, 2], A3, AX.X, ALU.add))
            step(tt(B3, B3, A3, ALU.subtract))
            step(ts(tab[:, :, 2], tab[:, :, 2], 48.0, 48.0, ALU.mult, ALU.add))
            step(tt(A3, B3, bc(par[r1].unsqueeze(1), full), ALU.mult))
            step(red(tab[:, :, 1], A3, AX.X, ALU.add))
            step(nc.vector.scalar_tensor_tensor(out=tq[r1], in0=Tex[r1], scalar=-float(P), in1=off[r1], op0=ALU.mult, op1=ALU.add))
            step(tt(A3, B3, bc(tq[r1].unsqueeze(1), full), ALU.mult))
            step(red(rowv[r1], A3, AX.X, ALU.add))
            step(red(sumb[r1], B3, AX.X, ALU.add))
            step(tt(sumb[r1], sumb[r1], tau[r1], ALU.mult))
            step(nc.vector.scalar_tensor_tensor(out=tab[:, :, 0], in0=sumb[r1], scalar=float(P), in1=rowv[r1], op0=ALU.mult, op1=ALU.add))
            step(ts(tabf[r1, 3 * MAXT:3 * MAXT + NE], T[r1], 1.0, None, ALU.add))
            step(nc.vector.tensor_copy(tabf[r1, 3 * MAXT + NE:3 * MAXT + NE + 1], T[r1, NE - 1:NE]))
            step(nc.vector.tensor_copy(m.table[:], tabf[r1]))


def experts(nc, m, io):
    base = 8192
    xg = m.RW[:, base:base + DM]
    xgT = view(m.RW, base + DM, KT, P)
    silu = m.RW[:, base + 2048:base + 2560]
    h = m.RW[:, base + 2560:base + 3072]
    hT = view(m.RW, base + 3072, FT, P)
    y = m.RW[:, base + 4096:base + 5120]
    s_x, s_xt, s_xk = m.sem("e_rows_in"), m.sem("e_rows_turned"), m.sem("e_rows_kept")
    s_g, s_u, s_silu, s_h, s_ht, s_hk = (m.sem("e_" + n) for n in ("gate", "up", "silu", "hidden", "hidden_turned", "hidden_kept"))
    s_d, s_y0, s_y1, s_done = m.sem("e_down"), m.sem("e_out0"), m.sem("e_out1"), m.sem("e_tiles_through")
    tiles = slice(3 * MAXT + NE, 3 * MAXT + NE + 1)
    with nc.Block() as block:

        @block.sync
        def _(sp):
            with sp.Fori(1, NE // 2) as ee:
                for b in range(2):
                    free = sp.value_load(m.table[0:1, bass.ds(2 * ee + (3 * MAXT + b - 2), 1)], min_val=1, max_val=MAXT + 1)
                    sp.wait_ge(m.sem_expert, 96 * ee + 48 * b)
                    sp.wait_ge(s_done, free)
                    sp.wait_ge(m.sem_expert, 96)
                    load_expert(nc, m, io, sp, 2 * ee + b, b)

        @block.gpsimd
        def _(pool):
            def load(t):
                row = pool.value_load(m.table[0:1, bass.ds(3 * t, 1)], min_val=0, max_val=NPAIR)
                nc.gpsimd.dma_start(xg, m.xs_dram[bass.ds(row, P), :]).then_inc(s_x, 16)
                return row

            row = load(0)
            n = pool.value_load(m.table[0:1, tiles], min_val=1, max_val=MAXT - 1)
            with pool.Fori(0, n) as t:
                pool.wait_ge(s_xt, t + 1)
                load(t + 1)
                row = pool.value_load(m.table[0:1, bass.ds(3 * t, 1)], min_val=0, max_val=NPAIR)
                pool.wait_ge(s_y0, t + 1)
                pool.wait_ge(s_y1, t + 1)
                pool.wait_ge(m.sem_stored, 16 * t + 16)
                nc.gpsimd.dma_start(m.ys_dram[bass.ds(row, P), :], y).then_inc(m.sem_stored, 16)
            pool.wait_ge(m.sem_stored, 16 * n + 16)
            pool.wait_ge(s_x, 16 * n + 16)

        @block.tensor
        def _(pe):
            def turn_rows(t):
                pe.wait_ge(s_x, 16 * t + 16)
                for k in range(KT):
                    last = nc.tensor.transpose(m.ps[:, 2 + k // 4, (k % 4) * P:(k % 4 + 1) * P], xg[:, k:DM:KT], m.ident[:])
                last.then_inc(s_xt, 1)

            pe.nop().then_inc(s_done, 1)
            turn_rows(0)
            n = pe.value_load(m.table[0:1, tiles], min_val=1, max_val=MAXT - 1)
            with pe.Fori(0, n) as t:
                slot = pe.value_load(m.table[0:1, bass.ds(3 * t + 1, 1)], min_val=0, max_val=12288)
                ready = pe.value_load(m.table[0:1, bass.ds(3 * t + 2, 1)], min_val=48, max_val=48 * (NE + 1))
                pe.wait_ge(m.sem_expert, ready)
                pe.wait_ge(s_xk, t + 1)
                for q, s in ((0, s_g), (1, s_u)):
                    for k in range(KT):
                        last = nc.tensor.matmul(m.ps[:, q, :], xgT[:, k, :], m.R3[:, bass.ds(slot + (q * 4096 + k * 512), 512)],
                                                start=(k == 0), stop=(k == KT - 1))
                    last.then_inc(s, 1)
                turn_rows(t + 1)
                pe.wait_ge(s_h, t + 1)
                for k in range(FT):
                    last = nc.tensor.transpose(m.ps[:, 4, k * P:(k + 1) * P], h[:, k:FE:FT], m.ident[:])
                last.then_inc(s_ht, 1)
                pe.wait_ge(s_hk, t + 1)
                for c in range(2):
                    for k in range(FT):
                        last = nc.tensor.matmul(m.ps[:, 5 + c, :], hT[:, k, :],
                                                m.R3[:, bass.ds(slot + (8192 + k * DM + c * 512), 512)],
                                                start=(k == 0), stop=(k == FT - 1))
                    last.then_inc(s_d if c == 0 else s_done, 1)

        @block.scalar
        def _(act):
            n = act.value_load(m.table[0:1, tiles], min_val=1, max_val=MAXT - 1)
            with act.Fori(0, n) as t:
                act.wait_ge(s_g, t + 1)
                nc.scalar.activation(silu, m.ps[:, 0, :], ACT.Silu).then_inc(s_silu, 1)
                act.wait_ge(s_done, t + 2)
                act.wait_ge(m.sem_stored, 16 * t + 16)
                nc.scalar.copy(y[:, 512:DM], m.ps[:, 6, :]).then_inc(s_y1, 1)

        @block.vector
        def _(dve):
            def keep_rows(t):
                dve.wait_ge(s_xt, t + 1)
                nc.vector.tensor_copy(xgT.rearrange("p (a k) c -> p a (k c)", a=2), m.ps[:, 2:4, :]).then_inc(s_xk, 1)

            keep_rows(0)
            n = dve.value_load(m.table[0:1, tiles], min_val=1, max_val=MAXT - 1)
            with dve.Fori(0, n) as t:
                dve.wait_ge(s_silu, t + 1)
                dve.wait_ge(s_u, t + 1)
                nc.vector.tensor_tensor(h, silu, m.ps[:, 1, :], ALU.mult).then_inc(s_h, 1)
                dve.wait_ge(s_ht, t + 1)
                nc.vector.tensor_copy(hT.rearrange("p k c -> p (k c)"), m.ps[:, 4, :]).then_inc(s_hk, 1)
                keep_rows(t + 1)
                dve.wait_ge(s_d, t + 1)
                dve.wait_ge(m.sem_stored, 16 * t + 16)
                nc.vector.tensor_copy(y[:, 0:512], m.ps[:, 5, :]).then_inc(s_y0, 1)


def combine(nc, m, io):
    yg = [[m.R3[:, (2 * t + c) * DM:(2 * t + c + 1) * DM] for c in range(2)] for t in range(NT9)]
    gain, bias = m.RK[:, 0:DM], m.RK[:, DM:2 * DM]
    sc = m.RK[:, 2 * DM:2 * DM + 20 * NT9].rearrange("p (t c) -> p t c", t=NT9)
    s_c, s_m1, s_z = m.sem("c_consts"), m.sem("c_scaled"), m.sem("c_added")
    s_g = [m.sem(f"c_gathered{t}") for t in range(NT9)]
    s_stat, s_mv, s_eps, s_rstd, s_norm = (m.sem("c_" + n) for n in ("stats", "moments", "eps", "rstd", "normal"))
    s_gain, s_y, s_out = m.sem("c_gain"), m.sem("c_y"), m.sem("c_out")
    s_nm = m.sem("c_shift")
    yp = io["y_prompt"].rearrange("a (t p) d -> p (a t) d", p=P)
    ys = io["y_sample"].rearrange("b t d -> (b t) d")
    with nc.Block() as block:

        @block.sync
        def _(sp):
            sp.dma_start(gain, io["ln2_g"].rearrange("l d -> (l d)").partition_broadcast(P)).then_inc(s_c, 16)
            sp.dma_start(bias, io["ln2_b"].rearrange("l d -> (l d)").partition_broadcast(P)).then_inc(s_c, 16)
            for t in range(NT9):
                sp.wait_ge(s_y, t + 1)
                sp.dma_start(yp[:, t, :] if t < TT else ys, m.x1[t]).then_inc(s_out, 16)
            sp.wait_ge(s_out, 16 * NT9)

        @block.gpsimd
        def _(pool):
            def scale_rows(t):
                n = rows_of(t)
                pool.wait_ge(s_norm, t + 1)
                nc.gpsimd.tensor_tensor(m.x1[t], m.x1[t], gain[0:n], ALU.mult).then_inc(s_gain, 1)

            for t in range(NT9):
                n = rows_of(t)
                for c in range(2):
                    col = 2 * t + c
                    nc.gpsimd.indirect_dma_start(
                        out=yg[t][c][0:n], out_offset=None, in_=m.ys_dram[0:NPAIR, :],
                        in_offset=bass.IndirectOffsetOnAxis(ap=m.slots[0:n, col:col + 1], axis=0)).then_inc(s_g[t], 16)
            pool.wait_ge(s_c, 32)
            for t in range(NT9):
                n = rows_of(t)
                inverse_deviation(nc, m, pool, n, sc[:, t, 12:14], sc[:, t, 14:15], s_mv, s_eps, s_rstd, t)
                if t >= 1:
                    scale_rows(t - 1)
            scale_rows(TT)

        @block.scalar
        def _(act):
            def normal(t):
                n = rows_of(t)
                act.wait_ge(s_nm, t + 1)
                nc.scalar.activation(m.x1[t], m.x1[t], ACT.Identity, bias=sc[0:n, t, 15:16],
                                     scale=sc[0:n, t, 14:15]).then_inc(s_norm, 1)

            for t in range(NT9):
                n = rows_of(t)
                act.wait_ge(s_g[t], 32)
                nc.scalar.mul(yg[t][0][0:n], yg[t][0][0:n], m.pair_w[0:n, t, 0:1]).then_inc(s_m1, 1)
                if t >= 1:
                    normal(t - 1)
            normal(TT)

        @block.vector
        def _(dve):
            stt = nc.vector.scalar_tensor_tensor

            def add(t):
                n = rows_of(t)
                dve.wait_ge(s_m1, t + 1)
                stt(out=m.x1[t], in0=m.x1[t], scalar=ALPHA, in1=yg[t][0][0:n], op0=ALU.mult, op1=ALU.add).then_inc(s_z, 1)
                dve.wait_ge(s_z, 2 * t + 1)
                stt(out=m.x1[t], in0=yg[t][1][0:n], scalar=m.pair_w[0:n, t, 1:2], in1=m.x1[t], op0=ALU.mult,
                    op1=ALU.add).then_inc(s_z, 1)
                dve.wait_ge(s_z, 2 * t + 2)
                nc.vector.bn_stats(sc[0:n, t, 0:6], m.x1[t][:, 0:512])
                nc.vector.bn_stats(sc[0:n, t, 6:12], m.x1[t][:, 512:1024]).then_inc(s_stat, 1)
                dve.wait_ge(s_stat, t + 1)
                nc.vector.bn_aggr(sc[0:n, t, 12:14], sc[0:n, t, 0:12]).then_inc(s_mv, 1)

            def shift(t):
                n = rows_of(t)
                dve.wait_ge(s_rstd, t + 1)
                stt(out=sc[0:n, t, 15:16], in0=sc[0:n, t, 12:13], scalar=-1.0, in1=sc[0:n, t, 14:15], op0=ALU.mult,
                    op1=ALU.mult).then_inc(s_nm, 1)

            def bias_rows(t):
                n = rows_of(t)
                dve.wait_ge(s_gain, t + 1)
                nc.vector.tensor_tensor(m.x1[t], m.x1[t], bias[0:n], ALU.add).then_inc(s_y, 1)

            dve.wait_ge(s_c, 32)
            for t in range(NT9 + 2):
                if t < NT9:
                    add(t)
                if 1 <= t <= NT9:
                    shift(t - 1)
                if t >= 2:
                    bias_rows(t - 2)


_INS = ["x_prompt", "x_sample", "cache_kv", "cache_win", "page_table", "w_in", "gmlp_ln_g", "gmlp_ln_b", "gmlp_ws",
        "gmlp_bs", "cmp_pos", "cmp_w1", "cmp_w2", "w_branch_a", "w_branch_b", "w_out", "ln1_g", "ln1_b", "ln2_g",
        "ln2_b", "w_router", "b_router", "w_gate", "w_up", "w_down"]
_OUTS = [("y_prompt", (1, SEQ, DM)), ("y_sample", (NB, 1, DM)), ("kv_rows_prompt", (1, 1, SEQ, 4, NKV, HD)),
         ("win_prompt", (1, 1, WINDOW, 2, NKV, HD)), ("kv_rows_sample", (NB, 1, 1, 4, NKV, HD)),
         ("win_sample", (NB, 1, PAST, 2, NKV, HD)), ("gmlp_v_sample", (NB, 1, 1, DM))]


def program(nc, io, upto=99):
    with ExitStack() as ctx:
        m = Memory(nc, ctx)
        stages = [lambda: load_and_turn_x(nc, m, io), lambda: project_kv(nc, m, io), lambda: project_q(nc, m, io),
                  lambda: compress_keys(nc, m, io), lambda: attend_samples(nc, m, io), lambda: attend_prompt(nc, m),
                  lambda: gmlp_values(nc, m, io), lambda: gmlp_gate(nc, m, io), lambda: merge(nc, m, io),
                  lambda: output_and_router(nc, m, io), lambda: route_and_dispatch(nc, m, io),
                  lambda: experts(nc, m, io), lambda: combine(nc, m, io)]
        for stage in stages[:upto]:
            stage()
            if stage is stages[5]:
                m.clear_semaphores()


def kernel(**inputs):
    from concourse import bacc
    from concourse.bass_utils import run_bass_kernel_spmd

    nc = bacc.Bacc("TRN2", target_bir_lowering=False, num_devices=1)
    arrays, io = {}, {}
    for name in _INS:
        a = np.ascontiguousarray(inputs[name])
        arrays[f"in_{name}"] = a
        io[name] = nc.dram_tensor(f"in_{name}", a.shape, mybir.dt.from_np(a.dtype), kind="ExternalInput").ap()
    for name, shape in _OUTS:
        io[name] = nc.dram_tensor(f"out_{name}", shape, F32, kind="ExternalOutput").ap()
    program(nc, io)
    r = run_bass_kernel_spmd(nc, [arrays], core_ids=[0])
    return tuple(r.results[0][f"out_{name}"] for name, _ in _OUTS)
```

```python
from contextlib import ExitStack

import concourse.bass as bass
import numpy as np
from concourse import mybir
from concourse.alu_op_type import AluOpType as ALU

F32 = mybir.dt.float32
F32R = mybir.dt.float32r
BF16 = mybir.dt.bfloat16
I32 = mybir.dt.int32
U32 = mybir.dt.uint32
ACT = mybir.ActivationFunctionType
AX = mybir.AxisListType

P = 128
DM = 1024
SEQ = 1024
NB = 8
NTOK = SEQ + NB
TT = SEQ // P
NT9 = TT + 1
KT = DM // P
NH, NKV, HD = 16, 2, 64
QPK = NH // NKV
CMP_STRIDE, CMP_BLOCK = 16, 32
NCMP = SEQ // CMP_STRIDE - 1
PAST, PAGE = 256, 128
NPAGE = PAST // PAGE
NPG = NB * NPAGE
CKEYS = NB * PAST
SCMP = PAST // CMP_STRIDE - 1
WINDOW = 512
WBLK = WINDOW // P
NEG = -1e30
SCALE = HD ** -0.5
ALPHA = 2.0 ** 0.25
EPS = 1e-5
NE, NG, EPG = 16, 4, 4
FE = 512
FT = FE // P
NPAIR = 2 * NTOK
EROWS = 216
EREST = EROWS - P
NROWS = NPAIR + EROWS
NEXTRA = (NPAIR - 1) // EROWS
NKX = (NTOK - 1) // EROWS
NSTEP = NE + NEXTRA
COL_V, COL_Q, COL_KV = 1024, 2048, 3072
COL_GA, COL_GB = 3888, 4912
KVW = 6 * 128 + 3 * NH
KVH = KVW // 2


def rows_of(t):
    return P if t < TT else NB


def span(t):
    return slice(t * P, t * P + rows_of(t))


class Memory:

    def __init__(self, nc, ctx):
        self.nc, self.ctx, self.sems = nc, ctx, []
        self.at_R3 = -(-nc.sbuf_base // 32) * 32
        self.R3 = self.sb("region_3", [P, 3 * KT * NTOK])
        self.RO = self.R3[:, KT * NTOK:2 * KT * NTOK]
        self.RA = self.R3[:, 2 * KT * NTOK:3 * KT * NTOK]
        self.RK = self.sb("region_k", [P, 8496])
        self.at_RW = -(-nc.sbuf_base // 32) * 32
        self.RW = self.sb("region_w", [P, 16384])
        self.ps = ctx.enter_context(nc.psum_tensor("ps", [P, 8, 512], F32))
        self.ident = self.sb("ident", [P, P])
        self.gates = self.sb("gates", [P, NT9, 3 * NH])
        self.xT = view(self.R3, 0, KT, NTOK)
        self.qT = view(self.RO, 0, KT, NTOK)
        self.aT = view(self.RA, 0, KT, NTOK)
        self.kT = view(self.RK, 0, 4, NTOK)
        self.vv = view(self.RK, 4 * NTOK, NT9, 256)
        self.kvst = view(self.RK, 4 * NTOK + NT9 * 256, 2, KVW)
        self.small = self.sb("small", [P, 1408])
        self.k_stacks = self.parts("key_stacks", self.at_RW + 4 * 6144, 8 * SEQ).rearrange(
            "p (a g h n) -> p a g h n", a=2, g=NKV, h=2)
        self.kc_stacks = self.sb("compressed_key_stacks", [P, NKV, 2, 64], F32R)
        self.q_stacks = self.parts("query_stacks", self.at_RW + 4 * 14336, 2 * SEQ).rearrange("p (g n) -> p g n", g=NKV)
        self.wg_parts, self.wu_parts, self.wd_parts = (
            self.parts(n + "_parts", self.at_R3 + 4 * 8192 * q, 8192) for q, n in enumerate(("gate", "up", "down")))
        self.xg_parts = self.parts("rows_parts", self.at_RW + 4 * 8192, 2 * KT * EROWS)
        self.h_parts = self.parts("hidden_parts", self.at_RW + 4 * 8192 + 4 * 2 * KT * EROWS, 2 * FT * EROWS)
        self.kcT = self.sb("kcT", [P, 2 * P])
        self.vc = self.sb("vc", [P, 2, P])
        self.gs = self.sb("gates_sample_rows", [P, 3])
        self.page_ids = self.sb("page_ids", [1, NPG], I32)
        self.identb = self.sb("ident_bf16", [P, P], BF16)
        self.mask_diag = self.sb("mask_diag", [P, P], BF16)
        self.mask_edge = self.sb("mask_edge", [P, P], BF16)
        self.mask_cmp = self.sb("mask_cmp", [P, 56 + NCMP], BF16)
        self.x1 = [self.RW[:, t * DM:(t + 1) * DM] for t in range(TT)] + [self.small[0:NB, 0:DM]]
        self.aff = self.small[:, 1024:1024 + NT9 * NE].rearrange("p (t e) -> p t e", e=NE)
        self.pair_w = self.small[:, 1168:1168 + 2 * NT9].rearrange("p (t c) -> p t c", c=2)
        self.sem_wout, self.sem_gate, self.sem_up, self.sem_down, self.sem_stored = (
            ctx.enter_context(nc.semaphore(n)) for n in ("w_out_in", "gate_in", "up_in", "down_in", "rows_stored"))
        self.mhalf = self.sb("minus_half", [P, 1])
        self.table = self.sb("tile_table", [1, 2 * NSTEP + 2], I32)
        self.slots = self.sb("slots", [P, 2 * NT9], U32)
        self.x1_dram = nc.dram_tensor("x1_prompt", [SEQ, DM], F32, kind="Internal").ap()
        self.xs_dram = nc.dram_tensor("dispatched", [NROWS, DM], F32, kind="Internal").ap()
        self.ys_dram = nc.dram_tensor("expert_out", [NROWS, DM], F32, kind="Internal").ap()
        self.gate_dram = nc.dram_tensor("gate_scratch", [NB, 3 * NH], F32, kind="Internal").ap()

    def sb(self, name, shape, dt=F32):
        return self.ctx.enter_context(self.nc.sbuf_tensor(name, shape, dt))

    def parts(self, name, offset, n):
        return self.nc.alloc_sbuf_tensor_at(name, [P, n], F32R, offset=offset)[:]

    def sem(self, name):
        self.sems.append(self.nc.alloc_semaphore(name))
        return self.sems[-1]

    def clear_semaphores(self):
        self.nc.clear_and_free_semaphores(self.sems)
        self.sems = []
        self.nc.all_engine_barrier()


def view(region, offset, a, b, parts=P):
    return region[0:parts, offset:offset + a * b].rearrange("p (a b) -> p a b", a=a)


def load_and_turn_x(nc, m, io):
    xst = view(m.RK, 0, 2, DM)
    s_in = [m.sem("x_in0"), m.sem("x_in1")]
    s_turned, s_kept = m.sem("x_turned"), m.sem("x_kept")
    s_id0, s_id = m.sem("ident_clear"), m.sem("ident_ready")
    s_m0, s_m = m.sem("masks_clear"), m.sem("masks_ready")
    xp = io["x_prompt"].rearrange("a (t p) d -> p (a t) d", p=P)
    xs = io["x_sample"].rearrange("b t d -> (b t) d")
    with nc.Block() as block:

        @block.sync
        def _(sp):
            for t in range(NT9):
                if t >= 2:
                    sp.wait_ge(s_turned, t - 1)
                src = xp[:, t, :] if t < TT else xs
                sp.dma_start(xst[0:rows_of(t), t % 2, :], src).then_inc(s_in[t % 2], 16)

        @block.gpsimd
        def _(pool):
            nc.gpsimd.memset(m.ident[:], 0.0).then_inc(s_id0, 1)
            pool.wait_ge(s_id0, 1)
            nc.gpsimd.affine_select(out=m.ident[:], in_=m.ident[:], compare_op=ALU.not_equal, fill=1.0,
                                    base=0, pattern=[[-1, P]], channel_multiplier=1).then_inc(s_id, 1)
            pool.wait_ge(s_id, 1)
            nc.gpsimd.tensor_copy(m.identb[:], m.ident[:])
            nc.gpsimd.memset(m.mhalf[:], -0.5)
            for mask in (m.mask_diag, m.mask_edge, m.mask_cmp):
                nc.gpsimd.memset(mask[:], 0.0).then_inc(s_m0, 1)
            pool.wait_ge(s_m0, 3)
            nc.gpsimd.affine_select(out=m.mask_diag[:], in_=m.mask_diag[:], compare_op=ALU.is_ge, fill=NEG,
                                    base=0, pattern=[[-1, P]], channel_multiplier=1)
            nc.gpsimd.affine_select(out=m.mask_edge[:], in_=m.mask_edge[:], compare_op=ALU.is_gt, fill=NEG,
                                    base=0, pattern=[[1, P]], channel_multiplier=-1)
            nc.gpsimd.affine_select(out=m.mask_cmp[:], in_=m.mask_cmp[:], compare_op=ALU.is_ge, fill=NEG,
                                    base=56 * CMP_STRIDE - (CMP_BLOCK - 1), pattern=[[-CMP_STRIDE, 56 + NCMP]],
                                    channel_multiplier=1).then_inc(s_m, 1)
            pool.wait_ge(s_m, 1)

        @block.tensor
        def _(pe):
            pe.wait_ge(s_id, 1)
            for t in range(NT9):
                n, bank = rows_of(t), 2 * (t % 2)
                pe.wait_ge(s_in[t % 2], 16 * (t // 2 + 1))
                if t >= 2:
                    pe.wait_ge(s_kept, t - 1)
                for k in range(KT):
                    out = m.ps[:, bank + k // 4, (k % 4) * P:(k % 4) * P + n]
                    last = nc.tensor.transpose(out, xst[0:n, t % 2, k * P:(k + 1) * P], m.ident[0:n, 0:n])
                last.then_inc(s_turned, 1)

        @block.vector
        def _(dve):
            for t in range(NT9):
                dve.wait_ge(s_turned, t + 1)
                bank = 2 * (t % 2)
                src = m.ps[:, bank:bank + 2, :].rearrange("p b (k c) -> p (b k) c", k=4)[:, :, 0:rows_of(t)]
                nc.vector.tensor_copy(m.xT[:, :, span(t)], src).then_inc(s_kept, 1)


def project_kv(nc, m, io):
    wkv = view(m.RW, 0, KT, KVW)
    st = m.kvst
    s_w, s_proj, s_row, s_gate = (m.sem(n) for n in ("kv_w", "kv_projected", "kv_rows_staged", "kv_gates"))
    s_vv, s_turned, s_kept = m.sem("kv_values"), m.sem("kv_turned"), m.sem("kv_kept")
    s_out = [m.sem("kv_out0"), m.sem("kv_out1")]
    s_gd, s_gw = m.sem("gates_bounced"), m.sem("gates_scattered")
    s_win = m.sem("win_sample_out")
    kvp = io["kv_rows_prompt"].rearrange("a l (t p) s h d -> p (a l t) (s h d)", p=P)
    kvs = io["kv_rows_sample"].rearrange("b l t s h d -> (b l t) (s h d)")
    winp = io["win_prompt"].rearrange("a l (t p) s h d -> p (a l t) (s h d)", p=P)
    wins = io["win_sample"].rearrange("b l w s h d -> b (l w) (s h d)")
    cwin = io["cache_win"].rearrange("b l w s h d -> b (l w) (s h d)")
    w_in = io["w_in"].rearrange("l (k p) n -> p (l k) n", p=P)
    outs = [0, 0]

    with nc.Block() as block:

        @block.sync
        def _(sp):
            for h in range(2):
                sp.dma_start(wkv[:, :, h * KVH:(h + 1) * KVH],
                             w_in[:, :, COL_KV + h * KVH:COL_KV + (h + 1) * KVH]).then_inc(s_w, 16)
            sp.dma_start(wins[:, 0:PAST - 1, :], cwin[:, 1:PAST, :]).then_inc(s_win, 16)
            for t in range(NT9):
                n, b = rows_of(t), t % 2
                sp.wait_ge(s_row, t + 1)
                dst = kvp[:, t, :] if t < TT else kvs
                sp.dma_start(dst, st[0:n, b, 0:512]).then_inc(s_out[b], 16)
                outs[b] += 16
                if t >= TT // 2:
                    dst = winp[:, t - TT // 2, :] if t < TT else wins[:, PAST - 1, :]
                    sp.dma_start(dst, st[0:n, b, 512:768]).then_inc(s_out[b], 16)
                    outs[b] += 16
            sp.wait_ge(s_gate, NT9)
            sp.dma_start(m.gate_dram, m.gates[0:NB, TT, :]).then_inc(s_gd, 16)
            sp.wait_ge(s_gd, 16)
            for h in range(NH):
                sp.dma_start(m.gs[h * NB:(h + 1) * NB, :], m.gate_dram[:, 3 * h:3 * h + 3]).then_inc(s_gw, 16)
            for b in range(2):
                sp.wait_ge(s_out[b], outs[b])
            sp.wait_ge(s_win, 16)
            sp.wait_ge(s_gw, 16 * NH)

        @block.tensor
        def _(pe):
            def turn(t):
                n = rows_of(t)
                pe.wait_ge(s_row, t + 1)
                if t >= 2:
                    pe.wait_ge(s_kept, t - 1)
                for c, col in enumerate((0, 128, 256, 512)):
                    last = nc.tensor.transpose(m.ps[:, 6 + t % 2, c * P:c * P + n], st[0:n, t % 2, col:col + P],
                                               m.ident[0:n, 0:n])
                last.then_inc(s_turned, 1)

            pe.wait_ge(s_w, 32)
            for t in range(NT9):
                n = rows_of(t)
                if t >= 2:
                    pe.wait_ge(s_row, t - 1)
                for h in range(2):
                    for k in range(KT):
                        last = nc.tensor.matmul(m.ps[0:n, 2 * (t % 2) + h, 0:KVH], m.xT[:, k, span(t)],
                                                wkv[:, k, h * KVH:(h + 1) * KVH], start=(k == 0), stop=(k == KT - 1))
                last.then_inc(s_proj, 1)
                if t >= 1:
                    turn(t - 1)
            turn(NT9 - 1)

        @block.scalar
        def _(act):
            for t in range(NT9):
                n, b = rows_of(t), t % 2
                act.wait_ge(s_proj, t + 1)
                if t >= 2:
                    act.wait_ge(s_turned, t - 1)
                    done = 16 * ((t - 2) // 2 + 1) + 16 * sum(1 for u in range(b, t - 1, 2) if u >= TT // 2)
                    act.wait_ge(s_out[b], done)
                    act.wait_ge(s_vv, t - 1)
                src = m.ps[0:n, 2 * b:2 * b + 2, 0:KVH]
                nc.scalar.copy(st[0:n, b, :].rearrange("p (h c) -> p h c", h=2), src).then_inc(s_row, 1)
                act.wait_ge(s_row, t + 1)
                nc.scalar.activation(m.gates[0:n, t, :], st[0:n, b, 768:KVW], ACT.Sigmoid).then_inc(s_gate, 1)

        @block.vector
        def _(dve):
            for t in range(NT9):
                n, b = rows_of(t), t % 2
                dve.wait_ge(s_row, t + 1)
                src = st[0:n, b, 384:896 - 128].rearrange("p (a c) -> p a c", c=P)[:, 0:3:2, :]
                nc.vector.tensor_copy(m.vv[0:n, t, :].rearrange("p (a c) -> p a c", a=2), src).then_inc(s_vv, 1)
                dve.wait_ge(s_turned, t + 1)
                src = m.ps[:, 6 + b, :].rearrange("p (a c) -> p a c", a=4)[:, :, 0:n]
                nc.vector.tensor_copy(m.kT[:, :, span(t)], src).then_inc(s_kept, 1)


def project_q(nc, m, io):
    wq = [view(m.RA, 0, KT, P), view(m.RA, KT * P, KT, P)]
    s_w = [m.sem("q_w0"), m.sem("q_w1")]
    s_proj, s_kept = m.sem("q_projected"), m.sem("q_kept")
    w_in = io["w_in"].rearrange("l (k p) n -> p (l k) n", p=P)
    with nc.Block() as block:

        @block.sync
        def _(sp):
            def load(j, b):
                for g in range(NKV):
                    col = j * HD + (COL_Q + g * QPK * HD)
                    sp.dma_start(wq[b][:, :, g * HD:(g + 1) * HD], w_in[:, :, bass.ds(col, HD)]).then_inc(s_w[b], 16)

            for b in range(2):
                load(b, b)
            with sp.Fori(1, KT // 2) as jj:
                for b in range(2):
                    sp.wait_ge(s_proj, 2 * jj + (b - 1))
                    load(2 * jj + b, b)

        @block.tensor
        def _(pe):
            def tile(b, jj=None):
                pe.wait_ge(s_w[b], 32 if jj is None else 32 * jj + 32)
                if jj is not None:
                    pe.wait_ge(s_kept, 2 * jj + (b - 1))
                for c in range(3):
                    cols = slice(c * 512, min((c + 1) * 512, NTOK))
                    for k in range(KT):
                        last = nc.tensor.matmul(m.ps[:, 3 * b + c, 0:cols.stop - cols.start], wq[b][:, k, :],
                                                m.xT[:, k, cols], start=(k == 0), stop=(k == KT - 1))
                last.then_inc(s_proj, 1)

            for b in range(2):
                tile(b)
            with pe.Fori(1, KT // 2) as jj:
                for b in range(2):
                    tile(b, jj)

        @block.vector
        def _(dve):
            with dve.Fori(0, KT // 2) as jj:
                for b in range(2):
                    dve.wait_ge(s_proj, 2 * jj + (b + 1))
                    at = (2 * jj + b) * NTOK
                    src = m.ps[:, 3 * b:3 * b + 2, :].rearrange("p a c -> p (a c)")
                    nc.vector.tensor_scalar(m.RO[:, bass.ds(at, SEQ)], src, SCALE, None, ALU.mult)
                    nc.vector.tensor_scalar(m.RO[:, bass.ds(at + SEQ, NB)], m.ps[:, 3 * b + 2, 0:NB],
                                            SCALE, None, ALU.mult).then_inc(s_kept, 1)


def compress_keys(nc, m, io):
    w1 = [view(m.RA, c * 4096, CMP_BLOCK, P) for c in range(2)]
    pages = view(m.RW, 0, NPG, 256)
    cT = view(m.RW, 4096, 2, CKEYS)
    small = m.small
    w2 = small[:, 0:128].rearrange("p (c d) -> p c d", c=2)
    pos = small[0:CMP_BLOCK, 128:256]
    posT = small[0:HD, 256:320].rearrange("p (c s) -> p c s", c=2)
    bias = small[:, 320:322]
    hid = small[:, 384:384 + 8 * P].rearrange("p (u n) -> p u n", u=8)
    s_w1, s_w2, s_pt, s_page = m.sem("cmp_w1"), m.sem("cmp_w2"), m.sem("page_table_in"), m.sem("cmp_pages")
    s_posT, s_posk = m.sem("pos_turned"), m.sem("pos_kept")
    s_bias, s_biask = m.sem("cmp_bias"), m.sem("cmp_bias_kept")
    s_turned, s_kept = m.sem("cmp_turned"), m.sem("cmp_turned_kept")
    s_hid, s_act, s_out, s_end = m.sem("cmp_hidden"), m.sem("cmp_gelu"), m.sem("cmp_outputs"), m.sem("cmp_kept")
    cache = io["cache_kv"].rearrange("n l p s h d -> (n l) p (s h d)")
    units = [(src, c, g) for src in range(2) for c in range(2) for g in range(2)]
    nkeys = (NCMP, NB * SCMP)
    with nc.Block() as block:

        @block.sync
        def _(sp):
            pt = io["page_table"].rearrange("(o b) n -> o (b n)", o=1)
            sp.dma_start(m.page_ids[:], pt).then_inc(s_pt, 16)
            for c in range(2):
                w = io["cmp_w1"][0, c].rearrange("(s d) f -> d s f", d=HD)
                for g in range(2):
                    sp.dma_start(w1[c][g * HD:(g + 1) * HD], w).then_inc(s_w1, 16)
            sp.dma_start(w2, io["cmp_w2"].rearrange("l c f d -> f (l c) d")).then_inc(s_w2, 16)
            sp.dma_start(pos.rearrange("s (c d) -> s c d", c=2),
                         io["cmp_pos"].rearrange("l c s d -> s (l c) d")).then_inc(s_w2, 16)
            sp.wait_ge(s_pt, 16)
            with sp.Fori(0, NPG) as i:
                page = sp.value_load(m.page_ids[0:1, bass.ds(i, 1)], min_val=0, max_val=cache.shape[0] - 1)
                sp.dma_start(m.RW[:, bass.ds(i * 256, 256)],
                             cache[bass.ds(page, 1), :, 0:256].rearrange("n p c -> p (n c)")).then_inc(s_page, 16)

        @block.tensor
        def _(pe):
            pe.wait_ge(s_w2, 32)
            for c in range(2):
                last = nc.tensor.transpose(m.ps[0:HD, 0, c * 32:c * 32 + 32], pos[:, c * HD:(c + 1) * HD],
                                           m.ident[0:32, 0:32])
            last.then_inc(s_posT, 1)
            pe.wait_ge(s_posk, 1)
            pe.wait_ge(s_w1, 64)
            for c in range(2):
                for s in range(CMP_BLOCK):
                    last = nc.tensor.matmul(m.ps[:, 1, c:c + 1], w1[c][0:HD, s, :], posT[:, c, s:s + 1],
                                            start=(s == 0), stop=(s == CMP_BLOCK - 1))
            last.then_inc(s_bias, 1)

            def hidden(u):
                src, c, g = units[u]
                rows = slice(g * HD, (g + 1) * HD)
                for s in range(CMP_BLOCK):
                    if src == 0:
                        rhs = m.kT[rows, c, s:s + CMP_STRIDE * (NCMP - 1) + 1:CMP_STRIDE]
                    else:
                        rhs = cT[rows, c, :].rearrange("p (b t) -> p b t", b=NB)[
                            :, :, s:s + CMP_STRIDE * (SCMP - 1) + 1:CMP_STRIDE]
                    out = m.ps[:, 2 + u % 2, 0:nkeys[src]]
                    last = nc.tensor.matmul(out, w1[c][rows, s, :], rhs, start=(s == 0), stop=(s == CMP_BLOCK - 1))
                last.then_inc(s_hid, 1)

            def outputs(src):
                n = nkeys[src]
                for g in range(2):
                    nc.tensor.matmul(m.ps[g * HD:(g + 1) * HD, 6, 0:n], w2[:, 0, :], hid[:, 4 * src + g, 0:n],
                                     start=True, stop=True)
                for g in range(2):
                    last = nc.tensor.matmul(m.ps[0:n, 7, g * HD:(g + 1) * HD], hid[:, 4 * src + 2 + g, 0:n],
                                            w2[:, 1, :], start=(g == 0), stop=(g == 1), skip_group_check=True)
                last.then_inc(s_out, 1)

            for u in range(4):
                if u >= 2:
                    pe.wait_ge(s_act, u - 1)
                hidden(u)
            for q in range(NPG // 4):
                for c in range(2):
                    i = 2 * q + c
                    if c == 0:
                        pe.wait_ge(s_page, 16 * NPG)
                    if i >= 2:
                        pe.wait_ge(s_kept, i - 1)
                    for r in range(4):
                        last = nc.tensor.transpose(m.ps[:, 4 + i % 2, r * P:(r + 1) * P],
                                                   pages[:, 4 * q + r, c * P:(c + 1) * P], m.ident[:])
                    last.then_inc(s_turned, 1)
            pe.wait_ge(s_act, 4)
            outputs(0)
            pe.wait_ge(s_kept, NPG // 2)
            for u in range(4, 8):
                pe.wait_ge(s_act, u - 1)
                hidden(u)
            pe.wait_ge(s_act, 8)
            pe.wait_ge(s_end, 1)
            outputs(1)

        @block.scalar
        def _(act):
            act.wait_ge(s_biask, 1)
            for u, (src, c, g) in enumerate(units):
                n = nkeys[src]
                act.wait_ge(s_hid, u + 1)
                nc.scalar.activation(hid[:, u, 0:n], m.ps[:, 2 + u % 2, 0:n], ACT.Gelu_apprx_tanh,
                                     bias=bias[:, c:c + 1]).then_inc(s_act, 1)

        @block.vector
        def _(dve):
            dve.wait_ge(s_posT, 1)
            nc.vector.tensor_copy(small[0:HD, 256:320], m.ps[0:HD, 0, 0:64]).then_inc(s_posk, 1)
            dve.wait_ge(s_bias, 1)
            nc.vector.tensor_copy(bias, m.ps[:, 1, 0:2]).then_inc(s_biask, 1)
            for i in range(NPG // 2):
                q, c = i // 2, i % 2
                dve.wait_ge(s_turned, i + 1)
                nc.vector.tensor_copy(cT[:, c, q * 512:(q + 1) * 512], m.ps[:, 4 + i % 2, :]).then_inc(s_kept, 1)
            for src in range(2):
                n = nkeys[src]
                dve.wait_ge(s_out, src + 1)
                nc.vector.tensor_copy(m.kcT[:, src * P:src * P + n], m.ps[:, 6, 0:n])
                nc.vector.tensor_copy(m.vc[0:n, src, :], m.ps[0:n, 7, 0:P]).then_inc(s_end, 1)


def attend_samples(nc, m, io):
    pages = [view(m.RW, 4096, NPG, 256), view(m.RW, 8192, NPG, 256)]
    cT = view(m.RW, 0, 2, CKEYS)
    NS = CKEYS + NB
    S = m.RA[:, 0:NS]
    PT = view(m.RA, 2176, NPG + 1, P)
    sm = m.small
    qs = sm[:, 0:64]
    onehot, mask = sm[:, 64:72], sm[:, 72:80]
    stat = sm[:, 80:92]
    O = view(sm, 128, 3, P)
    s_page, s_c0, s_c1, s_q = m.sem("att_pages"), m.sem("onehot"), m.sem("sample_mask"), m.sem("sample_q")
    s_turned, s_kept = m.sem("page_turned"), m.sem("page_kept")
    s_score, s_masked, s_max = m.sem("s_scores"), m.sem("s_masked"), m.sem("s_max")
    s_exp, s_pt, s_ptk = m.sem("s_probs"), m.sem("s_probs_turned"), m.sem("s_probs_kept")
    s_pv, s_sc, s_o, s_oT, s_sum = m.sem("s_values"), m.sem("s_scaled"), m.sem("s_branch"), m.sem("s_oT"), m.sem("s_rowsum")
    s_oTk = m.sem("s_oT_kept")
    cache = io["cache_kv"].rearrange("n l p s h d -> (n l) p (s h d)")
    win = io["cache_win"].rearrange("b l (n p) s h d -> (b l n) p (s h d)", p=P)
    ngroup = (1, 5, 5)
    with nc.Block() as block:

        @block.sync
        def _(sp):
            with sp.Fori(0, NPG) as i:
                page = sp.value_load(m.page_ids[0:1, bass.ds(i, 1)], min_val=0, max_val=cache.shape[0] - 1)
                sp.dma_start(m.RW[:, bass.ds(4096 + i * 256, 256)],
                             cache[bass.ds(page, 1), :, 256:512].rearrange("n p c -> p (n c)")).then_inc(s_page, 16)
            sp.dma_start(pages[1], win.rearrange("n p c -> p n c")).then_inc(s_page, 16)

        @block.tensor
        def _(pe):
            g_t = 0
            n_pt = 0
            for br in range(3):
                if br == 0:
                    pe.wait_ge(s_q, 1)
                else:
                    pe.wait_ge(s_page, 16 * (NPG + 1))
                    for q in range(NPG // 4):
                        if g_t >= 2:
                            pe.wait_ge(s_kept, g_t - 1)
                        for r in range(4):
                            last = nc.tensor.transpose(m.ps[:, 6 + g_t % 2, r * P:(r + 1) * P],
                                                       pages[br - 1][:, 4 * q + r, 0:P], m.ident[:])
                        last.then_inc(s_turned, 1)
                        g_t += 1
                    pe.wait_ge(s_kept, g_t)
                    pe.wait_ge(s_masked, br)
                for g in range(NKV):
                    rows = slice(g * HD, (g + 1) * HD)
                    if br == 0:
                        last = nc.tensor.matmul(m.ps[rows, 4, 0:NB * SCMP], qs[rows, :], m.kcT[rows, P:P + NB * SCMP],
                                                start=True, stop=True)
                    else:
                        for c in range(4):
                            nc.tensor.matmul(m.ps[rows, c, :], qs[rows, :], cT[rows, br - 1, c * 512:(c + 1) * 512],
                                             start=True, stop=True)
                        last = nc.tensor.matmul(m.ps[rows, 4, 0:NB], qs[rows, :], m.kT[rows, 1 + br, SEQ:NTOK],
                                                start=True, stop=True)
                last.then_inc(s_score, 1)
                pe.wait_ge(s_exp, br + 1)
                pe.wait_ge(s_kept, g_t)
                for q in range(ngroup[br]):
                    if n_pt >= 2:
                        pe.wait_ge(s_ptk, n_pt - 1)
                    if br == 0:
                        last = nc.tensor.transpose(m.ps[0:NB * SCMP, 6 + n_pt % 2, 0:P], S[:, 0:NB * SCMP], m.ident[:])
                    elif q < 4:
                        for r in range(4):
                            k = 4 * q + r
                            last = nc.tensor.transpose(m.ps[:, 6 + n_pt % 2, r * P:(r + 1) * P],
                                                       S[:, k * P:(k + 1) * P], m.ident[:])
                    else:
                        last = nc.tensor.transpose(m.ps[0:NB, 6 + n_pt % 2, 0:P], S[:, CKEYS:NS], m.ident[:])
                    last.then_inc(s_pt, 1)
                    n_pt += 1
                pe.wait_ge(s_ptk, n_pt)
                if br >= 1:
                    pe.wait_ge(s_o, br)
                if br == 0:
                    last = nc.tensor.matmul(m.ps[:, 5, 0:P], PT[0:NB * SCMP, 0, :], m.vc[0:NB * SCMP, 1, :],
                                            start=True, stop=True)
                else:
                    for k in range(NPG):
                        nc.tensor.matmul(m.ps[:, 5, 0:P], PT[:, k, :], pages[br - 1][:, k, P:2 * P],
                                         start=(k == 0), stop=False)
                    last = nc.tensor.matmul(m.ps[:, 5, 0:P], PT[0:NB, NPG, :],
                                            m.vv[0:NB, TT, (br - 1) * P:br * P], start=False, stop=True)
                last.then_inc(s_pv, 1)
            pe.wait_ge(s_sum, 1)
            nc.tensor.transpose(m.ps[:, 6, 0:P], O[:, 0, :], m.ident[:]).then_inc(s_oT, 1)

        @block.scalar
        def _(act):
            for br in range(3):
                act.wait_ge(s_max, br + 1)
                n = NB * SCMP if br == 0 else NS
                nc.scalar.activation(S[:, 0:n], S[:, 0:n], ACT.Exp, bias=stat[:, br:br + 1],
                                     accum_out=stat[:, 3 + br:4 + br]).then_inc(s_exp, 1)

        @block.vector
        def _(dve):
            nc.vector.tensor_reduce(onehot, m.ident[:].rearrange("p (a b) -> p b a", b=NB), AX.X, ALU.add).then_inc(s_c0, 1)
            nc.vector.tensor_copy(qs.rearrange("p (h b) -> p h b", b=NB), m.qT[:, :, SEQ:NTOK]).then_inc(s_q, 1)
            dve.wait_ge(s_c0, 1)
            nc.vector.tensor_scalar(mask, onehot, 1.0, -NEG, ALU.subtract, ALU.mult).then_inc(s_c1, 1)
            dve.wait_ge(s_c1, 1)
            g_t = n_pt = 0
            for br in range(3):
                if br >= 1:
                    for q in range(NPG // 4):
                        g_t += 1
                        dve.wait_ge(s_turned, g_t)
                        nc.vector.tensor_copy(cT[:, br - 1, q * 512:(q + 1) * 512],
                                              m.ps[:, 6 + (g_t - 1) % 2, :]).then_inc(s_kept, 1)
                dve.wait_ge(s_score, br + 1)
                if br >= 1:
                    dve.wait_ge(s_pt, n_pt)
                if br == 0:
                    nc.vector.tensor_tensor(S[:, 0:NB * SCMP].rearrange("p (b n) -> p b n", b=NB),
                                            m.ps[:, 4, 0:NB * SCMP].rearrange("p (b n) -> p b n", b=NB),
                                            mask.unsqueeze(2).to_broadcast([P, NB, SCMP]), ALU.add).then_inc(s_masked, 1)
                    n = NB * SCMP
                else:
                    nc.vector.tensor_tensor(S[:, 0:CKEYS].rearrange("p (b n) -> p b n", b=NB),
                                            m.ps[:, 0:4, :].rearrange("p a c -> p (a c)").rearrange("p (b n) -> p b n", b=NB),
                                            mask.unsqueeze(2).to_broadcast([P, NB, PAST]), ALU.add)
                    nc.vector.tensor_tensor(S[:, CKEYS:NS], m.ps[:, 4, 0:NB], mask, ALU.add).then_inc(s_masked, 1)
                    n = NS
                dve.wait_ge(s_masked, br + 1)
                nc.vector.tensor_reduce(stat[:, br:br + 1], S[:, 0:n], AX.X, ALU.max, negate=True).then_inc(s_max, 1)
                for q in range(ngroup[br]):
                    n_pt += 1
                    dve.wait_ge(s_pt, n_pt)
                    bank = 6 + (n_pt - 1) % 2
                    if br >= 1 and q == 0:
                        dve.wait_ge(s_pv, br)
                    if br == 0:
                        last = nc.vector.tensor_copy(PT[0:NB * SCMP, 0, :], m.ps[0:NB * SCMP, bank, 0:P])
                    elif q < 4:
                        last = nc.vector.tensor_copy(PT[:, 4 * q:4 * q + 4, :],
                                                     m.ps[:, bank, :].rearrange("p (a c) -> p a c", a=4))
                    else:
                        last = nc.vector.tensor_copy(PT[0:NB, NPG, :], m.ps[0:NB, bank, 0:P])
                    last.then_inc(s_ptk, 1)
                dve.wait_ge(s_exp, br + 1)
                nc.vector.reciprocal(stat[:, 6 + br:7 + br], stat[:, 3 + br:4 + br]).then_inc(s_sc, 1)
                dve.wait_ge(s_sc, 2 * br + 1)
                nc.vector.tensor_tensor(stat[:, 9 + br:10 + br], stat[:, 6 + br:7 + br], m.gs[:, br:br + 1],
                                        ALU.mult).then_inc(s_sc, 1)
                dve.wait_ge(s_sc, 2 * br + 2)
                dve.wait_ge(s_pv, br + 1)
                nc.vector.tensor_scalar(O[:, br, :], m.ps[:, 5, 0:P], stat[:, 9 + br:10 + br], None,
                                        ALU.mult).then_inc(s_o, 1)
            dve.wait_ge(s_o, 3)
            nc.vector.tensor_tensor(O[:, 1, :], O[:, 1, :], O[:, 2, :], ALU.add).then_inc(s_o, 1)
            dve.wait_ge(s_o, 4)
            nc.vector.tensor_tensor(O[:, 0, :], O[:, 0, :], O[:, 1, :], ALU.add).then_inc(s_sum, 1)
            dve.wait_ge(s_oT, 1)
            for g in range(NKV):
                rows = slice(g * HD, (g + 1) * HD)
                nc.vector.tensor_copy(m.qT[rows, :, SEQ:NTOK],
                                      m.ps[rows, 6, g * HD:(g + 1) * HD].rearrange("p (h b) -> p h b", b=NB)).then_inc(s_oTk, 1)


def attend_prompt(nc, m):
    probs = [m.RW[:, 1024 + b * 1024:2048 + b * 1024] for b in range(2)]
    probsT = [view(m.RW, 3072 + b * 1024, 8, P) for b in range(2)]
    onat = [m.RW[:, 5120 + b * P:5248 + b * P] for b in range(2)]
    otmp = [m.RW[:, 5376 + b * 384:5760 + b * 384] for b in range(2)]
    identb, diag, edge = m.identb, m.mask_diag, m.mask_edge
    stat = m.small[:, 0:64].rearrange("p (b w) -> p b w", b=2)
    nmax = m.small[:, 64:76]

    s_q, s_qk, s_max, s_exp = m.sem("a_queries"), m.sem("a_scores"), m.sem("a_max"), m.sem("a_probs")
    s_t, s_tkv, s_tka, s_pv = m.sem("a_turned"), m.sem("a_kept_by_dve"), m.sem("a_kept_by_act"), m.sem("a_values")
    s_sc, s_tmp, s_o, s_oT, s_oTk = (m.sem(n) for n in ("a_scale", "a_scaled", "a_output", "a_oT", "a_oT_kept"))
    s_clamp, s_qh, s_kh, s_kl = (m.sem("a_" + n) for n in ("clamp_input", "q_high", "k_high", "k_low"))

    LO, HI = slice(0, HD), slice(HD, P)
    qs, ks, kcs = m.q_stacks, m.k_stacks, m.kc_stacks
    pieces = [[(m.kT[g * HD:(g + 1) * HD, 2 + a, 0:SEQ], ks[:, a, g])] for g in range(NKV) for a in range(2)]
    for g in range(NKV):
        pieces[2 * g + 1].append((m.kcT[g * HD:(g + 1) * HD, 0:NCMP], kcs[:, g, :, 0:NCMP]))

    jobs = [(i, g, kind) for i in range(TT) for g in range(NKV) for kind in "AB"]
    NJ = len(jobs)
    NMAX = sum(1 if kind == "A" else 2 for _, _, kind in jobs)

    def wblocks(i):
        return list(range(max(0, i - WBLK), i + 1))

    def blocks(job):
        i, g, kind = job
        if kind == "A":
            return [(b * P, P) for b in range(i + 1)]
        win = [(b * P, P) for b in range(len(wblocks(i)))]
        at = cmp_at(i)
        return win[:at] + [(cmp_col(i), NCMP)] + win[at:]

    def cmp_at(i):
        return min(len(wblocks(i)), 3)

    def cmp_col(i):
        return len(wblocks(i)) * P

    def groups(job):
        bl = blocks(job)
        return [bl[a:a + 4] for a in range(0, len(bl), 4)]

    def nmaxes(job):
        return 1 if job[2] == "A" else 2

    NGRP = sum(len(groups(j)) for j in jobs)
    NGV = sum((len(groups(j)) + 1) // 2 for j in jobs)
    NGA = NGRP - NGV
    g_before = [sum(len(groups(j)) for j in jobs[:n]) for n in range(NJ + 1)]
    v_before = [sum((len(groups(j)) + 1) // 2 for j in jobs[:n]) for n in range(NJ + 1)]
    a_before = [g_before[n] - v_before[n] for n in range(NJ + 1)]
    m_before = [sum(nmaxes(j) for j in jobs[:n]) for n in range(NJ + 1)]
    kept_by = [("v" if q % 2 == 0 else "a") for j in jobs for q in range(len(groups(j)))]

    def keep_group(copy, n, q, grp, G):
        full = sum(1 for _, w in grp if w == P)
        last = None
        if full:
            last = copy(probsT[n % 2][:, 4 * q:4 * q + full, :],
                        m.ps[:, 4 + G % 2, 0:full * P].rearrange("p (a c) -> p a c", a=full))
        if full < len(grp):
            last = copy(probsT[n % 2][0:NCMP, 4 * q + full, :], m.ps[0:NCMP, 4 + G % 2, full * P:(full + 1) * P])
        return last

    def wait_from(eng, sem, base, value, first):
        if not (first and value <= 0):
            eng.wait_ge(sem, base + value)

    with nc.Block() as block:

        @block.gpsimd
        def _(pool):
            def high_queries(j, first):
                for i in range(TT):
                    if not first:
                        pool.wait_ge(s_qk, NJ * j + (4 * (i + 1) - NJ))
                    at, cols = bass.ds(j * NTOK + i * P, P), slice(i * P, (i + 1) * P)
                    nc.gpsimd.tensor_copy(qs[LO, 0, cols], m.RO[LO, at])
                    nc.gpsimd.tensor_copy(qs[HI, 1, cols], m.RO[HI, at]).then_inc(s_qh, 1)

            high_queries(0, True)
            with pool.Fori(1, QPK) as j:
                high_queries(j, False)

        @block.tensor
        def _(pe):
            def scores(n, j, first):
                i, g, kind = jobs[n]
                bank = 2 * (n % 2)

                def product(out, k, start=True):
                    for h in range(2):
                        nc.tensor.matmul(out, qs[:, g, i * P:(i + 1) * P], k[:, h], start=start and h == 0,
                                         stop=(h == 1), skip_group_check=True)

                if kind == "A" and g == 0:
                    pe.wait_ge(s_q, TT * j + (i + 1))
                if first and n < len(pieces):
                    pe.wait_ge(s_kh, n + 1)
                    pe.wait_ge(s_kl, n + 1)
                wait_from(pe, s_exp, NMAX * j, m_before[n - 1] if n >= 2 else m_before[NJ + n - 1] - NMAX, first)
                if kind == "A":
                    nk = (i + 1) * P
                    for c in range(0, nk, 512):
                        w = min(512, nk - c)
                        product(m.ps[:, bank + c // 512, 0:w], ks[:, 0, g, :, c:c + w])
                    mm = nc.tensor.matmul(m.ps[:, bank + i // 4, (i % 4) * P:(i % 4 + 1) * P], identb[:], diag[:],
                                          start=False, stop=True, skip_group_check=True)
                    mm.then_inc(s_qk, 1)
                else:
                    bl = wblocks(i)
                    k0, nk, cc = bl[0] * P, len(bl) * P, cmp_col(i)
                    if len(bl) > WBLK:
                        product(m.ps[:, bank, 0:512], ks[:, 1, g, :, k0:k0 + 512])
                        nc.tensor.matmul(m.ps[:, bank, 0:P], identb[:], edge[:], start=False, stop=True, skip_group_check=True)
                        product(m.ps[:, bank + 1, 0:P], ks[:, 1, g, :, k0 + 512:k0 + 640])
                    else:
                        product(m.ps[:, bank, 0:nk], ks[:, 1, g, :, k0:k0 + nk])
                    at = nk - P
                    nc.tensor.matmul(m.ps[:, bank + at // 512, at % 512:at % 512 + P], identb[:], diag[:], start=False,
                                     stop=True, skip_group_check=True)
                    out = m.ps[:, bank + cc // 512, cc % 512:cc % 512 + NCMP + 1]
                    product(out, kcs[:, g], start=(cc % 512 == 0))
                    out = out[:, 0:NCMP]
                    at = 56 - 8 * i
                    nc.tensor.matmul(out, identb[:], m.mask_cmp[:, at:at + NCMP], start=False, stop=True,
                                     skip_group_check=True).then_inc(s_qk, 1)

            def turn(n, j, first):
                pe.wait_ge(s_exp, NMAX * j + m_before[n + 1])
                for q, grp in enumerate(groups(jobs[n])):
                    G = g_before[n] + q
                    H = G - 2
                    if H >= 0:
                        by, cnt = kept_by[H], sum(1 for x in kept_by[:H + 1] if x == kept_by[H])
                    else:
                        by = kept_by[H + NGRP]
                        cnt = sum(1 for x in kept_by[:H + NGRP + 1] if x == by) - (NGV if by == "v" else NGA)
                    wait_from(pe, s_tkv if by == "v" else s_tka, (NGV if by == "v" else NGA) * j, cnt, first)
                    for r, (col, w) in enumerate(grp):
                        last = nc.tensor.transpose(m.ps[0:w, 4 + G % 2, r * P:(r + 1) * P],
                                                   probs[n % 2][:, col:col + w], m.ident[:])
                    last.then_inc(s_t, 1)

            def values(n, j, first):
                i, g, kind = jobs[n]
                pe.wait_ge(s_tkv, NGV * j + v_before[n + 1])
                wait_from(pe, s_tka, NGA * j, a_before[n + 1], first)
                if g == 0 and kind == "A":
                    wait_from(pe, s_oTk, TT * j, i - 1, first)
                bank = 6 + i % 2
                gc = slice(g * HD, (g + 1) * HD)
                pT = probsT[n % 2]
                if kind == "A":
                    out = m.ps[:, bank, g * 192 + 64:g * 192 + 128]
                    for b in range(i + 1):
                        last = nc.tensor.matmul(out, pT[:, b, :], m.vv[:, b, g * HD:(g + 1) * HD],
                                                start=(b == 0), stop=(b == i), skip_group_check=True)
                else:
                    bl = wblocks(i)
                    out = m.ps[:, bank, g * 192 + 128:g * 192 + 192]
                    for r, b in enumerate(bl):
                        nc.tensor.matmul(out, pT[:, r + (r >= cmp_at(i)), :], m.vv[:, b, P + g * HD:P + (g + 1) * HD],
                                         start=(r == 0), stop=(r == len(bl) - 1), skip_group_check=True)
                    last = nc.tensor.matmul(m.ps[:, bank, g * 192:g * 192 + 64], pT[0:NCMP, cmp_at(i), :],
                                            m.vc[0:NCMP, 0, gc], start=True, stop=True, skip_group_check=True)
                last.then_inc(s_pv, 1)

            def turn_output(i, j, first):
                pe.wait_ge(s_o, TT * j + (i + 1))
                nc.tensor.transpose(m.ps[:, 6 + i % 2, 384:512], onat[i % 2], m.ident[:]).then_inc(s_oT, 1)

            def one_pass(j, first):
                scores(0, j, first)
                for n in range(NJ + 2):
                    if n + 1 < NJ:
                        scores(n + 1, j, first)
                    if n < NJ:
                        turn(n, j, first)
                    if 1 <= n <= NJ:
                        values(n - 1, j, first)
                    if n >= 2 and jobs[n - 2][1:] == (1, "B"):
                        turn_output(jobs[n - 2][0], j, first)

            one_pass(0, True)
            with pe.Fori(1, QPK) as j:
                one_pass(j, False)

        @block.vector
        def _(dve):
            def job_max(n, j, first):
                i, g, kind = jobs[n]
                bank = 2 * (n % 2)
                dve.wait_ge(s_qk, NJ * j + (n + 1))
                sc = m.ps[:, bank:bank + 2, :].rearrange("p a c -> p (a c)")
                col = 2 * (n % 2)
                nk = (i + 1) * P if kind == "A" else cmp_col(i)
                nc.vector.tensor_reduce(nmax[:, col:col + 1], sc[:, 0:nk], AX.X, ALU.max, negate=True).then_inc(s_max, 1)
                if kind == "B":
                    dst = nmax[:, 4:5] if i == 0 else nmax[:, col + 1:col + 2]
                    red = nc.vector.tensor_reduce(dst, sc[:, nk:nk + NCMP], AX.X, ALU.max, negate=True)
                    if i > 0:
                        red.then_inc(s_max, 1)
                    else:
                        red.then_inc(s_clamp, 1)
                        dve.wait_ge(s_clamp, NKV * j + (g + 1))
                        nc.vector.tensor_scalar(nmax[:, col + 1:col + 2], nmax[:, 4:5], 1e29, None,
                                                ALU.min).then_inc(s_max, 1)

            def keep(n, j, first):
                for q, grp in enumerate(groups(jobs[n])):
                    if q % 2 == 0:
                        G = g_before[n] + q
                        dve.wait_ge(s_t, NGRP * j + (G + 1))
                        if n >= 2 or not first:
                            dve.wait_ge(s_pv, NJ * j + (n - 1))
                        keep_group(nc.vector.tensor_copy, n, q, grp, G).then_inc(s_tkv, 1)

            def finish(i, j, first):
                b = i % 2
                sums, rec, scl = stat[:, b, 0:6], stat[:, b, 8:14], stat[:, b, 16:22]
                dve.wait_ge(s_exp, NMAX * j + m_before[4 * i + 4])
                if i == 0:
                    nc.vector.tensor_scalar(sums, sums, 1e-30, None, ALU.max).then_inc(s_sc, 1)
                    dve.wait_ge(s_sc, 17 * j + 1)
                nc.vector.reciprocal(rec, sums).then_inc(s_sc, 1)
                dve.wait_ge(s_sc, 17 * j + (2 * i + 2))
                gate = m.gates[:, i, :].rearrange("p (g x) -> p g x", g=NKV)[:, :, bass.ds(3 * j, 3)]
                nc.vector.tensor_tensor(scl.rearrange("p (g x) -> p g x", g=NKV), rec.rearrange("p (g x) -> p g x", g=NKV),
                                        gate, ALU.mult).then_inc(s_sc, 1)
                dve.wait_ge(s_sc, 17 * j + (2 * i + 3))
                dve.wait_ge(s_pv, NJ * j + (4 * i + 4))
                nc.vector.tensor_tensor(otmp[b].rearrange("p (x d) -> p x d", d=HD),
                                        m.ps[:, 6 + b, 0:384].rearrange("p (x d) -> p x d", d=HD),
                                        scl.unsqueeze(2).to_broadcast([P, 6, HD]), ALU.mult).then_inc(s_tmp, 1)
                dve.wait_ge(s_tmp, TT * j + (i + 1))
                nc.vector.tensor_reduce(onat[b].rearrange("p (g d) -> p g d", g=NKV),
                                        otmp[b].rearrange("p (g x d) -> p g d x", g=NKV, x=3), AX.X, ALU.add).then_inc(s_o, 1)

            def low_queries(i, j):
                at, cols = bass.ds(j * NTOK + i * P, P), slice(i * P, (i + 1) * P)
                dve.wait_ge(s_qh, TT * j + (i + 1))
                nc.vector.tensor_tensor(qs[HI, 0, cols], m.RO[LO, at], qs[LO, 0, cols], ALU.subtract)
                nc.vector.tensor_tensor(qs[LO, 1, cols], m.RO[HI, at], qs[HI, 1, cols], ALU.subtract).then_inc(s_q, 1)

            def keep_output(i, j, first):
                dve.wait_ge(s_oT, TT * j + (i + 1))
                nc.vector.tensor_scalar(m.RO[:, bass.ds(j * NTOK + i * P, P)], m.ps[:, 6 + i % 2, 384:512],
                                        1.0, None, ALU.mult).then_inc(s_oTk, 1)

            def one_pass(j, first):
                low_queries(0, j)
                job_max(0, j, first)
                for n in range(NJ + 2):
                    if n % 4 == 0 and n // 4 + 1 < TT:
                        low_queries(n // 4 + 1, j)
                    if n + 1 < NJ:
                        job_max(n + 1, j, first)
                    if n < NJ:
                        keep(n, j, first)
                    if 1 <= n <= NJ and jobs[n - 1][1:] == (1, "B"):
                        finish(jobs[n - 1][0], j, first)
                    if n >= 2 and jobs[n - 2][1:] == (1, "B"):
                        keep_output(jobs[n - 2][0], j, first)

            nc.vector.memset(kcs[:, :, :, NCMP:NCMP + 1].bitcast(F32), 0.0)
            for n, piece in enumerate(pieces):
                dve.wait_ge(s_kh, n + 1)
                rows = slice(n // 2 * HD, (n // 2 + 1) * HD)
                for src, dst in piece:
                    for half in (LO, HI):
                        last = nc.vector.tensor_tensor(dst[half, 1], src, dst[rows, 0], ALU.subtract)
                last.then_inc(s_kl, 1)
            one_pass(0, True)
            with dve.Fori(1, QPK) as j:
                one_pass(j, False)

        @block.scalar
        def _(act):
            def exps(n, j, first):
                i, g, kind = jobs[n]
                bank, col = 2 * (n % 2), 2 * (n % 2)
                sc = m.ps[:, bank:bank + 2, :].rearrange("p a c -> p (a c)")
                if n >= 2 or not first:
                    act.wait_ge(s_t, NGRP * j + (g_before[n - 1] if n >= 2 else g_before[NJ + n - 1] - NGRP))
                if kind == "A" and g == 0 and (i >= 2 or not first):
                    act.wait_ge(s_sc, 17 * j + (2 * (i - 2) + 2 if i >= 2 else 2 * (i + 6) + 2 - 17))
                nk = (i + 1) * P if kind == "A" else cmp_col(i)
                branch = 1 if kind == "A" else 2
                act.wait_ge(s_max, NMAX * j + m_before[n + 1])
                nc.scalar.activation(probs[n % 2][:, 0:nk], sc[:, 0:nk], ACT.Exp, bias=nmax[:, col:col + 1],
                                     accum_out=stat[:, i % 2, 3 * g + branch:3 * g + branch + 1]).then_inc(s_exp, 1)
                if kind == "B":
                    nc.scalar.activation(probs[n % 2][:, nk:nk + NCMP], sc[:, nk:nk + NCMP], ACT.Exp,
                                         bias=nmax[:, col + 1:col + 2],
                                         accum_out=stat[:, i % 2, 3 * g:3 * g + 1]).then_inc(s_exp, 1)

            def keep(n, j, first):
                for q, grp in enumerate(groups(jobs[n])):
                    if q % 2 == 1:
                        G = g_before[n] + q
                        act.wait_ge(s_t, NGRP * j + (G + 1))
                        if n >= 2 or not first:
                            act.wait_ge(s_pv, NJ * j + (n - 1))
                        keep_group(nc.scalar.copy, n, q, grp, G).then_inc(s_tka, 1)

            def one_pass(j, first):
                exps(0, j, first)
                for n in range(NJ):
                    if n + 1 < NJ:
                        exps(n + 1, j, first)
                    keep(n, j, first)

            for piece in pieces:
                for src, dst in piece:
                    for half in (LO, HI):
                        last = nc.scalar.copy(dst[half, 0], src)
                last.then_inc(s_kh, 1)
            one_pass(0, True)
            with act.Fori(1, QPK) as j:
                one_pass(j, False)


def normalise(nc, dve, x, n, stats, mv, rstd, gain, bias, s_stat, s_mv, s_rstd, s_norm, t, done):
    nc.vector.bn_stats(stats[0:n, 0:6], x[:, 0:512])
    nc.vector.bn_stats(stats[0:n, 6:12], x[:, 512:1024]).then_inc(s_stat, 1)
    dve.wait_ge(s_stat, t + 1)
    nc.vector.bn_aggr(mv[0:n], stats[0:n, 0:12]).then_inc(s_mv, 1)
    dve.wait_ge(s_rstd, t + 1)
    nc.vector.tensor_scalar(x, x, mv[0:n, 0:1], rstd[0:n], ALU.subtract, ALU.mult).then_inc(s_norm, 1)
    dve.wait_ge(s_norm, 2 * t + 1)
    nc.vector.tensor_tensor(x, x, gain[0:n], ALU.mult).then_inc(s_norm, 1)
    dve.wait_ge(s_norm, 2 * t + 2)
    nc.vector.tensor_tensor(x, x, bias[0:n], ALU.add).then_inc(done, 1)


def inverse_deviation(nc, m, pool, n, mv, rstd, s_mv, s_eps, s_rstd, t):
    pool.wait_ge(s_mv, t + 1)
    nc.gpsimd.tensor_scalar(rstd[0:n], mv[0:n, 1:2], EPS, None, ALU.add).then_inc(s_eps, 1)
    pool.wait_ge(s_eps, t + 1)
    nc.gpsimd.tensor_tensor(rstd[0:n], rstd[0:n], m.mhalf[0:n], ALU.pow).then_inc(s_rstd, 1)


def gmlp_values(nc, m, io):
    wv = view(m.RW, 0, 2 * KT, 512)
    vn = [m.RK[:, t * DM:(t + 1) * DM] for t in range(TT)] + [m.RW[0:NB, 8192:9216]]
    gain, bias = m.RW[:, 9216:10240], m.RW[:, 10240:11264]
    wsT = view(m.RW, 11264, 8, P)
    bs = view(m.RW, 12288, 8, P)
    ws = view(m.RW, 13312, 8, P)
    stats, mv, rstd = m.small[:, 0:12], m.small[:, 12:14], m.small[:, 14:15]
    w00 = m.small[0:NB, 16:24]
    first = m.small[0:NB, 24:88].rearrange("p (g b) -> p g b", g=8)
    s_w, s_c, s_wsT, s_wsk, s_ws = (m.sem(n) for n in ("v_w", "v_consts", "ws_turned", "ws_kept", "ws_masked"))
    s_proj, s_gelu, s_stat, s_mv, s_eps = (m.sem(n) for n in ("v_projected", "v_gelu", "v_stats", "v_moments", "v_eps"))
    s_rstd, s_norm, s_v, s_mix, s_kept = (m.sem(n) for n in ("v_rstd", "v_scaling", "v_normal", "v_mixed", "v_mixed_kept"))
    s_first, s_out = m.sem("ws_first"), m.sem("v_sample_out")
    w_in = io["w_in"].rearrange("l (k p) n -> p (l k) n", p=P)
    with nc.Block() as block:

        @block.sync
        def _(sp):
            for c in range(2):
                sp.dma_start(wv[:, c * KT:(c + 1) * KT, :], w_in[:, :, COL_V + c * 512:COL_V + (c + 1) * 512]).then_inc(s_w, 16)
            sp.dma_start(ws, io["gmlp_ws"].rearrange("l g t s -> t (l g) s")).then_inc(s_c, 16)
            sp.dma_start(gain, io["gmlp_ln_g"].rearrange("l d -> (l d)").partition_broadcast(P)).then_inc(s_c, 16)
            sp.dma_start(bias, io["gmlp_ln_b"].rearrange("l d -> (l d)").partition_broadcast(P)).then_inc(s_c, 16)
            sp.dma_start(bs.rearrange("p g t -> p (g t)"),
                         io["gmlp_bs"].rearrange("l g t -> (l g t)").partition_broadcast(P)).then_inc(s_c, 16)
            with nc.allow_non_contiguous_dma(reason="one weight per group"):
                sp.dma_start(w00.unsqueeze(2), io["gmlp_ws"][0, :, 0, 0:1].partition_broadcast(NB)).then_inc(s_c, 16)
            sp.wait_ge(s_v, NT9)
            sp.dma_start(io["gmlp_v_sample"].rearrange("b l t d -> (b l t) d"), vn[TT]).then_inc(s_out, 16)
            sp.wait_ge(s_out, 16)

        @block.gpsimd
        def _(pool):
            pool.wait_ge(s_wsk, 1)
            nc.gpsimd.affine_select(out=wsT, in_=wsT, compare_op=ALU.is_ge, fill=0.0, base=0,
                                    pattern=[[0, 8], [1, P]], channel_multiplier=-1).then_inc(s_ws, 1)
            for t in range(NT9):
                inverse_deviation(nc, m, pool, rows_of(t), mv, rstd, s_mv, s_eps, s_rstd, t)

        @block.tensor
        def _(pe):
            pe.wait_ge(s_c, 80)
            for g in range(8):
                last = nc.tensor.transpose(m.ps[:, 4 + g // 4, (g % 4) * P:(g % 4 + 1) * P], ws[:, g, :], m.ident[:])
            last.then_inc(s_wsT, 1)

            def mix(t):
                n, bank = rows_of(t), 4 + 2 * (t % 2)
                pe.wait_ge(s_v, t + 1)
                if t == 0:
                    pe.wait_ge(s_ws, 1)
                if t == TT:
                    pe.wait_ge(s_first, 1)
                if t >= 2:
                    pe.wait_ge(s_kept, t - 1)
                for g in range(8):
                    out = m.ps[:, bank + g // 4, (g % 4) * P:(g % 4) * P + n]
                    rhs = wsT[:, g, :] if t < TT else first[:, g, :]
                    last = nc.tensor.matmul(out, vn[t][:, g * P:(g + 1) * P], rhs, start=True, stop=True)
                last.then_inc(s_mix, 1)

            pe.wait_ge(s_w, 32)
            for t in range(NT9):
                n = rows_of(t)
                if t >= 2:
                    pe.wait_ge(s_gelu, t - 1)
                for c in range(2):
                    for k in range(KT):
                        last = nc.tensor.matmul(m.ps[0:n, 2 * (t % 2) + c, :], m.xT[:, k, span(t)],
                                                wv[:, c * KT + k, :], start=(k == 0), stop=(k == KT - 1))
                last.then_inc(s_proj, 1)
                if t >= 1:
                    mix(t - 1)
            mix(TT)

        @block.scalar
        def _(act):
            for t in range(NT9):
                n, b = rows_of(t), t % 2
                act.wait_ge(s_proj, t + 1)
                nc.scalar.activation(vn[t].rearrange("p (a c) -> p a c", a=2), m.ps[0:n, 2 * b:2 * b + 2, :],
                                     ACT.Gelu_apprx_tanh).then_inc(s_gelu, 1)

        @block.vector
        def _(dve):
            dve.wait_ge(s_wsT, 1)
            nc.vector.tensor_copy(wsT.rearrange("p (a c) t -> p a (c t)", a=2), m.ps[:, 4:6, :]).then_inc(s_wsk, 1)
            dve.wait_ge(s_c, 80)
            nc.vector.tensor_tensor(first, m.ident[0:NB, 0:NB].unsqueeze(1).to_broadcast([NB, 8, NB]),
                                    w00.unsqueeze(2).to_broadcast([NB, 8, NB]), ALU.mult).then_inc(s_first, 1)

            def keep(t):
                n, bank = rows_of(t), 4 + 2 * (t % 2)
                dve.wait_ge(s_mix, t + 1)
                src = m.ps[:, bank:bank + 2, :].rearrange("p a (g c) -> p (a g) c", g=4)[:, :, 0:n]
                add = bs if t < TT else bs[:, :, 0:1].to_broadcast([P, 8, NB])
                nc.vector.tensor_tensor(m.aT[:, :, span(t)], src, add, ALU.add).then_inc(s_kept, 1)

            for t in range(NT9):
                dve.wait_ge(s_gelu, t + 1)
                normalise(nc, dve, vn[t], rows_of(t), stats, mv, rstd, gain, bias,
                          s_stat, s_mv, s_rstd, s_norm, t, s_v)
                if t >= 1:
                    keep(t - 1)
            keep(TT)


def gmlp_gate(nc, m, io):
    wu = [view(m.RW, 14336 + b * KT * P, KT, P) for b in range(2)]
    ug = [m.RW[:, b * NTOK:(b + 1) * NTOK] for b in range(2)]
    s_w = [m.sem("u_w0"), m.sem("u_w1")]
    s_proj, s_gelu, s_a = m.sem("u_projected"), m.sem("u_gelu"), m.sem("a_ready")
    w_in = io["w_in"].rearrange("l (k p) n -> p (l k) n", p=P)
    with nc.Block() as block:

        @block.sync
        def _(sp):
            for b in range(2):
                sp.dma_start(wu[b], w_in[:, :, b * P:(b + 1) * P]).then_inc(s_w[b], 16)
            with sp.Fori(1, KT // 2) as jj:
                for b in range(2):
                    sp.wait_ge(s_proj, 2 * jj + (b - 1))
                    sp.dma_start(wu[b], w_in[:, :, bass.ds(2 * P * jj + b * P, P)]).then_inc(s_w[b], 16)

        @block.tensor
        def _(pe):
            def tile(b, jj=None):
                pe.wait_ge(s_w[b], 16 if jj is None else 16 * jj + 16)
                if jj is not None:
                    pe.wait_ge(s_gelu, 2 * jj + (b - 1))
                for c in range(3):
                    cols = slice(c * 512, min((c + 1) * 512, NTOK))
                    for k in range(KT):
                        last = nc.tensor.matmul(m.ps[:, 3 * b + c, 0:cols.stop - cols.start], wu[b][:, k, :],
                                                m.xT[:, k, cols], start=(k == 0), stop=(k == KT - 1))
                last.then_inc(s_proj, 1)

            for b in range(2):
                tile(b)
            with pe.Fori(1, KT // 2) as jj:
                for b in range(2):
                    tile(b, jj)

        @block.scalar
        def _(act):
            def tile(b, jj=None):
                act.wait_ge(s_proj, b + 1 if jj is None else 2 * jj + (b + 1))
                if jj is not None:
                    act.wait_ge(s_a, 2 * jj + (b - 1))
                src = m.ps[:, 3 * b:3 * b + 2, :].rearrange("p a c -> p (a c)")
                nc.scalar.activation(ug[b][:, 0:SEQ], src, ACT.Gelu_apprx_tanh)
                nc.scalar.activation(ug[b][:, SEQ:NTOK], m.ps[:, 3 * b + 2, 0:NB], ACT.Gelu_apprx_tanh).then_inc(s_gelu, 1)

            for b in range(2):
                tile(b)
            with act.Fori(1, KT // 2) as jj:
                for b in range(2):
                    tile(b, jj)

        @block.vector
        def _(dve):
            with dve.Fori(0, KT // 2) as jj:
                for b in range(2):
                    dve.wait_ge(s_gelu, 2 * jj + (b + 1))
                    at = m.RA[:, bass.ds((2 * jj + b) * NTOK, NTOK)]
                    nc.vector.tensor_tensor(at, at, ug[b], ALU.mult).then_inc(s_a, 1)


def merge(nc, m, io):
    w = [m.RW[:, b * 4096:(b + 1) * 4096].rearrange("p (q k c) -> p q k c", q=4, k=KT) for b in range(2)]
    wout = view(m.RW, 8192, KT, DM)
    sa, sb = m.small[:, 0:512], m.small[:, 512:1024]
    s_w = [m.sem("m_w0"), m.sem("m_w1")]
    s_out = m.sem_wout
    s_mm, s_sig, s_mul, s_y = m.sem("m_products"), m.sem("m_sigmoid"), m.sem("m_gated"), m.sem("m_merged")
    w_in = io["w_in"].rearrange("l (k p) n -> p (l k) n", p=P)
    w_a = io["w_branch_a"].rearrange("l (k p) n -> p (l k) n", p=P)
    w_b = io["w_branch_b"].rearrange("l (g k d) n -> g d (l k) n", g=NKV, d=HD)
    NS = 3

    def columns(c):
        return slice(c * 512, min((c + 1) * 512, NTOK))

    with nc.Block() as block:

        @block.sync
        def _(sp):
            def load(col, b):
                sp.dma_start(w[b][:, 0], w_in[:, :, bass.ds(col + COL_GA, P)]).then_inc(s_w[b], 16)
                sp.dma_start(w[b][:, 1], w_in[:, :, bass.ds(col + COL_GB, P)]).then_inc(s_w[b], 16)
                sp.dma_start(w[b][:, 2], w_a[:, :, bass.ds(col, P)]).then_inc(s_w[b], 16)
                for g in range(NKV):
                    sp.dma_start(w[b][g * HD:(g + 1) * HD, 3], w_b[g, :, :, bass.ds(col, P)]).then_inc(s_w[b], 16)

            for b in range(2):
                load(b * P, b)
            sp.dma_start(wout, io["w_out"].rearrange("l (k p) n -> p (l k) n", p=P)).then_inc(s_out, 16)
            with sp.Fori(1, KT // 2) as jj:
                for b in range(2):
                    sp.wait_ge(s_mm, NS * 2 * jj + NS * (b - 1))
                    load(2 * P * jj + b * P, b)

        @block.tensor
        def _(pe):
            def tile(b, jj=None):
                pe.wait_ge(s_w[b], 80 if jj is None else 80 * jj + 80)
                for c in range(NS):
                    step = NS * b + c
                    half = step % 2
                    if jj is not None or step >= 2:
                        pe.wait_ge(s_mul, step - 1 if jj is None else 2 * NS * jj + (step - 1))
                    n = columns(c).stop - columns(c).start
                    for q, src in enumerate((m.xT, m.xT, m.aT, m.qT)):
                        for k in range(KT):
                            last = nc.tensor.matmul(m.ps[:, 4 * half + q, 0:n], w[b][:, q, k, :], src[:, k, columns(c)],
                                                    start=(k == 0), stop=(k == KT - 1))
                    last.then_inc(s_mm, 1)

            for b in range(2):
                tile(b)
            with pe.Fori(1, KT // 2) as jj:
                for b in range(2):
                    tile(b, jj)

        def step_of(jj, b, c):
            return 2 * NS * jj + (NS * b + c)

        @block.scalar
        def _(act):
            def tile(b, jj, first):
                for c in range(NS):
                    half, n = (NS * b + c) % 2, columns(c).stop - columns(c).start
                    act.wait_ge(s_mm, step_of(jj, b, c) + 1)
                    if not (first and b == 0 and c == 0):
                        act.wait_ge(s_y, step_of(jj, b, c))
                    nc.scalar.activation(sa[:, 0:n], m.ps[:, 4 * half, 0:n], ACT.Sigmoid)
                    nc.scalar.activation(sb[:, 0:n], m.ps[:, 4 * half + 1, 0:n], ACT.Sigmoid).then_inc(s_sig, 1)

            for b in range(2):
                tile(b, 0, True)
            with act.Fori(1, KT // 2) as jj:
                for b in range(2):
                    tile(b, jj, False)

        @block.vector
        def _(dve):
            with dve.Fori(0, KT // 2) as jj:
                for b in range(2):
                    for c in range(NS):
                        half, n = (NS * b + c) % 2, columns(c).stop - columns(c).start
                        dve.wait_ge(s_sig, step_of(jj, b, c) + 1)
                        nc.vector.tensor_tensor(sa[:, 0:n], sa[:, 0:n], m.ps[:, 4 * half + 2, 0:n], ALU.mult)
                        nc.vector.tensor_tensor(sb[:, 0:n], sb[:, 0:n], m.ps[:, 4 * half + 3, 0:n], ALU.mult).then_inc(s_mul, 1)
                        dve.wait_ge(s_mul, step_of(jj, b, c) + 1)
                        at = (2 * jj + b) * NTOK + c * 512
                        nc.vector.tensor_tensor(m.RK[:, bass.ds(at, n)], sa[:, 0:n], sb[:, 0:n], ALU.add).then_inc(s_y, 1)


def output_and_router(nc, m, io):
    yT = view(m.RK, 0, KT, NTOK)
    wout = view(m.RW, 8192, KT, DM)
    x1 = m.x1
    base = 0
    gain, bias = m.R3[:, base:base + DM], m.R3[:, base + DM:base + 2 * DM]
    x1T = view(m.R3, base + 2 * DM, KT, P)
    wr = m.R3[:, base + 3 * DM:base + 3 * DM + KT * NE].rearrange("p (k e) -> p k e", k=KT)
    sc = m.R3[:, base + 3 * DM + 128:base + 3 * DM + 160]
    stats, mv, rstd = sc[:, 0:12], sc[:, 12:14], sc[:, 14:15]
    aff = m.aff
    s_spill = m.sem("o_x1_out")
    s_x, s_c, s_mm, s_z = [m.sem(f"o_x{b}") for b in range(3)], m.sem("o_consts"), m.sem("o_products"), m.sem("o_residual")
    s_stat, s_mv, s_eps, s_rstd, s_norm = (m.sem("o_" + n) for n in ("stats", "moments", "eps", "rstd", "scaling"))
    s_x1, s_t, s_tk, s_r, s_aff, s_a0 = (m.sem("o_" + n) for n in ("x1_ready", "turned", "turned_kept", "routed", "affinity", "clear"))
    xp = io["x_prompt"].rearrange("a (t p) d -> p (a t) d", p=P)
    with nc.Block() as block:

        @block.sync
        def _(sp):
            sp.dma_start(gain, io["ln1_g"].rearrange("l d -> (l d)").partition_broadcast(P)).then_inc(s_c, 16)
            sp.dma_start(bias, io["ln1_b"].rearrange("l d -> (l d)").partition_broadcast(P)).then_inc(s_c, 16)
            sp.dma_start(wr, io["w_router"].rearrange("(k p) e -> p k e", p=P)).then_inc(s_c, 16)
            for t in range(NT9):
                if t >= 3:
                    sp.wait_ge(s_x[t % 3], 16 * (t // 3))
                src = xp[:, t, :] if t < TT else io["x_sample"].rearrange("b t d -> (b t) d")
                sp.dma_start(x1[t], src).then_inc(s_x[t % 3], 16)
            for t in range(TT):
                sp.wait_ge(s_x1, t + 1)
                sp.dma_start(m.x1_dram[t * P:(t + 1) * P, :], x1[t]).then_inc(s_spill, 16)
            sp.wait_ge(s_spill, 16 * TT)

        @block.gpsimd
        def _(pool):
            nc.gpsimd.memset(aff[:, TT, :], 0.0).then_inc(s_a0, 1)
            for t in range(NT9):
                inverse_deviation(nc, m, pool, rows_of(t), mv, rstd, s_mv, s_eps, s_rstd, t)

        @block.tensor
        def _(pe):
            def turn(t):
                n = rows_of(t)
                pe.wait_ge(s_x1, t + 1)
                if t >= 1:
                    pe.wait_ge(s_tk, t)
                for k in range(KT):
                    last = nc.tensor.transpose(m.ps[:, 4 + k // 4, (k % 4) * P:(k % 4) * P + n],
                                               x1[t][:, k * P:(k + 1) * P], m.ident[0:n, 0:n])
                last.then_inc(s_t, 1)

            def route(t):
                n = rows_of(t)
                pe.wait_ge(s_tk, t + 1)
                if t >= 2:
                    pe.wait_ge(s_aff, t - 1)
                for k in range(KT):
                    last = nc.tensor.matmul(m.ps[0:n, 6 + t % 2, 0:NE], x1T[:, k, 0:n], wr[:, k, :],
                                            start=(k == 0), stop=(k == KT - 1))
                last.then_inc(s_r, 1)

            pe.wait_ge(m.sem_wout, 16)
            pe.wait_ge(s_c, 48)
            for t in range(NT9):
                n = rows_of(t)
                if t >= 2:
                    pe.wait_ge(s_z, t - 1)
                for c in range(2):
                    for k in range(KT):
                        last = nc.tensor.matmul(m.ps[0:n, 2 * (t % 2) + c, :], yT[:, k, span(t)],
                                                wout[:, k, c * 512:(c + 1) * 512], start=(k == 0), stop=(k == KT - 1))
                last.then_inc(s_mm, 1)
                if t >= 2:
                    route(t - 2)
                if t >= 1:
                    turn(t - 1)
            route(TT - 1)
            turn(TT)
            route(TT)

        @block.scalar
        def _(act):
            for t in range(NT9):
                n = rows_of(t)
                act.wait_ge(s_t, t + 1)
                if t >= 1:
                    act.wait_ge(s_r, t)
                src = m.ps[:, 4:6, :].rearrange("p a (k c) -> p (a k) c", k=4)[:, :, 0:n]
                nc.scalar.copy(x1T[:, :, 0:n], src).then_inc(s_tk, 1)
                act.wait_ge(s_r, t + 1)
                if t == TT:
                    act.wait_ge(s_a0, 1)
                nc.scalar.activation(aff[0:n, t, :], m.ps[0:n, 6 + t % 2, 0:NE], ACT.Sigmoid).then_inc(s_aff, 1)

        @block.vector
        def _(dve):
            dve.wait_ge(s_c, 48)
            for t in range(NT9):
                n, b = rows_of(t), t % 2
                dve.wait_ge(s_mm, t + 1)
                dve.wait_ge(s_x[t % 3], 16 * (t // 3 + 1))
                src = m.ps[0:n, 2 * b:2 * b + 2, :].rearrange("p a c -> p (a c)")
                nc.vector.scalar_tensor_tensor(out=x1[t], in0=x1[t], scalar=ALPHA, in1=src, op0=ALU.mult,
                                               op1=ALU.add).then_inc(s_z, 1)
                dve.wait_ge(s_z, t + 1)
                normalise(nc, dve, x1[t], n, stats, mv, rstd, gain, bias, s_stat, s_mv, s_rstd, s_norm, t, s_x1)


GATE, UP, DOWN = range(3)


def raw_third(m, q):
    return (m.RK[:, 0:4096], m.RK[:, 4096:8192], m.RW[:, 0:4096])[q]


def load_third(m, io, sp, q, e):
    sem = (m.sem_gate, m.sem_up, m.sem_down)[q]
    if q == DOWN:
        src = io["w_down"].rearrange("l e (k p) n -> p (l e) k n", k=FT)[:, bass.ds(e, 1)].rearrange("p o k n -> p (o k) n")
        sp.dma_start(raw_third(m, q).rearrange("p (k n) -> p k n", k=FT), src).then_inc(sem, 16)
    else:
        w = io["w_gate" if q == GATE else "w_up"].rearrange("l e (p k) f -> p (l e) (k f)", k=KT)
        sp.dma_start(raw_third(m, q), w[:, bass.ds(e, 1), :].rearrange("p o c -> p (o c)")).then_inc(sem, 16)


def route_and_dispatch(nc, m, io):
    NQ = NT9 * NE
    cursor = [0]

    def take(n):
        a = m.RW[:, 8192 + cursor[0]:8192 + cursor[0] + n]
        cursor[0] += n
        return a

    def te(x):
        return x.rearrange("p (t e) -> p t e", e=NE)

    aff = m.aff.rearrange("p t e -> p (t e)")
    br, w4, w16, number = take(NE), take(4), take(NE), take(NE)
    kk, tau = take(NKX), take(NEXTRA)
    ones, before = take(P), take(P)
    rowmask = take(1)
    grp, vm, oh1, oh2, tmp, eqw = (take(NQ) for _ in range(6))
    M = take(NQ)
    a_, b_, c_, d_ = (take(NT9 * NG) for _ in range(4))
    gs_, goh = take(NT9 * NG), take(NT9 * NG)
    mx, mm = take(NT9), take(NT9)
    a12 = take(2 * NT9)
    tot, tb, pos = take(NQ), take(NQ), take(NQ)
    cnt, off, nt, T, Tex, tq = (take(NE) for _ in range(6))
    big1, big2 = take(NEXTRA * NE), take(NEXTRA * NE)
    rowv, endv, last = take(NEXTRA), take(NEXTRA), take(NE)
    slotf = take(2 * NT9)
    tabf = take(2 * NSTEP + 2)
    zeros = take(DM)
    assert cursor[0] <= 8192
    s_b, s_c0, s_c, s_v, s_m, s_cnt = (m.sem("r_" + n) for n in ("bias", "clear", "consts", "step", "chosen", "counted"))
    s_slot, s_send = m.sem("r_slots"), m.sem("r_rows_sent")
    with nc.Block() as block:

        @block.sync
        def _(sp):
            sp.dma_start(br, io["b_router"].partition_broadcast(P)).then_inc(s_b, 16)
            load_third(m, io, sp, GATE, 0)
            load_third(m, io, sp, UP, 0)
            sp.wait_ge(m.sem_gate, 16)
            sp.wait_ge(m.sem_up, 16)

        @block.gpsimd
        def _(pool):
            flt = dict(allow_small_or_imprecise_dtypes=True)
            nc.gpsimd.iota(w4, [[-1, 4]], base=4, channel_multiplier=0, **flt)
            nc.gpsimd.iota(w16, [[-1, NE]], base=NE, channel_multiplier=0, **flt)
            nc.gpsimd.iota(number, [[1, NE]], base=0, channel_multiplier=0, **flt)
            nc.gpsimd.iota(kk, [[EROWS, NKX]], base=EROWS, channel_multiplier=0, **flt)
            nc.gpsimd.iota(tau, [[1, NEXTRA]], base=0, channel_multiplier=0, **flt)
            nc.gpsimd.memset(ones, 1.0)
            nc.gpsimd.memset(zeros, 0.0)
            nc.gpsimd.memset(before, 1.0)
            nc.gpsimd.memset(rowmask, 1.0).then_inc(s_c0, 1)
            pool.wait_ge(s_c0, 1)
            nc.gpsimd.affine_select(out=before, in_=before, compare_op=ALU.is_gt, fill=0.0, base=0,
                                    pattern=[[1, P]], channel_multiplier=-1)
            nc.gpsimd.affine_select(out=rowmask, in_=rowmask, compare_op=ALU.is_gt, fill=0.0, base=NB,
                                    pattern=[[0, 1]], channel_multiplier=-1).then_inc(s_c, 1)
            pool.wait_ge(s_c, 1)
            nc.gpsimd.dma_start(m.xs_dram[NPAIR:NPAIR + P, :], zeros).then_inc(m.sem_stored, 16)
            nc.gpsimd.dma_start(m.xs_dram[NPAIR + P:NROWS, :], zeros[0:EREST]).then_inc(m.sem_stored, 16)
            pool.wait_ge(s_slot, 1)
            for t in range(NT9):
                for c in range(2):
                    n = rows_of(t)
                    col = t * 2 + c
                    nc.gpsimd.indirect_dma_start(
                        out=m.xs_dram, out_offset=bass.IndirectOffsetOnAxis(ap=m.slots[0:n, col:col + 1], axis=0),
                        in_=m.x1[t], in_offset=None).then_inc(s_send, 16)
            pool.wait_ge(s_send, 16 * 2 * NT9)
            pool.wait_ge(m.sem_stored, 32)

        @block.tensor
        def _(pe):
            pe.wait_ge(s_m, 1)
            pe.wait_ge(s_c, 1)
            nc.tensor.matmul(m.ps[:, 0, 0:NQ], before, M, start=True, stop=True)
            nc.tensor.matmul(m.ps[:, 1, 0:NQ], ones, M, start=True, stop=True).then_inc(s_cnt, 1)

        @block.vector
        def _(dve):
            steps = [0]

            def step(ins):
                steps[0] += 1
                ins.then_inc(s_v, 1)
                dve.wait_ge(s_v, steps[0])

            tt, ts, red = nc.vector.tensor_tensor, nc.vector.tensor_scalar, nc.vector.tensor_reduce

            def bc(x, shape):
                return x.to_broadcast(shape)

            def first_best(v, n, groups, width, weights, out):
                v3 = v.rearrange("p (a b) -> p a b", b=width)
                o3 = out.rearrange("p (a b) -> p a b", b=width)
                t3 = eqw[:, 0:n].rearrange("p (a b) -> p a b", b=width)
                step(red(mx[:, 0:groups], v3, AX.X, ALU.max))
                step(tt(t3, v3, bc(mx[:, 0:groups].unsqueeze(2), [P, groups, width]), ALU.is_equal))
                step(tt(t3, t3, bc(weights.unsqueeze(1), [P, groups, width]), ALU.mult))
                step(red(mm[:, 0:groups], t3, AX.X, ALU.max))
                step(tt(o3, t3, bc(mm[:, 0:groups].unsqueeze(2), [P, groups, width]), ALU.is_equal))

            dve.wait_ge(s_b, 16)
            dve.wait_ge(s_c, 1)
            step(tt(te(grp), te(aff), bc(br.unsqueeze(1), [P, NT9, NE]), ALU.add))
            v = [grp.rearrange("p (x q) -> p x q", q=EPG)[:, :, q] for q in range(EPG)]
            tt(a_, v[0], v[1], ALU.max)
            tt(b_, v[0], v[1], ALU.min)
            tt(c_, v[2], v[3], ALU.max)
            step(tt(d_, v[2], v[3], ALU.min))
            tt(gs_, a_, c_, ALU.max)
            tt(goh, a_, c_, ALU.min)
            step(tt(b_, b_, d_, ALU.max))
            step(tt(goh, goh, b_, ALU.max))
            step(tt(gs_, gs_, goh, ALU.add))
            first_best(gs_, NT9 * NG, NT9, NG, w4, goh)
            step(ts(goh, goh, 1.0, -NEG, ALU.subtract, ALU.mult))
            step(tt(vm.rearrange("p (x q) -> p x q", q=EPG), grp.rearrange("p (x q) -> p x q", q=EPG),
                    bc(goh.unsqueeze(2), [P, NT9 * NG, EPG]), ALU.add))
            first_best(vm, NQ, NT9, NE, w16, oh1)
            step(nc.vector.scalar_tensor_tensor(out=vm, in0=oh1, scalar=NEG, in1=vm, op0=ALU.mult, op1=ALU.add))
            first_best(vm, NQ, NT9, NE, w16, oh2)
            for oh in (oh1, oh2):
                step(ts(te(oh)[:, TT, :], te(oh)[:, TT, :], rowmask, None, ALU.mult))
            tt(M, oh1, oh2, ALU.add).then_inc(s_m, 1)
            wt = m.pair_w
            for c, oh in enumerate((oh1, oh2)):
                step(tt(tmp, aff, oh, ALU.mult))
                step(red(wt[:, :, c], te(tmp), AX.X, ALU.add))
            step(tt(mx, wt[:, :, 0], wt[:, :, 1], ALU.add))
            step(ts(mx, mx, 1e-38, None, ALU.max))
            step(nc.vector.reciprocal(mm, mx))
            step(tt(wt, wt, bc(mm.unsqueeze(2), [P, NT9, 2]), ALU.mult))
            dve.wait_ge(s_cnt, 1)
            step(nc.vector.tensor_copy(tot, m.ps[:, 1, 0:NQ]))
            step(nc.vector.memset(tb[:, 0:NE], 0.0))
            for t in range(1, NT9):
                step(tt(te(tb)[:, t, :], te(tb)[:, t - 1, :], te(tot)[:, t - 1, :], ALU.add))
            step(tt(cnt, te(tb)[:, TT, :], te(tot)[:, TT, :], ALU.add))
            step(nc.vector.tensor_tensor_scan(off, ones[:, 0:NE], cnt, 0.0, ALU.mult, ALU.add))
            step(tt(off, off, cnt, ALU.subtract))
            step(tt(te(pos), te(tb), bc(off.unsqueeze(1), [P, NT9, NE]), ALU.add))
            step(tt(pos, pos, m.ps[:, 0, 0:NQ], ALU.add))
            for c, oh in enumerate((oh1, oh2)):
                step(tt(tmp, pos, oh, ALU.mult))
                step(red(slotf.rearrange("p (t c) -> p t c", c=2)[:, :, c], te(tmp), AX.X, ALU.add))
            nc.vector.tensor_copy(m.slots[:], slotf).then_inc(s_slot, 1)
            r1 = slice(0, 1)
            more = big1[r1, 0:NE * NKX].rearrange("p (e k) -> p e k", e=NE)
            step(tt(more, bc(cnt[r1].unsqueeze(2), [1, NE, NKX]), bc(kk[r1].unsqueeze(1), [1, NE, NKX]), ALU.is_gt))
            step(red(nt[r1], more, AX.X, ALU.add))
            step(nc.vector.tensor_tensor_scan(T[r1], ones[r1, 0:NE], nt[r1], 0.0, ALU.mult, ALU.add))
            step(tt(Tex[r1], T[r1], nt[r1], ALU.subtract))
            A3 = big1[r1].rearrange("p (x e) -> p x e", e=NE)
            B3 = big2[r1].rearrange("p (x e) -> p x e", e=NE)
            tab = tabf[r1]
            full = [1, NEXTRA, NE]
            tt(A3, bc(tau[r1].unsqueeze(2), full), bc(T[r1].unsqueeze(1), full), ALU.is_ge)
            step(tt(B3, bc(tau[r1].unsqueeze(2), full), bc(Tex[r1].unsqueeze(1), full), ALU.is_ge))
            step(tt(B3, B3, A3, ALU.subtract))
            step(tt(A3, B3, bc(number[r1].unsqueeze(1), full), ALU.mult))
            step(red(tab[:, NSTEP + NE:2 * NSTEP], A3, AX.X, ALU.add))
            step(nc.vector.scalar_tensor_tensor(out=tq[r1], in0=Tex[r1], scalar=-float(EROWS), in1=off[r1], op0=ALU.mult, op1=ALU.add))
            step(tt(A3, B3, bc(tq[r1].unsqueeze(1), full), ALU.mult))
            step(red(rowv[r1], A3, AX.X, ALU.add))
            step(nc.vector.scalar_tensor_tensor(out=rowv[r1], in0=tau[r1], scalar=float(EROWS), in1=rowv[r1], op0=ALU.mult, op1=ALU.add))
            step(ts(rowv[r1], rowv[r1], float(EROWS), None, ALU.add))
            step(tt(last[r1], off[r1], cnt[r1], ALU.add))
            step(ts(last[r1], last[r1], -float(EROWS), None, ALU.add))
            step(tt(A3, B3, bc(last[r1].unsqueeze(1), full), ALU.mult))
            step(red(endv[r1], A3, AX.X, ALU.add))
            step(tt(tab[:, NE:NSTEP], rowv[r1], endv[r1], ALU.min))
            nc.vector.tensor_copy(tab[:, 0:NE], off[r1])
            nc.vector.tensor_copy(tab[:, NSTEP:NSTEP + NE], number[r1])
            for i in range(2):
                step(ts(tab[:, 2 * NSTEP + i:2 * NSTEP + i + 1], T[r1, NE - 1:NE], float(NE - 3 * i), None, ALU.add))
            step(nc.vector.tensor_copy(m.table[:], tab))


def experts(nc, m, io):
    xg = [m.RW[0:n, 4096 + b * DM:4096 + (b + 1) * DM] for b, n in enumerate((P, EREST))]
    y = [m.RW[0:n, 6144 + b * DM:6144 + (b + 1) * DM] for b, n in enumerate((P, EREST))]
    at = 8192 + 2 * (KT + FT) * EROWS
    silu, h = m.RW[:, at:at + FT * EROWS], m.RW[:, at + FT * EROWS:at + 2 * FT * EROWS]
    xT = m.xg_parts.rearrange("p (h k c) -> p h k c", h=2, k=KT)
    hT = m.h_parts.rearrange("p (h k c) -> p h k c", h=2, k=FT)
    wparts = [w.rearrange("p (h c) -> p h c", h=2) for w in (m.wg_parts, m.wu_parts, m.wd_parts)]
    wg, wu = (w.rearrange("p h (k f) -> p h k f", k=KT) for w in wparts[:2])
    wd = wparts[2].rearrange("p h (k n) -> p h k n", k=FT)
    sem_in = (m.sem_gate, m.sem_up, m.sem_down)
    s_hi, s_lo = ([m.sem(f"e_{n}_{w}") for w in ("gate", "up", "down")] for n in ("high", "low"))
    s_x, s_ta, s_tb, s_xh, s_xl = (m.sem("e_rows_" + n) for n in ("in", "turned_a", "turned_b", "high", "low"))
    s_g, s_u, s_silu, s_h, s_hh, s_hl = (m.sem("e_" + n) for n in ("gate", "up", "silu", "hidden", "hidden_high", "hidden_low"))
    s_da, s_db, s_ya, s_yb = m.sem("e_down_a"), m.sem("e_down_b"), m.sem("e_out_a"), m.sem("e_out_b")
    used = (s_g, s_u, s_da)
    PASSES = ((0, 0), (0, 1), (1, 0))
    HALF = 2048

    def after(eng, sem, value):
        if not (isinstance(value, int) and value <= 0):
            eng.wait_ge(sem, value)

    def steps_of(eng):
        return eng.value_load(m.table[0:1, 2 * NSTEP:2 * NSTEP + 1], min_val=NE, max_val=NSTEP)

    def last_three(eng):
        a = eng.value_load(m.table[0:1, 2 * NSTEP + 1:2 * NSTEP + 2], min_val=NE - 3, max_val=NSTEP - 3)
        return a, a + 1, a + 2

    def turned(k):
        bank = 4 + k // 2 if k < 4 else k // 2 - 2
        return m.ps[:, bank, k % 2 * EROWS:(k % 2 + 1) * EROWS]

    def pairs(bank):
        return m.ps[:, bank:bank + 2, 0:2 * EROWS]

    def two(x):
        return x.rearrange("p (a c) -> p a c", a=2)

    with nc.Block() as block:

        @block.sync
        def _(sp):
            def load(q, s):
                e = sp.value_load(m.table[0:1, bass.ds(s + NSTEP, 1)], min_val=0, max_val=NE - 1)
                after(sp, s_lo[q], 2 * s)
                if not isinstance(s, int):
                    sp.wait_ge(sem_in[q], 16)
                load_third(m, io, sp, q, e)

            load_third(m, io, sp, DOWN, 0)
            load(GATE, 1)
            load(UP, 1)
            n = steps_of(sp)
            with sp.Fori(2, n) as s:
                load(GATE, s)
                load(UP, s)
                load(DOWN, s - 1)
            load(DOWN, last_three(sp)[2])

        @block.gpsimd
        def _(pool):
            def load(s):
                row = pool.value_load(m.table[0:1, bass.ds(s, 1)], min_val=0, max_val=NPAIR)
                after(pool, s_tb, s)
                nc.gpsimd.dma_start(xg[0], m.xs_dram[bass.ds(row, P), :]).then_inc(s_x, 16)
                nc.gpsimd.dma_start(xg[1], m.xs_dram[bass.ds(row + P, EREST), :]).then_inc(s_x, 16)

            def store(s):
                row = pool.value_load(m.table[0:1, bass.ds(s, 1)], min_val=0, max_val=NPAIR)
                pool.wait_ge(m.sem_stored, 32 * s + 32)
                pool.wait_ge(s_ya, s + 1)
                nc.gpsimd.dma_start(m.ys_dram[bass.ds(row, P), :], y[0]).then_inc(m.sem_stored, 16)
                pool.wait_ge(s_yb, s + 1)
                nc.gpsimd.dma_start(m.ys_dram[bass.ds(row + P, EREST), :], y[1]).then_inc(m.sem_stored, 16)

            for s in range(3):
                load(s)
            n = steps_of(pool)
            with pool.Fori(3, n) as s:
                load(s)
                store(s - 3)
            for s in last_three(pool):
                store(s)
            pool.wait_ge(m.sem_stored, 32 * n + 32)

        @block.tensor
        def _(pe):
            def turn_rows(s):
                pe.wait_ge(s_x, 32 * s + 32)
                for k in range(KT):
                    if k == 0:
                        after(pe, s_ya, s - 2)
                    if k == 4:
                        after(pe, s_silu, s)
                    out = turned(k)
                    nc.tensor.transpose(out[:, 0:P], xg[0][:, k:DM:KT], m.ident[:])
                    last = nc.tensor.transpose(out[:, P:EROWS], xg[1][:, k:DM:KT], m.ident[0:EREST, 0:EREST])
                    if k == 3:
                        last.then_inc(s_ta, 1)
                last.then_inc(s_tb, 1)

            def products(w, bank, done):
                for f in range(FT):
                    out = m.ps[:, bank + f // 2, f % 2 * EROWS:(f % 2 + 1) * EROWS]
                    for k in range(KT):
                        for i, (a, b) in enumerate(PASSES):
                            last = nc.tensor.matmul(out, w[:, a, k, f * P:(f + 1) * P], xT[:, b, k, :],
                                                    start=(k == 0 and i == 0), stop=(k == KT - 1 and i == 2))
                last.then_inc(done, 1)

            def gate(s):
                pe.wait_ge(s_lo[GATE], 2 * s + 2)
                pe.wait_ge(s_xl, 2 * s + 2)
                products(wg, 0, s_g)

            def up(s):
                pe.wait_ge(s_lo[UP], 2 * s + 2)
                after(pe, s_h, s)
                products(wu, 2, s_u)

            def down(s, turned_since=True):
                pe.wait_ge(s_hl, s + 1)
                pe.wait_ge(s_lo[DOWN], 2 * s + 2)
                for b, rows in ((1, slice(P, EROWS)), (0, slice(0, P))):
                    after(pe, (s_ya, s_yb)[b], s)
                    if b == 0 and turned_since:
                        pe.wait_ge(s_xl, 2 * s + 5)
                    for c in range(2):
                        out = m.ps[0:rows.stop - rows.start, 4 + 2 * b + c, :]
                        for k in range(FT):
                            for i, (p, q) in enumerate(PASSES):
                                last = nc.tensor.matmul(out, hT[:, p, k, rows], wd[:, q, k, c * 512:(c + 1) * 512],
                                                        start=(k == 0 and i == 0), stop=(k == FT - 1 and i == 2))
                    last.then_inc((s_da, s_db)[b], 1)

            turn_rows(0)
            gate(0)
            up(0)
            turn_rows(1)
            gate(1)
            n = steps_of(pe)
            with pe.Fori(2, n) as s:
                up(s - 1)
                turn_rows(s)
                down(s - 2)
                gate(s)
            _, last_but_one, last_one = last_three(pe)
            up(last_one)
            down(last_but_one, False)
            down(last_one, False)

        @block.scalar
        def _(act):
            def high(q, s):
                act.wait_ge(sem_in[q], 16 * s + 16)
                after(act, used[q], s)
                for i in range(2):
                    part = slice(i * HALF, (i + 1) * HALF)
                    nc.scalar.copy(wparts[q][:, 0, part], raw_third(m, q)[:, part]).then_inc(s_hi[q], 1)

            def rows_high(s):
                after(act, s_u, s)
                for i, (t, bank) in enumerate(((s_ta, 4), (s_tb, 0))):
                    act.wait_ge(t, s + 1)
                    nc.scalar.copy(xT[:, 0, 4 * i:4 * i + 4, :].rearrange("p (a k) c -> p a (k c)", a=2),
                                   pairs(bank)).then_inc(s_xh, 1)

            def hidden_high(s):
                act.wait_ge(s_h, s + 1)
                after(act, s_da, s)
                nc.scalar.copy(hT[:, 0].rearrange("p k c -> p (k c)"), h).then_inc(s_hh, 1)

            def gated(s):
                act.wait_ge(s_g, s + 1)
                nc.scalar.activation(two(silu), pairs(0), ACT.Silu).then_inc(s_silu, 1)

            def keep(s):
                act.wait_ge(s_db, s + 1)
                act.wait_ge(m.sem_stored, 32 * s + 32)
                nc.scalar.copy(two(y[1]), m.ps[0:EREST, 6:8, :]).then_inc(s_yb, 1)

            high(GATE, 0)
            rows_high(0)
            high(UP, 0)
            gated(0)

            def body(s):
                high(GATE, s)
                rows_high(s)
                high(UP, s)
                if not isinstance(s, int):
                    keep(s - 2)
                hidden_high(s - 1)
                high(DOWN, s - 1)
                gated(s)

            body(1)
            n = steps_of(act)
            with act.Fori(2, n) as s:
                body(s)
            _, last_but_one, last_one = last_three(act)
            keep(last_but_one)
            hidden_high(last_one)
            high(DOWN, last_one)
            keep(last_one)

        @block.vector
        def _(dve):
            def low(q, s):
                for i in range(2):
                    part = slice(i * HALF, (i + 1) * HALF)
                    dve.wait_ge(s_hi[q], 2 * s + (i + 1))
                    nc.vector.tensor_tensor(wparts[q][:, 1, part], raw_third(m, q)[:, part], wparts[q][:, 0, part],
                                            ALU.subtract).then_inc(s_lo[q], 1)

            def rows_low(s):
                for i, bank in enumerate((4, 0)):
                    dve.wait_ge(s_xh, 2 * s + (i + 1))
                    part = xT[:, :, 4 * i:4 * i + 4, :].rearrange("p h (a k) c -> p h a (k c)", a=2)
                    nc.vector.tensor_tensor(part[:, 1], pairs(bank), part[:, 0], ALU.subtract).then_inc(s_xl, 1)

            def hidden(s):
                dve.wait_ge(s_silu, s + 1)
                dve.wait_ge(s_u, s + 1)
                after(dve, s_hl, s)
                nc.vector.tensor_tensor(two(h), two(silu), pairs(2), ALU.mult).then_inc(s_h, 1)

            def hidden_low(s):
                dve.wait_ge(s_hh, s + 1)
                nc.vector.tensor_tensor(hT[:, 1].rearrange("p k c -> p (k c)"), h, hT[:, 0].rearrange("p k c -> p (k c)"),
                                        ALU.subtract).then_inc(s_hl, 1)

            def keep(s):
                dve.wait_ge(s_da, s + 1)
                dve.wait_ge(m.sem_stored, 32 * s + 32)
                nc.vector.tensor_copy(two(y[0]), m.ps[:, 4:6, :]).then_inc(s_ya, 1)

            low(GATE, 0)
            rows_low(0)
            low(UP, 0)

            def body(s):
                low(GATE, s)
                hidden(s - 1)
                rows_low(s)
                low(UP, s)
                if not isinstance(s, int):
                    keep(s - 2)
                hidden_low(s - 1)
                low(DOWN, s - 1)

            body(1)
            n = steps_of(dve)
            with dve.Fori(2, n) as s:
                body(s)
            _, last_but_one, last_one = last_three(dve)
            hidden(last_one)
            keep(last_but_one)
            hidden_low(last_one)
            low(DOWN, last_one)
            keep(last_one)


def combine(nc, m, io):
    yg = [[m.R3[:, (2 * t + c) * DM:(2 * t + c + 1) * DM] for c in range(2)] for t in range(NT9)]
    gain, bias = m.RK[:, 0:DM], m.RK[:, DM:2 * DM]
    sc = m.RK[:, 2 * DM:2 * DM + 20 * NT9].rearrange("p (t c) -> p t c", t=NT9)
    s_c, s_m1, s_z = m.sem("c_consts"), m.sem("c_scaled"), m.sem("c_added")
    s_g = [m.sem(f"c_gathered{t}") for t in range(NT9)]
    s_x1 = [m.sem(f"c_x1_{t}") for t in range(TT)]
    s_stat, s_mv, s_eps, s_rstd, s_norm = (m.sem("c_" + n) for n in ("stats", "moments", "eps", "rstd", "normal"))
    s_gain, s_y, s_out = m.sem("c_gain"), m.sem("c_y"), m.sem("c_out")
    s_nm = m.sem("c_shift")
    yp = io["y_prompt"].rearrange("a (t p) d -> p (a t) d", p=P)
    ys = io["y_sample"].rearrange("b t d -> (b t) d")
    with nc.Block() as block:

        @block.sync
        def _(sp):
            sp.dma_start(gain, io["ln2_g"].rearrange("l d -> (l d)").partition_broadcast(P)).then_inc(s_c, 16)
            sp.dma_start(bias, io["ln2_b"].rearrange("l d -> (l d)").partition_broadcast(P)).then_inc(s_c, 16)
            for t in range(TT):
                sp.dma_start(m.x1[t], m.x1_dram[t * P:(t + 1) * P, :]).then_inc(s_x1[t], 16)
            for t in range(NT9):
                sp.wait_ge(s_y, t + 1)
                sp.dma_start(yp[:, t, :] if t < TT else ys, m.x1[t]).then_inc(s_out, 16)
            sp.wait_ge(s_out, 16 * NT9)

        @block.gpsimd
        def _(pool):
            def scale_rows(t):
                n = rows_of(t)
                pool.wait_ge(s_norm, t + 1)
                nc.gpsimd.tensor_tensor(m.x1[t], m.x1[t], gain[0:n], ALU.mult).then_inc(s_gain, 1)

            for t in range(NT9):
                n = rows_of(t)
                for c in range(2):
                    col = 2 * t + c
                    nc.gpsimd.indirect_dma_start(
                        out=yg[t][c][0:n], out_offset=None, in_=m.ys_dram[0:NPAIR, :],
                        in_offset=bass.IndirectOffsetOnAxis(ap=m.slots[0:n, col:col + 1], axis=0)).then_inc(s_g[t], 16)
            pool.wait_ge(s_c, 32)
            for t in range(NT9):
                n = rows_of(t)
                inverse_deviation(nc, m, pool, n, sc[:, t, 12:14], sc[:, t, 14:15], s_mv, s_eps, s_rstd, t)
                if t >= 1:
                    scale_rows(t - 1)
            scale_rows(TT)

        @block.scalar
        def _(act):
            def normal(t):
                n = rows_of(t)
                act.wait_ge(s_nm, t + 1)
                nc.scalar.activation(m.x1[t], m.x1[t], ACT.Identity, bias=sc[0:n, t, 15:16],
                                     scale=sc[0:n, t, 14:15]).then_inc(s_norm, 1)

            for t in range(NT9):
                n = rows_of(t)
                act.wait_ge(s_g[t], 32)
                nc.scalar.mul(yg[t][0][0:n], yg[t][0][0:n], m.pair_w[0:n, t, 0:1]).then_inc(s_m1, 1)
                if t >= 1:
                    normal(t - 1)
            normal(TT)

        @block.vector
        def _(dve):
            stt = nc.vector.scalar_tensor_tensor

            def add(t):
                n = rows_of(t)
                dve.wait_ge(s_m1, t + 1)
                if t < TT:
                    dve.wait_ge(s_x1[t], 16)
                stt(out=m.x1[t], in0=m.x1[t], scalar=ALPHA, in1=yg[t][0][0:n], op0=ALU.mult, op1=ALU.add).then_inc(s_z, 1)
                dve.wait_ge(s_z, 2 * t + 1)
                stt(out=m.x1[t], in0=yg[t][1][0:n], scalar=m.pair_w[0:n, t, 1:2], in1=m.x1[t], op0=ALU.mult,
                    op1=ALU.add).then_inc(s_z, 1)
                dve.wait_ge(s_z, 2 * t + 2)
                nc.vector.bn_stats(sc[0:n, t, 0:6], m.x1[t][:, 0:512])
                nc.vector.bn_stats(sc[0:n, t, 6:12], m.x1[t][:, 512:1024]).then_inc(s_stat, 1)
                dve.wait_ge(s_stat, t + 1)
                nc.vector.bn_aggr(sc[0:n, t, 12:14], sc[0:n, t, 0:12]).then_inc(s_mv, 1)

            def shift(t):
                n = rows_of(t)
                dve.wait_ge(s_rstd, t + 1)
                stt(out=sc[0:n, t, 15:16], in0=sc[0:n, t, 12:13], scalar=-1.0, in1=sc[0:n, t, 14:15], op0=ALU.mult,
                    op1=ALU.mult).then_inc(s_nm, 1)

            def bias_rows(t):
                n = rows_of(t)
                dve.wait_ge(s_gain, t + 1)
                nc.vector.tensor_tensor(m.x1[t], m.x1[t], bias[0:n], ALU.add).then_inc(s_y, 1)

            dve.wait_ge(s_c, 32)
            for t in range(NT9 + 2):
                if t < NT9:
                    add(t)
                if 1 <= t <= NT9:
                    shift(t - 1)
                if t >= 2:
                    bias_rows(t - 2)


_INS = ["x_prompt", "x_sample", "cache_kv", "cache_win", "page_table", "w_in", "gmlp_ln_g", "gmlp_ln_b", "gmlp_ws",
        "gmlp_bs", "cmp_pos", "cmp_w1", "cmp_w2", "w_branch_a", "w_branch_b", "w_out", "ln1_g", "ln1_b", "ln2_g",
        "ln2_b", "w_router", "b_router", "w_gate", "w_up", "w_down"]
_OUTS = [("y_prompt", (1, SEQ, DM)), ("y_sample", (NB, 1, DM)), ("kv_rows_prompt", (1, 1, SEQ, 4, NKV, HD)),
         ("win_prompt", (1, 1, WINDOW, 2, NKV, HD)), ("kv_rows_sample", (NB, 1, 1, 4, NKV, HD)),
         ("win_sample", (NB, 1, PAST, 2, NKV, HD)), ("gmlp_v_sample", (NB, 1, 1, DM))]


def program(nc, io, upto=99):
    with ExitStack() as ctx:
        m = Memory(nc, ctx)
        stages = [lambda: load_and_turn_x(nc, m, io), lambda: project_kv(nc, m, io), lambda: project_q(nc, m, io),
                  lambda: compress_keys(nc, m, io), lambda: attend_samples(nc, m, io), lambda: attend_prompt(nc, m),
                  lambda: gmlp_values(nc, m, io), lambda: gmlp_gate(nc, m, io), lambda: merge(nc, m, io),
                  lambda: output_and_router(nc, m, io), lambda: route_and_dispatch(nc, m, io),
                  lambda: experts(nc, m, io), lambda: combine(nc, m, io)]
        for stage in stages[:upto]:
            stage()
            if stage is stages[5]:
                m.clear_semaphores()


def kernel(**inputs):
    from concourse import bacc
    from concourse.bass_utils import run_bass_kernel_spmd

    nc = bacc.Bacc("TRN2", target_bir_lowering=False, num_devices=1)
    arrays, io = {}, {}
    for name in _INS:
        a = np.ascontiguousarray(inputs[name])
        arrays[f"in_{name}"] = a
        io[name] = nc.dram_tensor(f"in_{name}", a.shape, mybir.dt.from_np(a.dtype), kind="ExternalInput").ap()
    for name, shape in _OUTS:
        io[name] = nc.dram_tensor(f"out_{name}", shape, F32, kind="ExternalOutput").ap()
    program(nc, io)
    r = run_bass_kernel_spmd(nc, [arrays], core_ids=[0])
    return tuple(r.results[0][f"out_{name}"] for name, _ in _OUTS)
```

```python
from contextlib import ExitStack

import concourse.bass as bass
import numpy as np
from concourse import mybir
from concourse.alu_op_type import AluOpType as ALU

F32 = mybir.dt.float32
F32R = mybir.dt.float32r
BF16 = mybir.dt.bfloat16
I32 = mybir.dt.int32
U32 = mybir.dt.uint32
ACT = mybir.ActivationFunctionType
AX = mybir.AxisListType

P = 128
DM = 1024
SEQ = 1024
NB = 8
NTOK = SEQ + NB
TT = SEQ // P
NT9 = TT + 1
KT = DM // P
NC3 = 3
CW = NTOK // NC3
NH, NKV, HD = 16, 2, 64
QPK = NH // NKV
CMP_STRIDE, CMP_BLOCK = 16, 32
CMP_PAIRS = CMP_BLOCK // 2
NCMP = SEQ // CMP_STRIDE - 1
PAST, PAGE = 256, 128
NPAGE = PAST // PAGE
NPG = NB * NPAGE
CKEYS = NB * PAST
SCMP = PAST // CMP_STRIDE - 1
WINDOW = 512
WBLK = WINDOW // P
NEG = -1e30
SCALE = HD ** -0.5
ALPHA = 2.0 ** 0.25
EPS = 1e-5
NE, NG, EPG = 16, 4, 4
FE = 512
FT = FE // P
NPAIR = 2 * NTOK
NROWS = NPAIR + P
NSTEP = NE + (NPAIR - 1) // P
NKX = NTOK // P + 1
COL_V, COL_Q, COL_KV = 1024, 2048, 3072
COL_GA, COL_GB = 3888, 4912
KVW = 6 * 128 + 3 * NH
KVH = KVW // 2


def rows_of(t):
    return P if t < TT else NB


def span(t):
    return slice(t * P, t * P + rows_of(t))


class Memory:

    def __init__(self, nc, ctx):
        self.nc, self.ctx, self.sems = nc, ctx, []
        self.at_R3 = -(-nc.sbuf_base // 32) * 32
        self.R3 = self.sb("region_3", [P, 3 * KT * NTOK])
        self.RO = self.R3[:, KT * NTOK:2 * KT * NTOK]
        self.RA = self.R3[:, 2 * KT * NTOK:3 * KT * NTOK]
        self.RK = self.sb("region_k", [P, 8496])
        self.at_RW = -(-nc.sbuf_base // 32) * 32
        self.RW = self.sb("region_w", [P, 16384])
        self.ps = ctx.enter_context(nc.psum_tensor("ps", [P, 8, 512], F32))
        self.ident = self.sb("ident", [P, P])
        self.gates = self.sb("gates", [P, NT9, 3 * NH])
        self.xT = view(self.R3, 0, KT, NTOK)
        self.qT = view(self.RO, 0, KT, NTOK)
        self.aT = view(self.RA, 0, KT, NTOK)
        self.kT = view(self.RK, 0, 4, NTOK)
        self.vv = view(self.RK, 4 * NTOK, NT9, 256)
        self.kvst = view(self.RK, 4 * NTOK + NT9 * 256, 2, KVW)
        self.small = self.sb("small", [P, 1408])
        self.k_stacks = self.parts("key_stacks", self.at_RW + 4 * 6144, 8 * SEQ).rearrange(
            "p (a g h n) -> p a g h n", a=2, g=NKV, h=2)
        self.kc_stacks = self.sb("compressed_key_stacks", [P, NKV, 2, 64], F32R)
        self.q_stacks = self.parts("query_stacks", self.at_RW + 4 * 14336, 2 * SEQ).rearrange("p (g n) -> p g n", g=NKV)
        self.wkv_parts = self.parts("w_kv_parts", self.at_R3 + 4 * KT * NTOK, 2 * KT * KVW)
        self.x_parts = self.parts("x_parts", self.at_RW + 4 * KT * KVW, 4 * DM)
        self.wo_parts = self.parts("w_out_parts", self.at_R3, 2 * KT * DM)
        self.y_parts = self.parts("y_parts", self.at_R3 + 4 * 2 * KT * DM, 4 * DM)
        self.wg_parts, self.wu_parts, self.wd_parts = (
            self.parts(n + "_parts", self.at_R3 + 4 * 8192 * q, 8192) for q, n in enumerate(("gate", "up", "down")))
        self.xg_parts = self.parts("rows_parts", self.at_RW + 4 * 8192, 2 * DM)
        self.h_parts = self.parts("hidden_parts", self.at_RW + 4 * 10240, 2 * FE)
        self.kcT = self.sb("kcT", [P, 2 * P])
        self.vc = self.sb("vc", [P, 2, P])
        self.gs = self.sb("gates_sample_rows", [P, 3])
        self.page_ids = self.sb("page_ids", [1, NPG], I32)
        self.identb = self.sb("ident_bf16", [P, P], BF16)
        self.mask_diag = self.sb("mask_diag", [P, P], BF16)
        self.mask_edge = self.sb("mask_edge", [P, P], BF16)
        self.mask_cmp = self.sb("mask_cmp", [P, 56 + NCMP], BF16)
        self.x1 = [self.RW[:, t * DM:(t + 1) * DM] for t in range(TT)] + [self.small[0:NB, 0:DM]]
        self.aff = self.small[:, 1024:1024 + NT9 * NE].rearrange("p (t e) -> p t e", e=NE)
        self.pair_w = self.small[:, 1168:1168 + 2 * NT9].rearrange("p (t c) -> p t c", c=2)
        self.sem_wout, self.sem_gate, self.sem_up, self.sem_down, self.sem_stored = (
            ctx.enter_context(nc.semaphore(n)) for n in ("w_out_in", "gate_in", "up_in", "down_in", "rows_stored"))
        self.mhalf = self.sb("minus_half", [P, 1])
        self.table = self.sb("tile_table", [1, 3 * NSTEP + 2], I32)
        self.slots = self.sb("slots", [P, 2 * NT9], U32)
        self.x1_dram = nc.dram_tensor("x1_prompt", [SEQ, DM], F32, kind="Internal").ap()
        self.xs_dram = nc.dram_tensor("dispatched", [NROWS, DM], F32, kind="Internal").ap()
        self.ys_dram = nc.dram_tensor("expert_out", [NROWS, DM], F32, kind="Internal").ap()
        self.gate_dram = nc.dram_tensor("gate_scratch", [NB, 3 * NH], F32, kind="Internal").ap()

    def sb(self, name, shape, dt=F32):
        return self.ctx.enter_context(self.nc.sbuf_tensor(name, shape, dt))

    def parts(self, name, offset, n):
        return self.nc.alloc_sbuf_tensor_at(name, [P, n], F32R, offset=offset)[:]

    def sem(self, name):
        self.sems.append(self.nc.alloc_semaphore(name))
        return self.sems[-1]

    def clear_semaphores(self):
        self.nc.clear_and_free_semaphores(self.sems)
        self.sems = []
        self.nc.all_engine_barrier()


def view(region, offset, a, b, parts=P):
    return region[0:parts, offset:offset + a * b].rearrange("p (a b) -> p a b", a=a)


class FirstWeights:

    def __init__(self, m, io):
        self.w_in = io["w_in"].rearrange("l (k p) n -> p (l k) n", p=P)
        self.kv = view(m.RW, 0, KT, KVW)
        self.q = [view(m.RW, 12288 + b * KT * P, KT, P) for b in range(2)]
        self.s_kv = m.sem("kv_w")
        self.s_gd, self.s_gw = m.sem("gates_bounced"), m.sem("gates_scattered")
        self.s_kv_out, self.s_win = [m.sem("kv_out0"), m.sem("kv_out1")], m.sem("win_sample_out")
        self.kv_outs = [0, 0]
        self.s_q = [m.sem("q_w0"), m.sem("q_w1")]
        self.m = m

    def second_part(self):
        m = self.m
        self.u = [view(m.RW, 14336 + b * KT * P, KT, P) for b in range(2)]
        self.s_u = [m.sem("u_w0"), m.sem("u_w1")]
        self.s_merge = [m.sem("m_w0"), m.sem("m_w1")]

    def load_kv(self, sp):
        for h in range(2):
            sp.dma_start(self.kv[:, :, h * KVH:(h + 1) * KVH],
                         self.w_in[:, :, COL_KV + h * KVH:COL_KV + (h + 1) * KVH]).then_inc(self.s_kv, 16)

    def load_q(self, sp, j, b):
        for g in range(NKV):
            col = j * HD + (COL_Q + g * QPK * HD)
            sp.dma_start(self.q[b][:, :, g * HD:(g + 1) * HD], self.w_in[:, :, bass.ds(col, HD)]).then_inc(self.s_q[b], 16)

    def load_u(self, sp, jj, b):
        sp.dma_start(self.u[b], self.w_in[:, :, bass.ds(2 * P * jj + b * P, P)]).then_inc(self.s_u[b], 16)


class CompressInputs:

    def __init__(self, m):
        self.w1 = view(m.RA, 4096, 2 * CMP_PAIRS, P)
        self.pages = view(m.RW, 0, NPG, 256)
        self.w2 = m.small[:, 0:128].rearrange("p (c d) -> p c d", c=2)
        self.pos = m.small[0:CMP_PAIRS, 128:384].rearrange("p (c x) -> p c x", c=2)
        self.s_w1, self.s_w2, self.s_pt, self.s_page = (
            m.sem(n) for n in ("cmp_w1", "cmp_w2", "page_table_in", "cmp_pages"))


def load_pages(m, io, sp, columns, at, done):
    cache = io["cache_kv"].rearrange("n l p s h d -> (n l) p (s h d)")
    with sp.Fori(0, NPG) as i:
        page = sp.value_load(m.page_ids[0:1, bass.ds(i, 1)], min_val=0, max_val=cache.shape[0] - 1)
        sp.dma_start(m.RW[:, bass.ds(at + i * 256, 256)],
                     cache[bass.ds(page, 1), :, columns].rearrange("n p c -> p (n c)")).then_inc(done, 16)


def load_and_turn_x(nc, m, io, fw):
    xst = [m.RK[:, t * DM:(t + 1) * DM] for t in range(TT)] + [m.small[0:NB, 0:DM]]
    s_in = [m.sem(f"x_in{t}") for t in range(NT9)]
    s_turned, s_kept = m.sem("x_turned"), m.sem("x_kept")
    s_id0, s_id = m.sem("ident_clear"), m.sem("ident_ready")
    s_m0, s_m = m.sem("masks_clear"), m.sem("masks_ready")
    xp = io["x_prompt"].rearrange("a (t p) d -> p (a t) d", p=P)
    xs = io["x_sample"].rearrange("b t d -> (b t) d")
    with nc.Block() as block:

        @block.sync
        def _(sp):
            for t in range(NT9):
                sp.dma_start(xst[t], xp[:, t, :] if t < TT else xs).then_inc(s_in[t], 16)
            fw.load_kv(sp)

        @block.gpsimd
        def _(pool):
            nc.gpsimd.memset(m.ident[:], 0.0).then_inc(s_id0, 1)
            pool.wait_ge(s_id0, 1)
            nc.gpsimd.affine_select(out=m.ident[:], in_=m.ident[:], compare_op=ALU.not_equal, fill=1.0,
                                    base=0, pattern=[[-1, P]], channel_multiplier=1).then_inc(s_id, 1)
            pool.wait_ge(s_id, 1)
            nc.gpsimd.tensor_copy(m.identb[:], m.ident[:])
            nc.gpsimd.memset(m.mhalf[:], -0.5)
            for mask in (m.mask_diag, m.mask_edge, m.mask_cmp):
                nc.gpsimd.memset(mask[:], 0.0).then_inc(s_m0, 1)
            pool.wait_ge(s_m0, 3)
            nc.gpsimd.affine_select(out=m.mask_diag[:], in_=m.mask_diag[:], compare_op=ALU.is_ge, fill=NEG,
                                    base=0, pattern=[[-1, P]], channel_multiplier=1)
            nc.gpsimd.affine_select(out=m.mask_edge[:], in_=m.mask_edge[:], compare_op=ALU.is_gt, fill=NEG,
                                    base=0, pattern=[[1, P]], channel_multiplier=-1)
            nc.gpsimd.affine_select(out=m.mask_cmp[:], in_=m.mask_cmp[:], compare_op=ALU.is_ge, fill=NEG,
                                    base=56 * CMP_STRIDE - (CMP_BLOCK - 1), pattern=[[-CMP_STRIDE, 56 + NCMP]],
                                    channel_multiplier=1).then_inc(s_m, 1)
            pool.wait_ge(s_m, 1)

        @block.tensor
        def _(pe):
            pe.wait_ge(s_id, 1)
            for t in range(NT9):
                n, bank = rows_of(t), 2 * (t % 2)
                pe.wait_ge(s_in[t], 16)
                if t >= 2:
                    pe.wait_ge(s_kept, t - 1)
                for k in range(KT):
                    out = m.ps[:, bank + k // 4, (k % 4) * P:(k % 4) * P + n]
                    last = nc.tensor.transpose(out, xst[t][:, k * P:(k + 1) * P], m.ident[0:n, 0:n])
                last.then_inc(s_turned, 1)

        @block.vector
        def _(dve):
            for t in range(NT9):
                dve.wait_ge(s_turned, t + 1)
                bank = 2 * (t % 2)
                src = m.ps[:, bank:bank + 2, :].rearrange("p b (k c) -> p (b k) c", k=4)[:, :, 0:rows_of(t)]
                nc.vector.tensor_copy(m.xT[:, :, span(t)], src).then_inc(s_kept, 1)


def project_kv(nc, m, io, fw):
    wkv = fw.kv
    st = m.kvst
    wparts = m.wkv_parts.rearrange("p (h k c) -> p h k c", h=2, k=KT)
    xparts = m.x_parts.rearrange("p (b h k c) -> p b h k c", b=2, h=2, k=KT)
    s_wh, s_wl, s_xh, s_xl = (m.sem("kv_" + n) for n in ("w_high", "w_low", "x_high", "x_low"))
    PASSES = ((0, 0), (0, 1), (1, 0))
    s_proj, s_row, s_gate = (m.sem(n) for n in ("kv_projected", "kv_rows_staged", "kv_gates"))
    s_vv, s_turned, s_kept = m.sem("kv_values"), m.sem("kv_turned"), m.sem("kv_kept")
    s_out = fw.s_kv_out
    s_win = fw.s_win
    kvp = io["kv_rows_prompt"].rearrange("a l (t p) s h d -> p (a l t) (s h d)", p=P)
    kvs = io["kv_rows_sample"].rearrange("b l t s h d -> (b l t) (s h d)")
    winp = io["win_prompt"].rearrange("a l (t p) s h d -> p (a l t) (s h d)", p=P)
    wins = io["win_sample"].rearrange("b l w s h d -> b (l w) (s h d)")
    cwin = io["cache_win"].rearrange("b l w s h d -> b (l w) (s h d)")
    outs = fw.kv_outs

    with nc.Block() as block:

        @block.sync
        def _(sp):
            for b in range(2):
                fw.load_q(sp, b, b)
            sp.dma_start(wins[:, 0:PAST - 1, :], cwin[:, 1:PAST, :]).then_inc(s_win, 16)
            for t in range(NT9):
                n, b = rows_of(t), t % 2
                sp.wait_ge(s_row, t + 1)
                dst = kvp[:, t, :] if t < TT else kvs
                sp.dma_start(dst, st[0:n, b, 0:512]).then_inc(s_out[b], 16)
                outs[b] += 16
                if t >= TT // 2:
                    dst = winp[:, t - TT // 2, :] if t < TT else wins[:, PAST - 1, :]
                    sp.dma_start(dst, st[0:n, b, 512:768]).then_inc(s_out[b], 16)
                    outs[b] += 16

        @block.tensor
        def _(pe):
            def turn(t):
                n = rows_of(t)
                pe.wait_ge(s_row, t + 1)
                if t >= 2:
                    pe.wait_ge(s_kept, t - 1)
                for c, col in enumerate((0, 128, 256, 512)):
                    last = nc.tensor.transpose(m.ps[:, 6 + t % 2, c * P:c * P + n], st[0:n, t % 2, col:col + P],
                                               m.ident[0:n, 0:n])
                last.then_inc(s_turned, 1)

            for t in range(NT9):
                n = rows_of(t)
                if t >= 2:
                    pe.wait_ge(s_row, t - 1)
                pe.wait_ge(s_xl, t + 1)
                for k in range(KT):
                    if t == 0:
                        pe.wait_ge(s_wl, k + 1)
                    for h in range(2):
                        for i, (a, b) in enumerate(PASSES):
                            last = nc.tensor.matmul(m.ps[0:n, 2 * (t % 2) + h, 0:KVH], xparts[:, t % 2, a, k, 0:n],
                                                    wparts[:, b, k, h * KVH:(h + 1) * KVH],
                                                    start=(k == 0 and i == 0), stop=(k == KT - 1 and i == 2))
                last.then_inc(s_proj, 1)
                if t >= 1:
                    turn(t - 1)
            turn(NT9 - 1)

        @block.scalar
        def _(act):
            act.wait_ge(fw.s_kv, 32)
            for k in range(KT):
                nc.scalar.copy(wparts[:, 0, k, :], wkv[:, k, :]).then_inc(s_wh, 1)
            for t in range(NT9):
                n, b = rows_of(t), t % 2
                act.wait_ge(s_proj, t + 1)
                if t >= 2:
                    act.wait_ge(s_turned, t - 1)
                    done = 16 * ((t - 2) // 2 + 1) + 16 * sum(1 for u in range(b, t - 1, 2) if u >= TT // 2)
                    act.wait_ge(s_out[b], done)
                    act.wait_ge(s_vv, t - 1)
                src = m.ps[0:n, 2 * b:2 * b + 2, 0:KVH]
                nc.scalar.copy(st[0:n, b, :].rearrange("p (h c) -> p h c", h=2), src).then_inc(s_row, 1)
                act.wait_ge(s_row, t + 1)
                nc.scalar.activation(m.gates[0:n, t, :], st[0:n, b, 768:KVW], ACT.Sigmoid).then_inc(s_gate, 1)

        @block.gpsimd
        def _(pool):
            for t in range(NT9):
                if t >= 2:
                    pool.wait_ge(s_proj, t - 1)
                nc.gpsimd.tensor_copy(xparts[:, t % 2, 0, :, 0:rows_of(t)], m.xT[:, :, span(t)]).then_inc(s_xh, 1)

        @block.vector
        def _(dve):
            def low_x(t):
                dve.wait_ge(s_xh, t + 1)
                part = xparts[:, t % 2, :, :, 0:rows_of(t)]
                nc.vector.tensor_tensor(part[:, 1], m.xT[:, :, span(t)], part[:, 0], ALU.subtract).then_inc(s_xl, 1)

            low_x(0)
            for k in range(KT):
                dve.wait_ge(s_wh, k + 1)
                nc.vector.tensor_tensor(wparts[:, 1, k, :], wkv[:, k, :], wparts[:, 0, k, :], ALU.subtract).then_inc(s_wl, 1)
            low_x(1)
            for t in range(NT9):
                n, b = rows_of(t), t % 2
                if t + 2 < NT9:
                    low_x(t + 2)
                dve.wait_ge(s_row, t + 1)
                src = st[0:n, b, 384:896 - 128].rearrange("p (a c) -> p a c", c=P)[:, 0:3:2, :]
                nc.vector.tensor_copy(m.vv[0:n, t, :].rearrange("p (a c) -> p a c", a=2), src).then_inc(s_vv, 1)
                dve.wait_ge(s_turned, t + 1)
                src = m.ps[:, 6 + b, :].rearrange("p (a c) -> p a c", a=4)[:, :, 0:n]
                nc.vector.tensor_copy(m.kT[:, :, span(t)], src).then_inc(s_kept, 1)


def project_q(nc, m, io, fw, ci):
    wq, s_w = fw.q, fw.s_q
    s_proj, s_kept = m.sem("q_projected"), m.sem("q_kept")
    with nc.Block() as block:

        @block.sync
        def _(sp):
            sp.dma_start(m.page_ids[:], io["page_table"].rearrange("(o b) n -> o (b n)", o=1)).then_inc(ci.s_pt, 16)
            sp.dma_start(ci.w2, io["cmp_w2"].rearrange("l c f d -> f (l c) d")).then_inc(ci.s_w2, 16)
            sp.dma_start(ci.pos, io["cmp_pos"].rearrange("l c (u s) d -> u (l c) (s d)", s=2)).then_inc(ci.s_w2, 16)
            sp.dma_start(ci.w1, io["cmp_w1"].rearrange("l c (u x) f -> x (l c u) f", x=P)).then_inc(ci.s_w1, 16)
            sp.wait_ge(ci.s_pt, 16)
            load_pages(m, io, sp, slice(0, 256), 0, ci.s_page)
            with sp.Fori(1, KT // 2) as jj:
                for b in range(2):
                    sp.wait_ge(s_proj, 2 * jj + (b - 1))
                    fw.load_q(sp, 2 * jj + b, b)

        @block.tensor
        def _(pe):
            def tile(b, jj=None):
                pe.wait_ge(s_w[b], 32 if jj is None else 32 * jj + 32)
                if jj is not None:
                    pe.wait_ge(s_kept, 2 * jj + (b - 1))
                for c in range(NC3):
                    cols = slice(c * CW, (c + 1) * CW)
                    for k in range(KT):
                        last = nc.tensor.matmul(m.ps[:, 3 * b + c, 0:CW], wq[b][:, k, :],
                                                m.xT[:, k, cols], start=(k == 0), stop=(k == KT - 1))
                last.then_inc(s_proj, 1)

            for b in range(2):
                tile(b)
            with pe.Fori(1, KT // 2) as jj:
                for b in range(2):
                    tile(b, jj)

        @block.vector
        def _(dve):
            with dve.Fori(0, KT // 2) as jj:
                for b in range(2):
                    dve.wait_ge(s_proj, 2 * jj + (b + 1))
                    dst = m.RO[:, bass.ds((2 * jj + b) * NTOK, NTOK)].rearrange("p (a c) -> p a c", a=NC3)
                    nc.vector.tensor_scalar(dst, m.ps[:, 3 * b:3 * b + 3, 0:CW], SCALE, None, ALU.mult).then_inc(s_kept, 1)


class SampleInputs:

    def __init__(self, m):
        self.pages = [view(m.RW, 4096, NPG, 256), view(m.RW, 8192, NPG, 256)]
        self.s_page = m.sem("att_pages")


def compress_keys(nc, m, io, fw, ci, si):
    w1 = ci.w1.rearrange("p (c u) f -> p c u f", c=2)
    small = m.small
    posT = small[:, 384:384 + 2 * CMP_PAIRS].rearrange("p (c u) -> p c u", c=2)
    bias = small[:, 416:418]
    hid = small[:, 448:448 + 4 * 240].rearrange("p (u n) -> p u n", u=4)
    stacks = [m.RW[:, 12288:12288 + 4 * SEQ // 2].rearrange("p (c g u) -> p c g u", c=2, g=NKV),
              m.RA[:, 0:4 * CKEYS // 2].rearrange("p (c g u) -> p c g u", c=2, g=NKV)]
    s_posT, s_posk = m.sem("pos_turned"), m.sem("pos_kept")
    s_bias, s_biask = m.sem("cmp_bias"), m.sem("cmp_bias_kept")
    s_turned, s_sv, s_sa = m.sem("cmp_turned"), m.sem("cmp_stacked_by_dve"), m.sem("cmp_stacked_by_act")
    s_hid, s_act, s_out, s_end = m.sem("cmp_hidden"), m.sem("cmp_gelu"), m.sem("cmp_outputs"), m.sem("cmp_kept")
    units = [(src, c) for src in range(2) for c in range(2)]
    nkeys = (NCMP, NB * SCMP)
    NPT = NPG // 4 * 2

    def stack(copy, dst, src):
        for parity in range(2):
            last = copy(dst[parity * HD:(parity + 1) * HD], src[:, parity::2])
        return last

    with nc.Block() as block:

        @block.sync
        def _(sp):
            load_pages(m, io, sp, slice(256, 512), 4096, si.s_page)
            sp.dma_start(m.gate_dram, m.gates[0:NB, TT, :]).then_inc(fw.s_gd, 16)
            sp.wait_ge(fw.s_gd, 16)
            for h in range(NH):
                sp.dma_start(m.gs[h * NB:(h + 1) * NB, :], m.gate_dram[:, 3 * h:3 * h + 3]).then_inc(fw.s_gw, 16)
            win = io["cache_win"].rearrange("b l (n p) s h d -> (b l n) p (s h d)", p=P)
            sp.dma_start(si.pages[1], win.rearrange("n p c -> p n c")).then_inc(si.s_page, 16)
            for b in range(2):
                sp.wait_ge(fw.s_kv_out[b], fw.kv_outs[b])
            sp.wait_ge(fw.s_win, 16)

        @block.tensor
        def _(pe):
            pe.wait_ge(ci.s_w2, 32)
            for c in range(2):
                last = nc.tensor.transpose(m.ps[:, 0, c * CMP_PAIRS:(c + 1) * CMP_PAIRS], ci.pos[:, c, :],
                                           m.ident[0:CMP_PAIRS, 0:CMP_PAIRS])
            last.then_inc(s_posT, 1)
            pe.wait_ge(ci.s_page, 16 * NPG)
            for i in range(NPT):
                q, c = i // 2, i % 2
                if i >= 2:
                    pe.wait_ge(s_sv, i + 1)
                    pe.wait_ge(s_sa, i + 1)
                for r in range(4):
                    last = nc.tensor.transpose(m.ps[:, 4 + i % 2, r * P:(r + 1) * P],
                                               ci.pages[:, 4 * q + r, c * P:(c + 1) * P], m.ident[:])
                last.then_inc(s_turned, 1)
                if i == 1:
                    pe.wait_ge(s_posk, 1)
                    pe.wait_ge(ci.s_w1, 16)
                    for c in range(2):
                        for u in range(CMP_PAIRS):
                            last = nc.tensor.matmul(m.ps[:, 1, c:c + 1], w1[:, c, u, :], posT[:, c, u:u + 1],
                                                    start=(u == 0), stop=(u == CMP_PAIRS - 1))
                    last.then_inc(s_bias, 1)

            def hidden(n):
                src, c = units[n]
                for u in range(CMP_PAIRS):
                    half = CMP_STRIDE // 2
                    if src == 0:
                        rhs = stacks[0][:, c, :, u:u + half * (NCMP - 1) + 1:half]
                    else:
                        rhs = stacks[1][:, c].rearrange("p g (b t) -> p (g b) t", b=NB)[
                            :, :, u:u + half * (SCMP - 1) + 1:half]
                    out = m.ps[:, 2 + n % 2, 0:NKV * nkeys[src]]
                    last = nc.tensor.matmul(out, w1[:, c, u, :], rhs, start=(u == 0), stop=(u == CMP_PAIRS - 1))
                last.then_inc(s_hid, 1)

            def outputs(src):
                n = nkeys[src]
                for g in range(2):
                    nc.tensor.matmul(m.ps[g * HD:(g + 1) * HD, 6, 0:n], ci.w2[:, 0, :],
                                     hid[:, 2 * src, g * n:(g + 1) * n], start=True, stop=True)
                for g in range(2):
                    last = nc.tensor.matmul(m.ps[0:n, 7, g * HD:(g + 1) * HD], hid[:, 2 * src + 1, g * n:(g + 1) * n],
                                            ci.w2[:, 1, :], start=(g == 0), stop=(g == 1), skip_group_check=True)
                last.then_inc(s_out, 1)

            for n in range(4):
                if n < 2:
                    pe.wait_ge(s_sv, n + 1)
                    pe.wait_ge(s_sa, n + 1)
                if n == 2:
                    pe.wait_ge(s_sv, 2 + NPT)
                    pe.wait_ge(s_sa, 2 + NPT)
                if n >= 2:
                    pe.wait_ge(s_act, n - 1)
                hidden(n)
                if n == 2:
                    pe.wait_ge(s_act, 2)
                    outputs(0)
            pe.wait_ge(s_act, 4)
            pe.wait_ge(s_end, 1)
            outputs(1)

        @block.scalar
        def _(act):
            for c in range(2):
                stack(nc.scalar.copy, stacks[0][:, c, 1], m.kT[HD:P, c, 0:SEQ]).then_inc(s_sa, 1)
            for i in range(NPT):
                q, c = i // 2, i % 2
                act.wait_ge(s_turned, i + 1)
                act.wait_ge(s_sv, i + 3)
                stack(nc.scalar.copy, stacks[1][:, c, 1, q * 256:(q + 1) * 256], m.ps[HD:P, 4 + i % 2, :]).then_inc(s_sa, 1)
            act.wait_ge(s_biask, 1)
            for n, (src, c) in enumerate(units):
                act.wait_ge(s_hid, n + 1)
                nc.scalar.activation(hid[:, n, 0:NKV * nkeys[src]], m.ps[:, 2 + n % 2, 0:NKV * nkeys[src]],
                                     ACT.Gelu_apprx_tanh, bias=bias[:, c:c + 1]).then_inc(s_act, 1)

        @block.vector
        def _(dve):
            for c in range(2):
                stack(nc.vector.tensor_copy, stacks[0][:, c, 0], m.kT[0:HD, c, 0:SEQ]).then_inc(s_sv, 1)
            dve.wait_ge(s_posT, 1)
            nc.vector.tensor_copy(small[:, 384:384 + 2 * CMP_PAIRS], m.ps[:, 0, 0:2 * CMP_PAIRS]).then_inc(s_posk, 1)
            for i in range(NPT):
                q, c = i // 2, i % 2
                dve.wait_ge(s_turned, i + 1)
                stack(nc.vector.tensor_copy, stacks[1][:, c, 0, q * 256:(q + 1) * 256], m.ps[0:HD, 4 + i % 2, :]).then_inc(s_sv, 1)
            dve.wait_ge(s_bias, 1)
            nc.vector.tensor_copy(bias, m.ps[:, 1, 0:2]).then_inc(s_biask, 1)
            for src in range(2):
                n = nkeys[src]
                dve.wait_ge(s_out, src + 1)
                nc.vector.tensor_copy(m.kcT[:, src * P:src * P + n], m.ps[:, 6, 0:n])
                nc.vector.tensor_copy(m.vc[0:n, src, :], m.ps[0:n, 7, 0:P]).then_inc(s_end, 1)


def attend_samples(nc, m, fw, si):
    pages = si.pages
    cT = view(m.RW, 0, 2, CKEYS)
    NS = CKEYS + NB
    S = m.RA[:, 0:NS]
    PT = view(m.RA, 2176, NPG + 1, P)
    sm = m.small
    qs = sm[:, 0:64]
    onehot, mask = sm[:, 64:72], sm[:, 72:80]
    stat = sm[:, 80:92]
    O = view(sm, 128, 3, P)
    s_c0, s_c1, s_q = m.sem("onehot"), m.sem("sample_mask"), m.sem("sample_q")
    s_turned, s_kept = m.sem("page_turned"), m.sem("page_kept")
    s_score, s_masked, s_max = m.sem("s_scores"), m.sem("s_masked"), m.sem("s_max")
    s_exp, s_pt, s_ptk = m.sem("s_probs"), m.sem("s_probs_turned"), m.sem("s_probs_kept")
    s_pv, s_sc, s_o, s_oT, s_sum = m.sem("s_values"), m.sem("s_scaled"), m.sem("s_branch"), m.sem("s_oT"), m.sem("s_rowsum")
    s_oTk = m.sem("s_oT_kept")
    ngroup = (1, 5, 5)
    with nc.Block() as block:

        @block.tensor
        def _(pe):
            g_t = 0
            n_pt = 0
            for br in range(3):
                if br == 0:
                    pe.wait_ge(s_q, 1)
                else:
                    pe.wait_ge(si.s_page, 16 * (NPG + 1))
                    for q in range(NPG // 4):
                        if g_t >= 2:
                            pe.wait_ge(s_kept, g_t - 1)
                        for r in range(4):
                            last = nc.tensor.transpose(m.ps[:, 6 + g_t % 2, r * P:(r + 1) * P],
                                                       pages[br - 1][:, 4 * q + r, 0:P], m.ident[:])
                        last.then_inc(s_turned, 1)
                        g_t += 1
                    pe.wait_ge(s_kept, g_t)
                    pe.wait_ge(s_masked, br)
                for g in range(NKV):
                    rows = slice(g * HD, (g + 1) * HD)
                    if br == 0:
                        last = nc.tensor.matmul(m.ps[rows, 4, 0:NB * SCMP], qs[rows, :], m.kcT[rows, P:P + NB * SCMP],
                                                start=True, stop=True)
                    else:
                        for c in range(4):
                            nc.tensor.matmul(m.ps[rows, c, :], qs[rows, :], cT[rows, br - 1, c * 512:(c + 1) * 512],
                                             start=True, stop=True)
                        last = nc.tensor.matmul(m.ps[rows, 4, 0:NB], qs[rows, :], m.kT[rows, 1 + br, SEQ:NTOK],
                                                start=True, stop=True)
                last.then_inc(s_score, 1)
                pe.wait_ge(s_exp, br + 1)
                pe.wait_ge(s_kept, g_t)
                for q in range(ngroup[br]):
                    if n_pt >= 2:
                        pe.wait_ge(s_ptk, n_pt - 1)
                    if br == 0:
                        last = nc.tensor.transpose(m.ps[0:NB * SCMP, 6 + n_pt % 2, 0:P], S[:, 0:NB * SCMP], m.ident[:])
                    elif q < 4:
                        for r in range(4):
                            k = 4 * q + r
                            last = nc.tensor.transpose(m.ps[:, 6 + n_pt % 2, r * P:(r + 1) * P],
                                                       S[:, k * P:(k + 1) * P], m.ident[:])
                    else:
                        last = nc.tensor.transpose(m.ps[0:NB, 6 + n_pt % 2, 0:P], S[:, CKEYS:NS], m.ident[:])
                    last.then_inc(s_pt, 1)
                    n_pt += 1
                pe.wait_ge(s_ptk, n_pt)
                if br >= 1:
                    pe.wait_ge(s_o, br)
                if br == 0:
                    last = nc.tensor.matmul(m.ps[:, 5, 0:P], PT[0:NB * SCMP, 0, :], m.vc[0:NB * SCMP, 1, :],
                                            start=True, stop=True)
                else:
                    for k in range(NPG):
                        nc.tensor.matmul(m.ps[:, 5, 0:P], PT[:, k, :], pages[br - 1][:, k, P:2 * P],
                                         start=(k == 0), stop=False)
                    last = nc.tensor.matmul(m.ps[:, 5, 0:P], PT[0:NB, NPG, :],
                                            m.vv[0:NB, TT, (br - 1) * P:br * P], start=False, stop=True)
                last.then_inc(s_pv, 1)
            pe.wait_ge(s_sum, 1)
            nc.tensor.transpose(m.ps[:, 6, 0:P], O[:, 0, :], m.ident[:]).then_inc(s_oT, 1)

        @block.scalar
        def _(act):
            for br in range(3):
                act.wait_ge(s_max, br + 1)
                n = NB * SCMP if br == 0 else NS
                nc.scalar.activation(S[:, 0:n], S[:, 0:n], ACT.Exp, bias=stat[:, br:br + 1],
                                     accum_out=stat[:, 3 + br:4 + br]).then_inc(s_exp, 1)

        @block.vector
        def _(dve):
            nc.vector.tensor_reduce(onehot, m.ident[:].rearrange("p (a b) -> p b a", b=NB), AX.X, ALU.add).then_inc(s_c0, 1)
            nc.vector.tensor_copy(qs.rearrange("p (h b) -> p h b", b=NB), m.qT[:, :, SEQ:NTOK]).then_inc(s_q, 1)
            dve.wait_ge(s_c0, 1)
            nc.vector.tensor_scalar(mask, onehot, 1.0, -NEG, ALU.subtract, ALU.mult).then_inc(s_c1, 1)
            dve.wait_ge(s_c1, 1)
            g_t = n_pt = 0
            for br in range(3):
                if br >= 1:
                    for q in range(NPG // 4):
                        g_t += 1
                        dve.wait_ge(s_turned, g_t)
                        nc.vector.tensor_copy(cT[:, br - 1, q * 512:(q + 1) * 512],
                                              m.ps[:, 6 + (g_t - 1) % 2, :]).then_inc(s_kept, 1)
                dve.wait_ge(s_score, br + 1)
                if br >= 1:
                    dve.wait_ge(s_pt, n_pt)
                if br == 0:
                    nc.vector.tensor_tensor(S[:, 0:NB * SCMP].rearrange("p (b n) -> p b n", b=NB),
                                            m.ps[:, 4, 0:NB * SCMP].rearrange("p (b n) -> p b n", b=NB),
                                            mask.unsqueeze(2).to_broadcast([P, NB, SCMP]), ALU.add).then_inc(s_masked, 1)
                    n = NB * SCMP
                else:
                    nc.vector.tensor_tensor(S[:, 0:CKEYS].rearrange("p (b n) -> p b n", b=NB),
                                            m.ps[:, 0:4, :].rearrange("p a c -> p (a c)").rearrange("p (b n) -> p b n", b=NB),
                                            mask.unsqueeze(2).to_broadcast([P, NB, PAST]), ALU.add)
                    nc.vector.tensor_tensor(S[:, CKEYS:NS], m.ps[:, 4, 0:NB], mask, ALU.add).then_inc(s_masked, 1)
                    n = NS
                dve.wait_ge(s_masked, br + 1)
                nc.vector.tensor_reduce(stat[:, br:br + 1], S[:, 0:n], AX.X, ALU.max, negate=True).then_inc(s_max, 1)
                for q in range(ngroup[br]):
                    n_pt += 1
                    dve.wait_ge(s_pt, n_pt)
                    bank = 6 + (n_pt - 1) % 2
                    if br >= 1 and q == 0:
                        dve.wait_ge(s_pv, br)
                    if br == 0:
                        last = nc.vector.tensor_copy(PT[0:NB * SCMP, 0, :], m.ps[0:NB * SCMP, bank, 0:P])
                    elif q < 4:
                        last = nc.vector.tensor_copy(PT[:, 4 * q:4 * q + 4, :],
                                                     m.ps[:, bank, :].rearrange("p (a c) -> p a c", a=4))
                    else:
                        last = nc.vector.tensor_copy(PT[0:NB, NPG, :], m.ps[0:NB, bank, 0:P])
                    last.then_inc(s_ptk, 1)
                if br == 0:
                    dve.wait_ge(fw.s_gw, 16 * NH)
                dve.wait_ge(s_exp, br + 1)
                nc.vector.reciprocal(stat[:, 6 + br:7 + br], stat[:, 3 + br:4 + br]).then_inc(s_sc, 1)
                dve.wait_ge(s_sc, 2 * br + 1)
                nc.vector.tensor_tensor(stat[:, 9 + br:10 + br], stat[:, 6 + br:7 + br], m.gs[:, br:br + 1],
                                        ALU.mult).then_inc(s_sc, 1)
                dve.wait_ge(s_sc, 2 * br + 2)
                dve.wait_ge(s_pv, br + 1)
                nc.vector.tensor_scalar(O[:, br, :], m.ps[:, 5, 0:P], stat[:, 9 + br:10 + br], None,
                                        ALU.mult).then_inc(s_o, 1)
            dve.wait_ge(s_o, 3)
            nc.vector.tensor_tensor(O[:, 1, :], O[:, 1, :], O[:, 2, :], ALU.add).then_inc(s_o, 1)
            dve.wait_ge(s_o, 4)
            nc.vector.tensor_tensor(O[:, 0, :], O[:, 0, :], O[:, 1, :], ALU.add).then_inc(s_sum, 1)
            dve.wait_ge(s_oT, 1)
            for g in range(NKV):
                rows = slice(g * HD, (g + 1) * HD)
                nc.vector.tensor_copy(m.qT[rows, :, SEQ:NTOK],
                                      m.ps[rows, 6, g * HD:(g + 1) * HD].rearrange("p (h b) -> p h b", b=NB)).then_inc(s_oTk, 1)


def attend_prompt(nc, m):
    probs = [m.RW[:, 1024 + b * 1024:2048 + b * 1024] for b in range(2)]
    probsT = [view(m.RW, 3072 + b * 1024, 8, P) for b in range(2)]
    onat = [m.RW[:, 5120 + b * P:5248 + b * P] for b in range(2)]
    otmp = [m.RW[:, 5376 + b * 384:5760 + b * 384] for b in range(2)]
    identb, diag, edge = m.identb, m.mask_diag, m.mask_edge
    stat = m.small[:, 0:64].rearrange("p (b w) -> p b w", b=2)
    nmax = m.small[:, 64:76]

    s_q, s_qk, s_max, s_exp = m.sem("a_queries"), m.sem("a_scores"), m.sem("a_max"), m.sem("a_probs")
    s_t, s_tkv, s_tka, s_pv = m.sem("a_turned"), m.sem("a_kept_by_dve"), m.sem("a_kept_by_act"), m.sem("a_values")
    s_sc, s_tmp, s_o, s_oT, s_oTk = (m.sem(n) for n in ("a_scale", "a_scaled", "a_output", "a_oT", "a_oT_kept"))
    s_clamp, s_qh, s_kh, s_kl = (m.sem("a_" + n) for n in ("clamp_input", "q_high", "k_high", "k_low"))

    LO, HI = slice(0, HD), slice(HD, P)
    qs, ks, kcs = m.q_stacks, m.k_stacks, m.kc_stacks
    pieces = [[(m.kT[g * HD:(g + 1) * HD, 2 + a, 0:SEQ], ks[:, a, g])] for g in range(NKV) for a in range(2)]
    for g in range(NKV):
        pieces[2 * g + 1].append((m.kcT[g * HD:(g + 1) * HD, 0:NCMP], kcs[:, g, :, 0:NCMP]))

    jobs = [(i, g, kind) for i in range(TT) for g in range(NKV) for kind in "AB"]
    NJ = len(jobs)
    NMAX = sum(1 if kind == "A" else 2 for _, _, kind in jobs)

    def wblocks(i):
        return list(range(max(0, i - WBLK), i + 1))

    def blocks(job):
        i, g, kind = job
        if kind == "A":
            return [(b * P, P) for b in range(i + 1)]
        win = [(b * P, P) for b in range(len(wblocks(i)))]
        at = cmp_at(i)
        return win[:at] + [(cmp_col(i), NCMP)] + win[at:]

    def cmp_at(i):
        return min(len(wblocks(i)), 3)

    def cmp_col(i):
        return len(wblocks(i)) * P

    def key_blocks(job):
        return job[0] + 1 if job[2] == "A" else len(wblocks(job[0]))

    def first_column(job):
        return P if key_blocks(job) == 5 else 0

    def groups(job):
        bl = blocks(job)
        return [bl[a:a + 4] for a in range(0, len(bl), 4)]

    def nmaxes(job):
        return 1 if job[2] == "A" else 2

    NGRP = sum(len(groups(j)) for j in jobs)
    NGV = sum((len(groups(j)) + 1) // 2 for j in jobs)
    NGA = NGRP - NGV
    g_before = [sum(len(groups(j)) for j in jobs[:n]) for n in range(NJ + 1)]
    v_before = [sum((len(groups(j)) + 1) // 2 for j in jobs[:n]) for n in range(NJ + 1)]
    a_before = [g_before[n] - v_before[n] for n in range(NJ + 1)]
    m_before = [sum(nmaxes(j) for j in jobs[:n]) for n in range(NJ + 1)]
    kept_by = [("v" if q % 2 == 0 else "a") for j in jobs for q in range(len(groups(j)))]

    def keep_group(copy, n, q, grp, G):
        full = sum(1 for _, w in grp if w == P)
        last = None
        if full:
            last = copy(probsT[n % 2][:, 4 * q:4 * q + full, :],
                        m.ps[:, 4 + G % 2, 0:full * P].rearrange("p (a c) -> p a c", a=full))
        if full < len(grp):
            last = copy(probsT[n % 2][0:NCMP, 4 * q + full, :], m.ps[0:NCMP, 4 + G % 2, full * P:(full + 1) * P])
        return last

    def wait_from(eng, sem, base, value, first):
        if not (first and value <= 0):
            eng.wait_ge(sem, base + value)

    with nc.Block() as block:

        @block.gpsimd
        def _(pool):
            def high_queries(j, first):
                for i in range(TT):
                    if not first:
                        pool.wait_ge(s_qk, NJ * j + (4 * (i + 1) - NJ))
                    at, cols = bass.ds(j * NTOK + i * P, P), slice(i * P, (i + 1) * P)
                    nc.gpsimd.tensor_copy(qs[LO, 0, cols], m.RO[LO, at])
                    nc.gpsimd.tensor_copy(qs[HI, 1, cols], m.RO[HI, at]).then_inc(s_qh, 1)

            high_queries(0, True)
            with pool.Fori(1, QPK) as j:
                high_queries(j, False)

        @block.tensor
        def _(pe):
            def scores(n, j, first):
                i, g, kind = jobs[n]
                bank = 2 * (n % 2)

                def product(out, k, start=True):
                    for h in range(2):
                        nc.tensor.matmul(out, qs[:, g, i * P:(i + 1) * P], k[:, h], start=start and h == 0,
                                         stop=(h == 1), skip_group_check=True)

                if kind == "A" and g == 0:
                    pe.wait_ge(s_q, TT * j + (i + 1))
                if first and n < len(pieces):
                    pe.wait_ge(s_kh, n + 1)
                    pe.wait_ge(s_kl, n + 1)
                wait_from(pe, s_exp, NMAX * j, m_before[n - 1] if n >= 2 else m_before[NJ + n - 1] - NMAX, first)
                def mask(at, width, values):
                    return nc.tensor.matmul(m.ps[:, bank + at // 512, at % 512:at % 512 + width], identb[:], values,
                                            start=False, stop=True, skip_group_check=True)

                a, k0, at = (0, 0, first_column(jobs[n])) if kind == "A" else (1, wblocks(i)[0] * P, first_column(jobs[n]))
                end = at + key_blocks(jobs[n]) * P
                while at < end:
                    width = min(512 - at % 512, end - at)
                    product(m.ps[:, bank + at // 512, at % 512:at % 512 + width], ks[:, a, g, :, k0:k0 + width])
                    k0, at = k0 + width, at + width
                last = mask(end - P, P, diag[:])
                if kind == "B":
                    if len(wblocks(i)) > WBLK:
                        mask(first_column(jobs[n]), P, edge[:])
                    product(m.ps[:, bank + end // 512, end % 512:end % 512 + NCMP + 1], kcs[:, g], start=(end % 512 == 0))
                    at = 56 - 8 * i
                    last = mask(end, NCMP, m.mask_cmp[:, at:at + NCMP])
                last.then_inc(s_qk, 1)

            def turn(n, j, first):
                pe.wait_ge(s_exp, NMAX * j + m_before[n + 1])
                for q, grp in enumerate(groups(jobs[n])):
                    G = g_before[n] + q
                    H = G - 2
                    if H >= 0:
                        by, cnt = kept_by[H], sum(1 for x in kept_by[:H + 1] if x == kept_by[H])
                    else:
                        by = kept_by[H + NGRP]
                        cnt = sum(1 for x in kept_by[:H + NGRP + 1] if x == by) - (NGV if by == "v" else NGA)
                    wait_from(pe, s_tkv if by == "v" else s_tka, (NGV if by == "v" else NGA) * j, cnt, first)
                    for r, (col, w) in enumerate(grp):
                        last = nc.tensor.transpose(m.ps[0:w, 4 + G % 2, r * P:(r + 1) * P],
                                                   probs[n % 2][:, col:col + w], m.ident[:])
                    last.then_inc(s_t, 1)

            def values(n, j, first):
                i, g, kind = jobs[n]
                pe.wait_ge(s_tkv, NGV * j + v_before[n + 1])
                wait_from(pe, s_tka, NGA * j, a_before[n + 1], first)
                if g == 0 and kind == "A":
                    wait_from(pe, s_oTk, TT * j, i - 1, first)
                bank = 6 + i % 2
                gc = slice(g * HD, (g + 1) * HD)
                pT = probsT[n % 2]
                if kind == "A":
                    out = m.ps[:, bank, g * 192 + 64:g * 192 + 128]
                    for b in range(i + 1):
                        last = nc.tensor.matmul(out, pT[:, b, :], m.vv[:, b, g * HD:(g + 1) * HD],
                                                start=(b == 0), stop=(b == i), skip_group_check=True)
                else:
                    bl = wblocks(i)
                    out = m.ps[:, bank, g * 192 + 128:g * 192 + 192]
                    for r, b in enumerate(bl):
                        nc.tensor.matmul(out, pT[:, r + (r >= cmp_at(i)), :], m.vv[:, b, P + g * HD:P + (g + 1) * HD],
                                         start=(r == 0), stop=(r == len(bl) - 1), skip_group_check=True)
                    last = nc.tensor.matmul(m.ps[:, bank, g * 192:g * 192 + 64], pT[0:NCMP, cmp_at(i), :],
                                            m.vc[0:NCMP, 0, gc], start=True, stop=True, skip_group_check=True)
                last.then_inc(s_pv, 1)

            def turn_output(i, j, first):
                pe.wait_ge(s_o, TT * j + (i + 1))
                nc.tensor.transpose(m.ps[:, 6 + i % 2, 384:512], onat[i % 2], m.ident[:]).then_inc(s_oT, 1)

            def one_pass(j, first):
                scores(0, j, first)
                for n in range(NJ + 2):
                    if n + 1 < NJ:
                        scores(n + 1, j, first)
                    if n < NJ:
                        turn(n, j, first)
                    if 1 <= n <= NJ:
                        values(n - 1, j, first)
                    if n >= 2 and jobs[n - 2][1:] == (1, "B"):
                        turn_output(jobs[n - 2][0], j, first)

            one_pass(0, True)
            with pe.Fori(1, QPK) as j:
                one_pass(j, False)

        @block.vector
        def _(dve):
            def low_keys(n):
                dve.wait_ge(s_kh, n + 1)
                rows = slice(n // 2 * HD, (n // 2 + 1) * HD)
                for src, dst in pieces[n]:
                    for half in (LO, HI):
                        last = nc.vector.tensor_tensor(dst[half, 1], src, dst[rows, 0], ALU.subtract)
                last.then_inc(s_kl, 1)

            def job_max(n, j, first):
                i, g, kind = jobs[n]
                bank = 2 * (n % 2)
                if first and n + 1 < len(pieces):
                    low_keys(n + 1)
                dve.wait_ge(s_qk, NJ * j + (n + 1))
                sc = m.ps[:, bank:bank + 2, :].rearrange("p a c -> p (a c)")[:, first_column(jobs[n]):]
                col = 2 * (n % 2)
                nk = (i + 1) * P if kind == "A" else cmp_col(i)
                nc.vector.tensor_reduce(nmax[:, col:col + 1], sc[:, 0:nk], AX.X, ALU.max, negate=True).then_inc(s_max, 1)
                if kind == "B":
                    dst = nmax[:, 4:5] if i == 0 else nmax[:, col + 1:col + 2]
                    red = nc.vector.tensor_reduce(dst, sc[:, nk:nk + NCMP], AX.X, ALU.max, negate=True)
                    if i > 0:
                        red.then_inc(s_max, 1)
                    else:
                        red.then_inc(s_clamp, 1)
                        dve.wait_ge(s_clamp, NKV * j + (g + 1))
                        nc.vector.tensor_scalar(nmax[:, col + 1:col + 2], nmax[:, 4:5], 1e29, None,
                                                ALU.min).then_inc(s_max, 1)

            def keep(n, j, first):
                for q, grp in enumerate(groups(jobs[n])):
                    if q % 2 == 0:
                        G = g_before[n] + q
                        dve.wait_ge(s_t, NGRP * j + (G + 1))
                        if n >= 2 or not first:
                            dve.wait_ge(s_pv, NJ * j + (n - 1))
                        keep_group(nc.vector.tensor_copy, n, q, grp, G).then_inc(s_tkv, 1)

            def finish(i, j, first):
                b = i % 2
                sums, rec, scl = stat[:, b, 0:6], stat[:, b, 8:14], stat[:, b, 16:22]
                dve.wait_ge(s_exp, NMAX * j + m_before[4 * i + 4])
                if i == 0:
                    nc.vector.tensor_scalar(sums, sums, 1e-30, None, ALU.max).then_inc(s_sc, 1)
                    dve.wait_ge(s_sc, 17 * j + 1)
                nc.vector.reciprocal(rec, sums).then_inc(s_sc, 1)
                dve.wait_ge(s_sc, 17 * j + (2 * i + 2))
                gate = m.gates[:, i, :].rearrange("p (g x) -> p g x", g=NKV)[:, :, bass.ds(3 * j, 3)]
                nc.vector.tensor_tensor(scl.rearrange("p (g x) -> p g x", g=NKV), rec.rearrange("p (g x) -> p g x", g=NKV),
                                        gate, ALU.mult).then_inc(s_sc, 1)
                dve.wait_ge(s_sc, 17 * j + (2 * i + 3))
                dve.wait_ge(s_pv, NJ * j + (4 * i + 4))
                nc.vector.tensor_tensor(otmp[b].rearrange("p (x d) -> p x d", d=HD),
                                        m.ps[:, 6 + b, 0:384].rearrange("p (x d) -> p x d", d=HD),
                                        scl.unsqueeze(2).to_broadcast([P, 6, HD]), ALU.mult).then_inc(s_tmp, 1)
                dve.wait_ge(s_tmp, TT * j + (i + 1))
                nc.vector.tensor_reduce(onat[b].rearrange("p (g d) -> p g d", g=NKV),
                                        otmp[b].rearrange("p (g x d) -> p g d x", g=NKV, x=3), AX.X, ALU.add).then_inc(s_o, 1)

            def low_queries(i, j):
                at, cols = bass.ds(j * NTOK + i * P, P), slice(i * P, (i + 1) * P)
                dve.wait_ge(s_qh, TT * j + (i + 1))
                nc.vector.tensor_tensor(qs[HI, 0, cols], m.RO[LO, at], qs[LO, 0, cols], ALU.subtract)
                nc.vector.tensor_tensor(qs[LO, 1, cols], m.RO[HI, at], qs[HI, 1, cols], ALU.subtract).then_inc(s_q, 1)

            def keep_output(i, j, first):
                dve.wait_ge(s_oT, TT * j + (i + 1))
                nc.vector.tensor_scalar(m.RO[:, bass.ds(j * NTOK + i * P, P)], m.ps[:, 6 + i % 2, 384:512],
                                        1.0, None, ALU.mult).then_inc(s_oTk, 1)

            def one_pass(j, first):
                low_queries(0, j)
                if first:
                    low_keys(0)
                job_max(0, j, first)
                for n in range(NJ + 2):
                    if n % 4 == 2 and n // 4 + 1 < TT:
                        low_queries(n // 4 + 1, j)
                    if n + 1 < NJ:
                        job_max(n + 1, j, first)
                    if n < NJ:
                        keep(n, j, first)
                    if 1 <= n <= NJ and jobs[n - 1][1:] == (1, "B"):
                        finish(jobs[n - 1][0], j, first)
                    if n >= 2 and jobs[n - 2][1:] == (1, "B"):
                        keep_output(jobs[n - 2][0], j, first)

            nc.vector.memset(kcs[:, :, :, NCMP:NCMP + 1].bitcast(F32), 0.0)
            one_pass(0, True)
            with dve.Fori(1, QPK) as j:
                one_pass(j, False)

        @block.scalar
        def _(act):
            def high_keys(n):
                for src, dst in pieces[n]:
                    for half in (LO, HI):
                        last = nc.scalar.copy(dst[half, 0], src)
                last.then_inc(s_kh, 1)

            def exps(n, j, first):
                i, g, kind = jobs[n]
                if first and n + 1 < len(pieces):
                    high_keys(n + 1)
                bank, col = 2 * (n % 2), 2 * (n % 2)
                sc = m.ps[:, bank:bank + 2, :].rearrange("p a c -> p (a c)")[:, first_column(jobs[n]):]
                if n >= 2 or not first:
                    act.wait_ge(s_t, NGRP * j + (g_before[n - 1] if n >= 2 else g_before[NJ + n - 1] - NGRP))
                if kind == "A" and g == 0 and (i >= 2 or not first):
                    act.wait_ge(s_sc, 17 * j + (2 * (i - 2) + 2 if i >= 2 else 2 * (i + 6) + 2 - 17))
                nk = (i + 1) * P if kind == "A" else cmp_col(i)
                branch = 1 if kind == "A" else 2
                act.wait_ge(s_max, NMAX * j + m_before[n + 1])
                nc.scalar.activation(probs[n % 2][:, 0:nk], sc[:, 0:nk], ACT.Exp, bias=nmax[:, col:col + 1],
                                     accum_out=stat[:, i % 2, 3 * g + branch:3 * g + branch + 1]).then_inc(s_exp, 1)
                if kind == "B":
                    nc.scalar.activation(probs[n % 2][:, nk:nk + NCMP], sc[:, nk:nk + NCMP], ACT.Exp,
                                         bias=nmax[:, col + 1:col + 2],
                                         accum_out=stat[:, i % 2, 3 * g:3 * g + 1]).then_inc(s_exp, 1)

            def keep(n, j, first):
                for q, grp in enumerate(groups(jobs[n])):
                    if q % 2 == 1:
                        G = g_before[n] + q
                        act.wait_ge(s_t, NGRP * j + (G + 1))
                        if n >= 2 or not first:
                            act.wait_ge(s_pv, NJ * j + (n - 1))
                        keep_group(nc.scalar.copy, n, q, grp, G).then_inc(s_tka, 1)

            def one_pass(j, first):
                if first:
                    high_keys(0)
                exps(0, j, first)
                for n in range(NJ):
                    if n + 1 < NJ:
                        exps(n + 1, j, first)
                    keep(n, j, first)

            one_pass(0, True)
            with act.Fori(1, QPK) as j:
                one_pass(j, False)


def normalise(nc, dve, x, n, stats, mv, rstd, gain, bias, s_stat, s_mv, s_rstd, s_norm, t, done):
    nc.vector.bn_stats(stats[0:n, 0:6], x[:, 0:512])
    nc.vector.bn_stats(stats[0:n, 6:12], x[:, 512:1024]).then_inc(s_stat, 1)
    dve.wait_ge(s_stat, t + 1)
    nc.vector.bn_aggr(mv[0:n], stats[0:n, 0:12]).then_inc(s_mv, 1)
    dve.wait_ge(s_rstd, t + 1)
    nc.vector.tensor_scalar(x, x, mv[0:n, 0:1], rstd[0:n], ALU.subtract, ALU.mult).then_inc(s_norm, 1)
    dve.wait_ge(s_norm, 2 * t + 1)
    nc.vector.tensor_tensor(x, x, gain[0:n], ALU.mult).then_inc(s_norm, 1)
    dve.wait_ge(s_norm, 2 * t + 2)
    nc.vector.tensor_tensor(x, x, bias[0:n], ALU.add).then_inc(done, 1)


def inverse_deviation(nc, m, pool, n, mv, rstd, s_mv, s_eps, s_rstd, t):
    pool.wait_ge(s_mv, t + 1)
    nc.gpsimd.tensor_scalar(rstd[0:n], mv[0:n, 1:2], EPS, None, ALU.add).then_inc(s_eps, 1)
    pool.wait_ge(s_eps, t + 1)
    nc.gpsimd.tensor_tensor(rstd[0:n], rstd[0:n], m.mhalf[0:n], ALU.pow).then_inc(s_rstd, 1)


def gmlp_values(nc, m, io, fw):
    wv = view(m.RW, 0, 2 * KT, 512)
    vn = [m.RK[:, t * DM:(t + 1) * DM] for t in range(TT)] + [m.RW[0:NB, 8192:9216]]
    gain, bias = m.RW[:, 9216:10240], m.RW[:, 10240:11264]
    wsT = view(m.RW, 11264, 8, P)
    bs = view(m.RW, 12288, 8, P)
    ws = view(m.RW, 13312, 8, P)
    stats, mv, rstd = m.small[:, 0:12], m.small[:, 12:14], m.small[:, 14:15]
    w00 = m.small[0:NB, 16:24]
    first = m.small[0:NB, 24:88].rearrange("p (g b) -> p g b", g=8)
    s_w = [m.sem(f"v_w{i}") for i in range(4)]
    s_c, s_wsT, s_wsk, s_ws = (m.sem(n) for n in ("v_consts", "ws_turned", "ws_kept", "ws_masked"))
    s_proj, s_gelu, s_stat, s_mv, s_eps = (m.sem(n) for n in ("v_projected", "v_gelu", "v_stats", "v_moments", "v_eps"))
    s_rstd, s_norm, s_v, s_mix, s_kept = (m.sem(n) for n in ("v_rstd", "v_scaling", "v_normal", "v_mixed", "v_mixed_kept"))
    s_first, s_out = m.sem("ws_first"), m.sem("v_sample_out")
    w_in = io["w_in"].rearrange("l (k p) n -> p (l k) n", p=P)
    with nc.Block() as block:

        @block.sync
        def _(sp):
            for c in range(2):
                for h in range(2):
                    k0, k1 = h * KT // 2, (h + 1) * KT // 2
                    sp.dma_start(wv[:, c * KT + k0:c * KT + k1, :],
                                 w_in[:, k0:k1, COL_V + c * 512:COL_V + (c + 1) * 512]).then_inc(s_w[2 * c + h], 16)
            sp.dma_start(ws, io["gmlp_ws"].rearrange("l g t s -> t (l g) s")).then_inc(s_c, 16)
            sp.dma_start(gain, io["gmlp_ln_g"].rearrange("l d -> (l d)").partition_broadcast(P)).then_inc(s_c, 16)
            sp.dma_start(bias, io["gmlp_ln_b"].rearrange("l d -> (l d)").partition_broadcast(P)).then_inc(s_c, 16)
            sp.dma_start(bs.rearrange("p g t -> p (g t)"),
                         io["gmlp_bs"].rearrange("l g t -> (l g t)").partition_broadcast(P)).then_inc(s_c, 16)
            with nc.allow_non_contiguous_dma(reason="one weight per group"):
                sp.dma_start(w00.unsqueeze(2), io["gmlp_ws"][0, :, 0, 0:1].partition_broadcast(NB)).then_inc(s_c, 16)
            for b in range(2):
                fw.load_u(sp, 0, b)
            sp.wait_ge(s_v, NT9)
            sp.dma_start(io["gmlp_v_sample"].rearrange("b l t d -> (b l t) d"), vn[TT]).then_inc(s_out, 16)
            sp.wait_ge(s_out, 16)

        @block.gpsimd
        def _(pool):
            pool.wait_ge(s_wsk, 1)
            nc.gpsimd.affine_select(out=wsT, in_=wsT, compare_op=ALU.is_ge, fill=0.0, base=0,
                                    pattern=[[0, 8], [1, P]], channel_multiplier=-1).then_inc(s_ws, 1)
            for t in range(NT9):
                inverse_deviation(nc, m, pool, rows_of(t), mv, rstd, s_mv, s_eps, s_rstd, t)

        @block.tensor
        def _(pe):
            def turn_ws():
                pe.wait_ge(s_c, 80)
                for g in range(8):
                    last = nc.tensor.transpose(m.ps[:, 4 + g // 4, (g % 4) * P:(g % 4 + 1) * P], ws[:, g, :], m.ident[:])
                last.then_inc(s_wsT, 1)

            def mix(t):
                n, bank = rows_of(t), 4 + 2 * (t % 2)
                pe.wait_ge(s_v, t + 1)
                if t == 0:
                    pe.wait_ge(s_ws, 1)
                if t == TT:
                    pe.wait_ge(s_first, 1)
                if t >= 2:
                    pe.wait_ge(s_kept, t - 1)
                for g in range(8):
                    out = m.ps[:, bank + g // 4, (g % 4) * P:(g % 4) * P + n]
                    rhs = wsT[:, g, :] if t < TT else first[:, g, :]
                    last = nc.tensor.matmul(out, vn[t][:, g * P:(g + 1) * P], rhs, start=True, stop=True)
                last.then_inc(s_mix, 1)

            for t in range(NT9):
                n = rows_of(t)
                if t >= 2:
                    pe.wait_ge(s_gelu, t - 1)
                for c in range(2):
                    for k in range(KT):
                        if t == 0 and k % (KT // 2) == 0:
                            pe.wait_ge(s_w[2 * c + k // (KT // 2)], 16)
                        last = nc.tensor.matmul(m.ps[0:n, 2 * (t % 2) + c, :], m.xT[:, k, span(t)],
                                                wv[:, c * KT + k, :], start=(k == 0), stop=(k == KT - 1))
                last.then_inc(s_proj, 1)
                if t == 0:
                    turn_ws()
                if t >= 1:
                    mix(t - 1)
            mix(TT)

        @block.scalar
        def _(act):
            for t in range(NT9):
                n, b = rows_of(t), t % 2
                act.wait_ge(s_proj, t + 1)
                nc.scalar.activation(vn[t].rearrange("p (a c) -> p a c", a=2), m.ps[0:n, 2 * b:2 * b + 2, :],
                                     ACT.Gelu_apprx_tanh).then_inc(s_gelu, 1)

        @block.vector
        def _(dve):
            dve.wait_ge(s_wsT, 1)
            nc.vector.tensor_copy(wsT.rearrange("p (a c) t -> p a (c t)", a=2), m.ps[:, 4:6, :]).then_inc(s_wsk, 1)
            dve.wait_ge(s_c, 80)
            nc.vector.tensor_tensor(first, m.ident[0:NB, 0:NB].unsqueeze(1).to_broadcast([NB, 8, NB]),
                                    w00.unsqueeze(2).to_broadcast([NB, 8, NB]), ALU.mult).then_inc(s_first, 1)

            def keep(t):
                n, bank = rows_of(t), 4 + 2 * (t % 2)
                dve.wait_ge(s_mix, t + 1)
                src = m.ps[:, bank:bank + 2, :].rearrange("p a (g c) -> p (a g) c", g=4)[:, :, 0:n]
                add = bs if t < TT else bs[:, :, 0:1].to_broadcast([P, 8, NB])
                nc.vector.tensor_tensor(m.aT[:, :, span(t)], src, add, ALU.add).then_inc(s_kept, 1)

            for t in range(NT9):
                dve.wait_ge(s_gelu, t + 1)
                normalise(nc, dve, vn[t], rows_of(t), stats, mv, rstd, gain, bias,
                          s_stat, s_mv, s_rstd, s_norm, t, s_v)
                if t >= 1:
                    keep(t - 1)
            keep(TT)


def gmlp_gate(nc, m, io, fw):
    wu, s_w = fw.u, fw.s_u
    ug = [m.RW[:, 12256 + b * NTOK:12256 + (b + 1) * NTOK] for b in range(2)]
    s_proj, s_gelu, s_a = m.sem("u_projected"), m.sem("u_gelu"), m.sem("a_ready")
    with nc.Block() as block:

        @block.sync
        def _(sp):
            for b in range(2):
                load_merge(m, io, fw, sp, b * P, b)
            with sp.Fori(1, KT // 2) as jj:
                for b in range(2):
                    sp.wait_ge(s_proj, 2 * jj + (b - 1))
                    fw.load_u(sp, jj, b)

        @block.tensor
        def _(pe):
            def tile(b, jj=None):
                pe.wait_ge(s_w[b], 16 if jj is None else 16 * jj + 16)
                if jj is not None:
                    pe.wait_ge(s_gelu, 2 * jj + (b - 1))
                for c in range(NC3):
                    cols = slice(c * CW, (c + 1) * CW)
                    for k in range(KT):
                        last = nc.tensor.matmul(m.ps[:, 3 * b + c, 0:CW], wu[b][:, k, :],
                                                m.xT[:, k, cols], start=(k == 0), stop=(k == KT - 1))
                last.then_inc(s_proj, 1)

            for b in range(2):
                tile(b)
            with pe.Fori(1, KT // 2) as jj:
                for b in range(2):
                    tile(b, jj)

        @block.scalar
        def _(act):
            def tile(b, jj=None):
                act.wait_ge(s_proj, b + 1 if jj is None else 2 * jj + (b + 1))
                if jj is not None:
                    act.wait_ge(s_a, 2 * jj + (b - 1))
                nc.scalar.activation(ug[b].rearrange("p (a c) -> p a c", a=NC3), m.ps[:, 3 * b:3 * b + 3, 0:CW],
                                     ACT.Gelu_apprx_tanh).then_inc(s_gelu, 1)

            for b in range(2):
                tile(b)
            with act.Fori(1, KT // 2) as jj:
                for b in range(2):
                    tile(b, jj)

        @block.vector
        def _(dve):
            with dve.Fori(0, KT // 2) as jj:
                for b in range(2):
                    dve.wait_ge(s_gelu, 2 * jj + (b + 1))
                    at = m.RA[:, bass.ds((2 * jj + b) * NTOK, NTOK)]
                    nc.vector.tensor_tensor(at, at, ug[b], ALU.mult).then_inc(s_a, 1)


def merge_weights(m, b):
    return m.RW[:, b * 4096:(b + 1) * 4096].rearrange("p (q k c) -> p q k c", q=4, k=KT)


def load_merge(m, io, fw, sp, col, b):
    w, done = merge_weights(m, b), fw.s_merge[b]
    w_a = io["w_branch_a"].rearrange("l (k p) n -> p (l k) n", p=P)
    w_b = io["w_branch_b"].rearrange("l (g k d) n -> g d (l k) n", g=NKV, d=HD)
    sp.dma_start(w[:, 0], fw.w_in[:, :, bass.ds(col + COL_GA, P)]).then_inc(done, 16)
    sp.dma_start(w[:, 1], fw.w_in[:, :, bass.ds(col + COL_GB, P)]).then_inc(done, 16)
    sp.dma_start(w[:, 2], w_a[:, :, bass.ds(col, P)]).then_inc(done, 16)
    for g in range(NKV):
        sp.dma_start(w[g * HD:(g + 1) * HD, 3], w_b[g, :, :, bass.ds(col, P)]).then_inc(done, 16)


def merge(nc, m, io, fw):
    w, s_w = [merge_weights(m, b) for b in range(2)], fw.s_merge
    wout = view(m.RW, 8192, KT, DM)
    sa, sb = m.small[:, 0:512], m.small[:, 512:1024]
    s_out = m.sem_wout
    s_mm, s_sig, s_mul, s_y = m.sem("m_products"), m.sem("m_sigmoid"), m.sem("m_gated"), m.sem("m_merged")
    NS = NC3

    def columns(c):
        return slice(c * CW, (c + 1) * CW)

    with nc.Block() as block:

        @block.sync
        def _(sp):
            sp.dma_start(wout, io["w_out"].rearrange("l (k p) n -> p (l k) n", p=P)).then_inc(s_out, 16)
            with sp.Fori(1, KT // 2) as jj:
                for b in range(2):
                    sp.wait_ge(s_mm, NS * 2 * jj + NS * (b - 1))
                    load_merge(m, io, fw, sp, 2 * P * jj + b * P, b)

        @block.tensor
        def _(pe):
            def tile(b, jj=None):
                pe.wait_ge(s_w[b], 80 if jj is None else 80 * jj + 80)
                for c in range(NS):
                    step = NS * b + c
                    half = step % 2
                    if jj is not None or step >= 2:
                        pe.wait_ge(s_mul, step - 1 if jj is None else 2 * NS * jj + (step - 1))
                    n = columns(c).stop - columns(c).start
                    for q, src in enumerate((m.xT, m.xT, m.aT, m.qT)):
                        for k in range(KT):
                            last = nc.tensor.matmul(m.ps[:, 4 * half + q, 0:n], w[b][:, q, k, :], src[:, k, columns(c)],
                                                    start=(k == 0), stop=(k == KT - 1))
                    last.then_inc(s_mm, 1)

            for b in range(2):
                tile(b)
            with pe.Fori(1, KT // 2) as jj:
                for b in range(2):
                    tile(b, jj)

        def step_of(jj, b, c):
            return 2 * NS * jj + (NS * b + c)

        @block.scalar
        def _(act):
            def tile(b, jj, first):
                for c in range(NS):
                    half, n = (NS * b + c) % 2, columns(c).stop - columns(c).start
                    act.wait_ge(s_mm, step_of(jj, b, c) + 1)
                    if not (first and b == 0 and c == 0):
                        act.wait_ge(s_y, step_of(jj, b, c))
                    nc.scalar.activation(sa[:, 0:n], m.ps[:, 4 * half, 0:n], ACT.Sigmoid)
                    nc.scalar.activation(sb[:, 0:n], m.ps[:, 4 * half + 1, 0:n], ACT.Sigmoid).then_inc(s_sig, 1)

            for b in range(2):
                tile(b, 0, True)
            with act.Fori(1, KT // 2) as jj:
                for b in range(2):
                    tile(b, jj, False)

        @block.vector
        def _(dve):
            with dve.Fori(0, KT // 2) as jj:
                for b in range(2):
                    for c in range(NS):
                        half, n = (NS * b + c) % 2, columns(c).stop - columns(c).start
                        dve.wait_ge(s_sig, step_of(jj, b, c) + 1)
                        nc.vector.tensor_tensor(sa[:, 0:n], sa[:, 0:n], m.ps[:, 4 * half + 2, 0:n], ALU.mult)
                        nc.vector.tensor_tensor(sb[:, 0:n], sb[:, 0:n], m.ps[:, 4 * half + 3, 0:n], ALU.mult).then_inc(s_mul, 1)
                        dve.wait_ge(s_mul, step_of(jj, b, c) + 1)
                        at = (2 * jj + b) * NTOK + c * CW
                        nc.vector.tensor_tensor(m.RK[:, bass.ds(at, n)], sa[:, 0:n], sb[:, 0:n], ALU.add).then_inc(s_y, 1)


def output_and_router(nc, m, io):
    yT = view(m.RK, 0, KT, NTOK)
    wout = view(m.RW, 8192, KT, DM)
    x1 = m.x1
    base = 20480
    wparts = m.wo_parts.rearrange("p (h k c) -> p h k c", h=2, k=KT)
    yparts = m.y_parts.rearrange("p (b h k c) -> p b h k c", b=2, h=2, k=KT)
    PASSES = ((0, 0), (0, 1), (1, 0))
    gain, bias = m.R3[:, base:base + DM], m.R3[:, base + DM:base + 2 * DM]
    x1T = view(m.R3, base + 2 * DM, KT, P)
    wr = m.R3[:, base + 3 * DM:base + 3 * DM + KT * NE].rearrange("p (k e) -> p k e", k=KT)
    sc = m.R3[:, base + 3 * DM + 128:base + 3 * DM + 160]
    stats, mv, rstd = sc[:, 0:12], sc[:, 12:14], sc[:, 14:15]
    aff = m.aff
    s_spill = m.sem("o_x1_out")
    s_wh, s_wl, s_yh, s_yl = (m.sem("o_" + n) for n in ("w_high", "w_low", "y_high", "y_low"))
    s_x, s_c, s_mm, s_z = [m.sem(f"o_x{b}") for b in range(3)], m.sem("o_consts"), m.sem("o_products"), m.sem("o_residual")
    s_stat, s_mv, s_eps, s_rstd, s_norm = (m.sem("o_" + n) for n in ("stats", "moments", "eps", "rstd", "scaling"))
    s_x1, s_t, s_tk, s_r, s_aff, s_a0 = (m.sem("o_" + n) for n in ("x1_ready", "turned", "turned_kept", "routed", "affinity", "clear"))
    xp = io["x_prompt"].rearrange("a (t p) d -> p (a t) d", p=P)
    with nc.Block() as block:

        @block.sync
        def _(sp):
            sp.dma_start(gain, io["ln1_g"].rearrange("l d -> (l d)").partition_broadcast(P)).then_inc(s_c, 16)
            sp.dma_start(bias, io["ln1_b"].rearrange("l d -> (l d)").partition_broadcast(P)).then_inc(s_c, 16)
            sp.dma_start(wr, io["w_router"].rearrange("(k p) e -> p k e", p=P)).then_inc(s_c, 16)
            for t in range(NT9):
                if t >= 3:
                    sp.wait_ge(s_x[t % 3], 16 * (t // 3))
                src = xp[:, t, :] if t < TT else io["x_sample"].rearrange("b t d -> (b t) d")
                sp.dma_start(x1[t], src).then_inc(s_x[t % 3], 16)
            for t in range(TT):
                sp.wait_ge(s_x1, t + 1)
                sp.dma_start(m.x1_dram[t * P:(t + 1) * P, :], x1[t]).then_inc(s_spill, 16)
            sp.wait_ge(s_spill, 16 * TT)

        @block.gpsimd
        def _(pool):
            def high_y(t):
                if t >= 2:
                    pool.wait_ge(s_mm, t - 1)
                nc.gpsimd.tensor_copy(yparts[:, t % 2, 0, :, 0:rows_of(t)], yT[:, :, span(t)]).then_inc(s_yh, 1)

            high_y(0)
            high_y(1)
            nc.gpsimd.memset(aff[:, TT, :], 0.0).then_inc(s_a0, 1)
            for t in range(NT9):
                if t + 2 < NT9:
                    high_y(t + 2)
                inverse_deviation(nc, m, pool, rows_of(t), mv, rstd, s_mv, s_eps, s_rstd, t)

        @block.tensor
        def _(pe):
            def turn(t):
                n = rows_of(t)
                pe.wait_ge(s_x1, t + 1)
                if t >= 1:
                    pe.wait_ge(s_tk, t)
                for k in range(KT):
                    last = nc.tensor.transpose(m.ps[:, 4 + k // 4, (k % 4) * P:(k % 4) * P + n],
                                               x1[t][:, k * P:(k + 1) * P], m.ident[0:n, 0:n])
                last.then_inc(s_t, 1)

            def route(t):
                n = rows_of(t)
                pe.wait_ge(s_tk, t + 1)
                if t >= 2:
                    pe.wait_ge(s_aff, t - 1)
                for k in range(KT):
                    last = nc.tensor.matmul(m.ps[0:n, 6 + t % 2, 0:NE], x1T[:, k, 0:n], wr[:, k, :],
                                            start=(k == 0), stop=(k == KT - 1))
                last.then_inc(s_r, 1)

            for t in range(NT9):
                n = rows_of(t)
                if t >= 2:
                    pe.wait_ge(s_z, t - 1)
                pe.wait_ge(s_yl, t + 1)
                for k in range(KT):
                    if t == 0:
                        pe.wait_ge(s_wl, k + 1)
                    for c in range(2):
                        for i, (a, b) in enumerate(PASSES):
                            last = nc.tensor.matmul(m.ps[0:n, 2 * (t % 2) + c, :], yparts[:, t % 2, a, k, 0:n],
                                                    wparts[:, b, k, c * 512:(c + 1) * 512],
                                                    start=(k == 0 and i == 0), stop=(k == KT - 1 and i == 2))
                last.then_inc(s_mm, 1)
                if t == 2:
                    pe.wait_ge(s_c, 48)
                if t >= 2:
                    route(t - 2)
                if t >= 1:
                    turn(t - 1)
            route(TT - 1)
            turn(TT)
            route(TT)

        @block.scalar
        def _(act):
            act.wait_ge(m.sem_wout, 16)
            for k in range(KT):
                nc.scalar.copy(wparts[:, 0, k, :], wout[:, k, :]).then_inc(s_wh, 1)
            for t in range(NT9):
                n = rows_of(t)
                act.wait_ge(s_t, t + 1)
                if t >= 1:
                    act.wait_ge(s_r, t)
                src = m.ps[:, 4:6, :].rearrange("p a (k c) -> p (a k) c", k=4)[:, :, 0:n]
                nc.scalar.copy(x1T[:, :, 0:n], src).then_inc(s_tk, 1)
                act.wait_ge(s_r, t + 1)
                if t == TT:
                    act.wait_ge(s_a0, 1)
                nc.scalar.activation(aff[0:n, t, :], m.ps[0:n, 6 + t % 2, 0:NE], ACT.Sigmoid).then_inc(s_aff, 1)

        @block.vector
        def _(dve):
            def low_y(t):
                dve.wait_ge(s_yh, t + 1)
                part = yparts[:, t % 2, :, :, 0:rows_of(t)]
                nc.vector.tensor_tensor(part[:, 1], yT[:, :, span(t)], part[:, 0], ALU.subtract).then_inc(s_yl, 1)

            low_y(0)
            for k in range(KT):
                dve.wait_ge(s_wh, k + 1)
                nc.vector.tensor_tensor(wparts[:, 1, k, :], wout[:, k, :], wparts[:, 0, k, :], ALU.subtract).then_inc(s_wl, 1)
            low_y(1)
            dve.wait_ge(s_c, 48)
            for t in range(NT9):
                n, b = rows_of(t), t % 2
                dve.wait_ge(s_mm, t + 1)
                if t + 2 < NT9:
                    low_y(t + 2)
                dve.wait_ge(s_x[t % 3], 16 * (t // 3 + 1))
                src = m.ps[0:n, 2 * b:2 * b + 2, :].rearrange("p a c -> p (a c)")
                nc.vector.scalar_tensor_tensor(out=x1[t], in0=x1[t], scalar=ALPHA, in1=src, op0=ALU.mult,
                                               op1=ALU.add).then_inc(s_z, 1)
                dve.wait_ge(s_z, t + 1)
                normalise(nc, dve, x1[t], n, stats, mv, rstd, gain, bias, s_stat, s_mv, s_rstd, s_norm, t, s_x1)


GATE, UP, DOWN = range(3)


def raw_third(m, q):
    return (m.RK[:, 0:4096], m.RK[:, 4096:8192], m.RW[:, 0:4096])[q]


def load_third(m, io, sp, q, e):
    w = (io["w_gate"], io["w_up"], io["w_down"])[q].rearrange("l e (p k) f -> p (l e) (k f)", p=P)
    sp.dma_start(raw_third(m, q), w[:, bass.ds(e, 1), :].rearrange("p o c -> p (o c)")).then_inc(
        (m.sem_gate, m.sem_up, m.sem_down)[q], 16)


def route_and_dispatch(nc, m, io):
    NQ = NT9 * NE
    cursor = [0]

    def take(n):
        a = m.RW[:, 8192 + cursor[0]:8192 + cursor[0] + n]
        cursor[0] += n
        return a

    def te(x):
        return x.rearrange("p (t e) -> p t e", e=NE)

    aff = m.aff.rearrange("p t e -> p (t e)")
    br, w4, w16 = take(NE), take(4), take(NE)
    kk, tau = take(NKX), take(NSTEP)
    ones, before = take(P), take(P)
    rowmask = take(1)
    grp, vm, oh1, oh2, tmp, eqw = (take(NQ) for _ in range(6))
    M = take(NQ)
    a_, b_, c_, d_ = (take(NT9 * NG) for _ in range(4))
    gs_, goh = take(NT9 * NG), take(NT9 * NG)
    mx, mm = take(NT9), take(NT9)
    a12 = take(2 * NT9)
    tot, tb, pos = take(NQ), take(NQ), take(NQ)
    cnt, off, nt, T, Tex, tq = (take(NE) for _ in range(6))
    big1, big2 = take(NSTEP * NE), take(NSTEP * NE)
    sumb = take(NSTEP)
    slotf = take(2 * NT9)
    tabf = take(3 * NSTEP + 2)
    zeros = take(DM)
    assert cursor[0] <= 8192
    s_b, s_c0, s_c, s_v, s_m, s_cnt = (m.sem("r_" + n) for n in ("bias", "clear", "consts", "step", "chosen", "counted"))
    s_slot, s_send = m.sem("r_slots"), m.sem("r_rows_sent")
    with nc.Block() as block:

        @block.sync
        def _(sp):
            sp.dma_start(br, io["b_router"].partition_broadcast(P)).then_inc(s_b, 16)
            load_third(m, io, sp, GATE, 0)
            load_third(m, io, sp, UP, 0)
            sp.wait_ge(m.sem_gate, 16)
            sp.wait_ge(m.sem_up, 16)

        @block.gpsimd
        def _(pool):
            flt = dict(allow_small_or_imprecise_dtypes=True)
            nc.gpsimd.iota(w4, [[-1, 4]], base=4, channel_multiplier=0, **flt)
            nc.gpsimd.iota(w16, [[-1, NE]], base=NE, channel_multiplier=0, **flt)
            nc.gpsimd.iota(kk, [[P, NKX]], base=0, channel_multiplier=0, **flt)
            nc.gpsimd.iota(tau, [[1, NSTEP]], base=0, channel_multiplier=0, **flt)
            nc.gpsimd.memset(ones, 1.0)
            nc.gpsimd.memset(zeros, 0.0)
            nc.gpsimd.memset(before, 1.0)
            nc.gpsimd.memset(rowmask, 1.0).then_inc(s_c0, 1)
            pool.wait_ge(s_c0, 1)
            nc.gpsimd.affine_select(out=before, in_=before, compare_op=ALU.is_gt, fill=0.0, base=0,
                                    pattern=[[1, P]], channel_multiplier=-1)
            nc.gpsimd.affine_select(out=rowmask, in_=rowmask, compare_op=ALU.is_gt, fill=0.0, base=NB,
                                    pattern=[[0, 1]], channel_multiplier=-1).then_inc(s_c, 1)
            pool.wait_ge(s_c, 1)
            nc.gpsimd.dma_start(m.xs_dram[NPAIR:NROWS, :], zeros).then_inc(m.sem_stored, 16)
            pool.wait_ge(s_slot, 1)
            for t in range(NT9):
                for c in range(2):
                    n = rows_of(t)
                    col = t * 2 + c
                    nc.gpsimd.indirect_dma_start(
                        out=m.xs_dram, out_offset=bass.IndirectOffsetOnAxis(ap=m.slots[0:n, col:col + 1], axis=0),
                        in_=m.x1[t], in_offset=None).then_inc(s_send, 16)
            pool.wait_ge(s_send, 16 * 2 * NT9)
            pool.wait_ge(m.sem_stored, 16)

        @block.tensor
        def _(pe):
            pe.wait_ge(s_m, 1)
            pe.wait_ge(s_c, 1)
            nc.tensor.matmul(m.ps[:, 0, 0:NQ], before, M, start=True, stop=True)
            nc.tensor.matmul(m.ps[:, 1, 0:NQ], ones, M, start=True, stop=True).then_inc(s_cnt, 1)

        @block.vector
        def _(dve):
            steps = [0]

            def step(ins):
                steps[0] += 1
                ins.then_inc(s_v, 1)
                dve.wait_ge(s_v, steps[0])

            tt, ts, red = nc.vector.tensor_tensor, nc.vector.tensor_scalar, nc.vector.tensor_reduce

            def bc(x, shape):
                return x.to_broadcast(shape)

            def first_best(v, n, groups, width, weights, out):
                v3 = v.rearrange("p (a b) -> p a b", b=width)
                o3 = out.rearrange("p (a b) -> p a b", b=width)
                t3 = eqw[:, 0:n].rearrange("p (a b) -> p a b", b=width)
                step(red(mx[:, 0:groups], v3, AX.X, ALU.max))
                step(tt(t3, v3, bc(mx[:, 0:groups].unsqueeze(2), [P, groups, width]), ALU.is_equal))
                step(tt(t3, t3, bc(weights.unsqueeze(1), [P, groups, width]), ALU.mult))
                step(red(mm[:, 0:groups], t3, AX.X, ALU.max))
                step(tt(o3, t3, bc(mm[:, 0:groups].unsqueeze(2), [P, groups, width]), ALU.is_equal))

            dve.wait_ge(s_b, 16)
            dve.wait_ge(s_c, 1)
            step(tt(te(grp), te(aff), bc(br.unsqueeze(1), [P, NT9, NE]), ALU.add))
            v = [grp.rearrange("p (x q) -> p x q", q=EPG)[:, :, q] for q in range(EPG)]
            tt(a_, v[0], v[1], ALU.max)
            tt(b_, v[0], v[1], ALU.min)
            tt(c_, v[2], v[3], ALU.max)
            step(tt(d_, v[2], v[3], ALU.min))
            tt(gs_, a_, c_, ALU.max)
            tt(goh, a_, c_, ALU.min)
            step(tt(b_, b_, d_, ALU.max))
            step(tt(goh, goh, b_, ALU.max))
            step(tt(gs_, gs_, goh, ALU.add))
            first_best(gs_, NT9 * NG, NT9, NG, w4, goh)
            step(ts(goh, goh, 1.0, -NEG, ALU.subtract, ALU.mult))
            step(tt(vm.rearrange("p (x q) -> p x q", q=EPG), grp.rearrange("p (x q) -> p x q", q=EPG),
                    bc(goh.unsqueeze(2), [P, NT9 * NG, EPG]), ALU.add))
            first_best(vm, NQ, NT9, NE, w16, oh1)
            step(nc.vector.scalar_tensor_tensor(out=vm, in0=oh1, scalar=NEG, in1=vm, op0=ALU.mult, op1=ALU.add))
            first_best(vm, NQ, NT9, NE, w16, oh2)
            for oh in (oh1, oh2):
                step(ts(te(oh)[:, TT, :], te(oh)[:, TT, :], rowmask, None, ALU.mult))
            tt(M, oh1, oh2, ALU.add).then_inc(s_m, 1)
            dve.wait_ge(s_cnt, 1)
            step(nc.vector.tensor_copy(tot, m.ps[:, 1, 0:NQ]))
            step(nc.vector.memset(tb[:, 0:NE], 0.0))
            for t in range(1, NT9):
                step(tt(te(tb)[:, t, :], te(tb)[:, t - 1, :], te(tot)[:, t - 1, :], ALU.add))
            step(tt(cnt, te(tb)[:, TT, :], te(tot)[:, TT, :], ALU.add))
            step(nc.vector.tensor_tensor_scan(off, ones[:, 0:NE], cnt, 0.0, ALU.mult, ALU.add))
            step(tt(off, off, cnt, ALU.subtract))
            step(tt(te(pos), te(tb), bc(off.unsqueeze(1), [P, NT9, NE]), ALU.add))
            step(tt(pos, pos, m.ps[:, 0, 0:NQ], ALU.add))
            for c, oh in enumerate((oh1, oh2)):
                step(tt(tmp, pos, oh, ALU.mult))
                step(red(slotf.rearrange("p (t c) -> p t c", c=2)[:, :, c], te(tmp), AX.X, ALU.add))
            nc.vector.tensor_copy(m.slots[:], slotf).then_inc(s_slot, 1)
            wt = m.pair_w
            for c, oh in enumerate((oh1, oh2)):
                step(tt(tmp, aff, oh, ALU.mult))
                step(red(wt[:, :, c], te(tmp), AX.X, ALU.add))
            step(tt(mx, wt[:, :, 0], wt[:, :, 1], ALU.add))
            step(ts(mx, mx, 1e-38, None, ALU.max))
            step(nc.vector.reciprocal(mm, mx))
            step(tt(wt, wt, bc(mm.unsqueeze(2), [P, NT9, 2]), ALU.mult))
            r1 = slice(0, 1)
            more = big1[r1, 0:NE * NKX].rearrange("p (e k) -> p e k", e=NE)
            step(tt(more, bc(cnt[r1].unsqueeze(2), [1, NE, NKX]), bc(kk[r1].unsqueeze(1), [1, NE, NKX]), ALU.is_gt))
            step(red(nt[r1], more, AX.X, ALU.add))
            step(ts(nt[r1], nt[r1], 1.0, None, ALU.max))
            step(nc.vector.tensor_tensor_scan(T[r1], ones[r1, 0:NE], nt[r1], 0.0, ALU.mult, ALU.add))
            step(tt(Tex[r1], T[r1], nt[r1], ALU.subtract))
            A3 = big1[r1].rearrange("p (x e) -> p x e", e=NE)
            B3 = big2[r1].rearrange("p (x e) -> p x e", e=NE)
            rowv, expert, new = (tabf[r1, i * NSTEP:(i + 1) * NSTEP] for i in range(3))
            full = [1, NSTEP, NE]
            tt(A3, bc(tau[r1].unsqueeze(2), full), bc(T[r1].unsqueeze(1), full), ALU.is_ge)
            step(tt(B3, bc(tau[r1].unsqueeze(2), full), bc(Tex[r1].unsqueeze(1), full), ALU.is_ge))
            step(red(expert, A3, AX.X, ALU.add))
            step(tt(B3, B3, A3, ALU.subtract))
            step(tt(A3, bc(tau[r1].unsqueeze(2), full), bc(Tex[r1].unsqueeze(1), full), ALU.is_equal))
            step(red(new, A3, AX.X, ALU.add))
            step(nc.vector.scalar_tensor_tensor(out=tq[r1], in0=Tex[r1], scalar=-float(P), in1=off[r1], op0=ALU.mult, op1=ALU.add))
            step(tt(A3, B3, bc(tq[r1].unsqueeze(1), full), ALU.mult))
            step(red(rowv, A3, AX.X, ALU.add))
            step(red(sumb[r1], B3, AX.X, ALU.add))
            step(tt(sumb[r1], sumb[r1], tau[r1], ALU.mult))
            step(nc.vector.scalar_tensor_tensor(out=rowv, in0=sumb[r1], scalar=float(P), in1=rowv, op0=ALU.mult, op1=ALU.add))
            for i in range(2):
                step(ts(tabf[r1, 3 * NSTEP + i:3 * NSTEP + i + 1], T[r1, NE - 1:NE], -3.0 * i, None, ALU.add))
            step(nc.vector.tensor_copy(m.table[:], tabf[r1]))


def experts(nc, m, io):
    xg, y = m.RW[:, 4096:4096 + DM], m.RW[:, 5120:5120 + DM]
    silu, h = m.RW[:, 11264:11264 + FE], m.RW[:, 11264 + FE:11264 + 2 * FE]
    xT = m.xg_parts.rearrange("p (h k c) -> p h k c", h=2, k=KT)
    hT = m.h_parts.rearrange("p (h k c) -> p h k c", h=2, k=FT)
    wparts = [w.rearrange("p (h c) -> p h c", h=2) for w in (m.wg_parts, m.wu_parts, m.wd_parts)]
    wg, wu = (w.rearrange("p h (k f) -> p h k f", k=KT) for w in wparts[:2])
    wd = wparts[2].rearrange("p h (k n) -> p h k n", k=FT)
    sem_in = (m.sem_gate, m.sem_up, m.sem_down)
    s_hi, s_lo = ([m.sem(f"e_{n}_{w}") for w in ("gate", "up", "down")] for n in ("high", "low"))
    s_x, s_t, s_xh, s_xl = (m.sem("e_rows_" + n) for n in ("in", "turned", "high", "low"))
    s_g, s_u, s_silu, s_h, s_ht, s_hh, s_hl = (m.sem("e_" + n) for n in (
        "gate", "up", "silu", "hidden", "hidden_turned", "hidden_high", "hidden_low"))
    s_d, s_y = m.sem("e_down"), m.sem("e_out")
    used = (s_g, s_u, s_d)
    PASSES = ((0, 0), (0, 1), (1, 0))
    HALF = 2048

    def after(eng, sem, value):
        if not (isinstance(value, int) and value <= 0):
            eng.wait_ge(sem, value)

    def entry(eng, kind, s, low, high):
        return eng.value_load(m.table[0:1, bass.ds(s + kind * NSTEP, 1)], min_val=low, max_val=high)

    def first_row(eng, s):
        return entry(eng, 0, s, 0, NPAIR)

    def expert_of(eng, s):
        return entry(eng, 1, s, 0, NE - 1)

    def where_new(eng, s):
        return eng.If(entry(eng, 2, s, 0, 1) > 0)

    def steps_of(eng):
        return eng.value_load(m.table[0:1, 3 * NSTEP:3 * NSTEP + 1], min_val=NE, max_val=NSTEP)

    def last_three(eng):
        a = eng.value_load(m.table[0:1, 3 * NSTEP + 1:3 * NSTEP + 2], min_val=NE - 3, max_val=NSTEP - 3)
        return a, a + 1, a + 2

    def banks(b, n):
        return m.ps[:, b:b + n, :].rearrange("p a c -> p (a c)")

    with nc.Block() as block:

        @block.sync
        def _(sp):
            def load(q, e):
                sp.wait_ge(s_lo[q], 2 * e)
                sp.wait_ge(sem_in[q], 16)
                load_third(m, io, sp, q, e)

            load_third(m, io, sp, DOWN, 0)
            load(GATE, 1)
            load(UP, 1)
            with sp.Fori(2, NE) as e:
                load(GATE, e)
                load(UP, e)
                load(DOWN, e - 1)
            load(DOWN, NE - 1)

        @block.gpsimd
        def _(pool):
            def load(s):
                row = first_row(pool, s)
                after(pool, s_t, s)
                nc.gpsimd.dma_start(xg, m.xs_dram[bass.ds(row, P), :]).then_inc(s_x, 16)

            def store(s):
                row = first_row(pool, s)
                pool.wait_ge(m.sem_stored, 16 * s + 16)
                pool.wait_ge(s_y, s + 1)
                nc.gpsimd.dma_start(m.ys_dram[bass.ds(row, P), :], y).then_inc(m.sem_stored, 16)

            for s in range(3):
                load(s)
            n = steps_of(pool)
            with pool.Fori(3, n) as s:
                load(s)
                store(s - 3)
            for s in last_three(pool):
                store(s)
            pool.wait_ge(m.sem_stored, 16 * n + 16)

        @block.tensor
        def _(pe):
            def turn_rows(s):
                pe.wait_ge(s_x, 16 * s + 16)
                for k in range(KT):
                    last = nc.tensor.transpose(m.ps[:, 2 + k // 4, (k % 4) * P:(k % 4 + 1) * P], xg[:, k:DM:KT], m.ident[:])
                last.then_inc(s_t, 1)

            def turn_hidden(s):
                pe.wait_ge(s_h, s + 1)
                for k in range(FT):
                    last = nc.tensor.transpose(m.ps[:, 4, k * P:(k + 1) * P], h[:, k:FE:FT], m.ident[:])
                last.then_inc(s_ht, 1)

            def products(out, x, w, count, columns):
                for k in range(count):
                    for i, (a, b) in enumerate(PASSES):
                        last = nc.tensor.matmul(out, x[:, a, k, :], w[:, b, k, columns],
                                                start=(k == 0 and i == 0), stop=(k == count - 1 and i == 2))
                return last

            def gate(s):
                ready = 2 * expert_of(pe, s) + 2
                pe.wait_ge(s_lo[GATE], ready)
                pe.wait_ge(s_xl, s + 1)
                after(pe, s_silu, s)
                products(m.ps[:, 0, :], xT, wg, KT, slice(0, FE)).then_inc(s_g, 1)

            def up(s):
                ready = 2 * expert_of(pe, s) + 2
                pe.wait_ge(s_lo[UP], ready)
                after(pe, s_h, s)
                products(m.ps[:, 1, :], xT, wu, KT, slice(0, FE)).then_inc(s_u, 1)

            def down(s):
                ready = 2 * expert_of(pe, s) + 2
                pe.wait_ge(s_lo[DOWN], ready)
                pe.wait_ge(s_hl, s + 1)
                after(pe, s_y, s)
                for c in range(2):
                    last = products(m.ps[:, 5 + c, :], hT, wd, FT, slice(c * 512, (c + 1) * 512))
                last.then_inc(s_d, 1)

            turn_rows(0)
            gate(0)
            up(0)
            turn_rows(1)
            turn_hidden(0)
            gate(1)
            n = steps_of(pe)
            with pe.Fori(2, n) as s:
                up(s - 1)
                turn_rows(s)
                down(s - 2)
                turn_hidden(s - 1)
                gate(s)
            _, last_but_one, last_one = last_three(pe)
            up(last_one)
            down(last_but_one)
            turn_hidden(last_one)
            down(last_one)

        @block.scalar
        def _(act):
            def high(q, s):
                with where_new(act, s):
                    there = 16 * expert_of(act, s) + 16
                    act.wait_ge(sem_in[q], there)
                    after(act, used[q], s)
                    for i in range(2):
                        part = slice(i * HALF, (i + 1) * HALF)
                        nc.scalar.copy(wparts[q][:, 0, part], raw_third(m, q)[:, part]).then_inc(s_hi[q], 1)

            def rows_high(s):
                act.wait_ge(s_t, s + 1)
                nc.scalar.copy(xT[:, 0].rearrange("p k c -> p (k c)"), banks(2, 2)).then_inc(s_xh, 1)

            def hidden_high(s):
                act.wait_ge(s_ht, s + 1)
                nc.scalar.copy(hT[:, 0].rearrange("p k c -> p (k c)"), banks(4, 1)).then_inc(s_hh, 1)

            def gated(s):
                act.wait_ge(s_g, s + 1)
                after(act, s_h, s)
                nc.scalar.activation(silu, m.ps[:, 0, :], ACT.Silu).then_inc(s_silu, 1)

            def keep(s):
                act.wait_ge(s_d, s + 1)
                act.wait_ge(m.sem_stored, 16 * s + 16)
                nc.scalar.copy(y, banks(5, 2)).then_inc(s_y, 1)

            high(GATE, 0)
            rows_high(0)
            high(UP, 0)
            gated(0)

            def body(s):
                high(GATE, s)
                rows_high(s)
                high(UP, s)
                if not isinstance(s, int):
                    keep(s - 2)
                hidden_high(s - 1)
                high(DOWN, s - 1)
                gated(s)

            body(1)
            n = steps_of(act)
            with act.Fori(2, n) as s:
                body(s)
            _, last_but_one, last_one = last_three(act)
            keep(last_but_one)
            hidden_high(last_one)
            high(DOWN, last_one)
            keep(last_one)

        @block.vector
        def _(dve):
            def low(q, s):
                with where_new(dve, s):
                    split = 2 * expert_of(dve, s)
                    for i in range(2):
                        part = slice(i * HALF, (i + 1) * HALF)
                        dve.wait_ge(s_hi[q], split + (i + 1))
                        nc.vector.tensor_tensor(wparts[q][:, 1, part], raw_third(m, q)[:, part], wparts[q][:, 0, part],
                                                ALU.subtract).then_inc(s_lo[q], 1)

            def rows_low(s):
                dve.wait_ge(s_xh, s + 1)
                nc.vector.tensor_tensor(xT[:, 1].rearrange("p k c -> p (k c)"), banks(2, 2),
                                        xT[:, 0].rearrange("p k c -> p (k c)"), ALU.subtract).then_inc(s_xl, 1)

            def hidden(s):
                dve.wait_ge(s_silu, s + 1)
                dve.wait_ge(s_u, s + 1)
                after(dve, s_ht, s)
                nc.vector.tensor_tensor(h, silu, m.ps[:, 1, :], ALU.mult).then_inc(s_h, 1)

            def hidden_low(s):
                dve.wait_ge(s_hh, s + 1)
                nc.vector.tensor_tensor(hT[:, 1].rearrange("p k c -> p (k c)"), banks(4, 1),
                                        hT[:, 0].rearrange("p k c -> p (k c)"), ALU.subtract).then_inc(s_hl, 1)

            low(GATE, 0)
            rows_low(0)
            low(UP, 0)

            def body(s):
                low(GATE, s)
                hidden(s - 1)
                rows_low(s)
                low(UP, s)
                hidden_low(s - 1)
                low(DOWN, s - 1)

            body(1)
            n = steps_of(dve)
            with dve.Fori(2, n) as s:
                body(s)
            _, last_but_one, last_one = last_three(dve)
            hidden(last_one)
            hidden_low(last_one)
            low(DOWN, last_one)


def combine(nc, m, io):
    yg = [[m.R3[:, (2 * t + c) * DM:(2 * t + c + 1) * DM] for c in range(2)] for t in range(NT9)]
    gain, bias = m.RK[:, 0:DM], m.RK[:, DM:2 * DM]
    sc = m.RK[:, 2 * DM:2 * DM + 20 * NT9].rearrange("p (t c) -> p t c", t=NT9)
    s_c, s_m1, s_z = m.sem("c_consts"), m.sem("c_scaled"), m.sem("c_added")
    s_g = [m.sem(f"c_gathered{t}") for t in range(NT9)]
    s_x1 = [m.sem(f"c_x1_{t}") for t in range(TT)]
    s_stat, s_mv, s_eps, s_rstd, s_norm = (m.sem("c_" + n) for n in ("stats", "moments", "eps", "rstd", "normal"))
    s_gain, s_ye, s_yo, s_out = m.sem("c_gain"), m.sem("c_y_even"), m.sem("c_y_odd"), m.sem("c_out")
    s_nm = m.sem("c_shift")
    yp = io["y_prompt"].rearrange("a (t p) d -> p (a t) d", p=P)
    ys = io["y_sample"].rearrange("b t d -> (b t) d")
    with nc.Block() as block:

        @block.sync
        def _(sp):
            sp.dma_start(gain, io["ln2_g"].rearrange("l d -> (l d)").partition_broadcast(P)).then_inc(s_c, 16)
            sp.dma_start(bias, io["ln2_b"].rearrange("l d -> (l d)").partition_broadcast(P)).then_inc(s_c, 16)
            for t in range(TT):
                sp.dma_start(m.x1[t], m.x1_dram[t * P:(t + 1) * P, :]).then_inc(s_x1[t], 16)
            for t in range(NT9):
                sp.wait_ge((s_ye, s_yo)[t % 2], t // 2 + 1)
                sp.dma_start(yp[:, t, :] if t < TT else ys, m.x1[t]).then_inc(s_out, 16)
            sp.wait_ge(s_out, 16 * NT9)

        @block.gpsimd
        def _(pool):
            def scale_rows(t):
                n = rows_of(t)
                pool.wait_ge(s_norm, t + 1)
                nc.gpsimd.tensor_tensor(m.x1[t], m.x1[t], gain[0:n], ALU.mult).then_inc(s_gain, 1)
                if t % 2 == 1:
                    pool.wait_ge(s_gain, t + 1)
                    nc.gpsimd.tensor_tensor(m.x1[t], m.x1[t], bias[0:n], ALU.add).then_inc(s_yo, 1)

            for t in range(NT9):
                n = rows_of(t)
                for c in range(2):
                    col = 2 * t + c
                    nc.gpsimd.indirect_dma_start(
                        out=yg[t][c][0:n], out_offset=None, in_=m.ys_dram[0:NPAIR, :],
                        in_offset=bass.IndirectOffsetOnAxis(ap=m.slots[0:n, col:col + 1], axis=0)).then_inc(s_g[t], 16)
            pool.wait_ge(s_c, 32)
            for t in range(NT9):
                n = rows_of(t)
                inverse_deviation(nc, m, pool, n, sc[:, t, 12:14], sc[:, t, 14:15], s_mv, s_eps, s_rstd, t)
                if t >= 1:
                    scale_rows(t - 1)
            scale_rows(TT)

        @block.scalar
        def _(act):
            def normal(t):
                n = rows_of(t)
                act.wait_ge(s_nm, t + 1)
                nc.scalar.activation(m.x1[t], m.x1[t], ACT.Identity, bias=sc[0:n, t, 15:16],
                                     scale=sc[0:n, t, 14:15]).then_inc(s_norm, 1)

            def weigh(t):
                n = rows_of(t)
                act.wait_ge(s_g[t], 32)
                nc.scalar.mul(yg[t][0][0:n], yg[t][0][0:n], m.pair_w[0:n, t, 0:1]).then_inc(s_m1, 1)

            for t in range(3):
                weigh(t)
            for t in range(NT9):
                normal(t)
                if t + 3 < NT9:
                    weigh(t + 3)

        @block.vector
        def _(dve):
            stt = nc.vector.scalar_tensor_tensor

            def add(t):
                n = rows_of(t)
                dve.wait_ge(s_m1, t + 1)
                if t < TT:
                    dve.wait_ge(s_x1[t], 16)
                stt(out=m.x1[t], in0=m.x1[t], scalar=ALPHA, in1=yg[t][0][0:n], op0=ALU.mult, op1=ALU.add).then_inc(s_z, 1)
                dve.wait_ge(s_z, 2 * t + 1)
                stt(out=m.x1[t], in0=yg[t][1][0:n], scalar=m.pair_w[0:n, t, 1:2], in1=m.x1[t], op0=ALU.mult,
                    op1=ALU.add).then_inc(s_z, 1)
                dve.wait_ge(s_z, 2 * t + 2)
                nc.vector.bn_stats(sc[0:n, t, 0:6], m.x1[t][:, 0:512])
                nc.vector.bn_stats(sc[0:n, t, 6:12], m.x1[t][:, 512:1024]).then_inc(s_stat, 1)
                dve.wait_ge(s_stat, t + 1)
                nc.vector.bn_aggr(sc[0:n, t, 12:14], sc[0:n, t, 0:12]).then_inc(s_mv, 1)

            def shift(t):
                n = rows_of(t)
                dve.wait_ge(s_rstd, t + 1)
                stt(out=sc[0:n, t, 15:16], in0=sc[0:n, t, 12:13], scalar=-1.0, in1=sc[0:n, t, 14:15], op0=ALU.mult,
                    op1=ALU.mult).then_inc(s_nm, 1)

            def bias_rows(t):
                n = rows_of(t)
                dve.wait_ge(s_gain, t + 1)
                nc.vector.tensor_tensor(m.x1[t], m.x1[t], bias[0:n], ALU.add).then_inc(s_ye, 1)

            dve.wait_ge(s_c, 32)
            for t in range(NT9 + 2):
                if t < NT9:
                    add(t)
                if 1 <= t <= NT9:
                    shift(t - 1)
                if t >= 2 and t % 2 == 0:
                    bias_rows(t - 2)


_INS = ["x_prompt", "x_sample", "cache_kv", "cache_win", "page_table", "w_in", "gmlp_ln_g", "gmlp_ln_b", "gmlp_ws",
        "gmlp_bs", "cmp_pos", "cmp_w1", "cmp_w2", "w_branch_a", "w_branch_b", "w_out", "ln1_g", "ln1_b", "ln2_g",
        "ln2_b", "w_router", "b_router", "w_gate", "w_up", "w_down"]
_OUTS = [("y_prompt", (1, SEQ, DM)), ("y_sample", (NB, 1, DM)), ("kv_rows_prompt", (1, 1, SEQ, 4, NKV, HD)),
         ("win_prompt", (1, 1, WINDOW, 2, NKV, HD)), ("kv_rows_sample", (NB, 1, 1, 4, NKV, HD)),
         ("win_sample", (NB, 1, PAST, 2, NKV, HD)), ("gmlp_v_sample", (NB, 1, 1, DM))]


def program(nc, io, upto=99):
    with ExitStack() as ctx:
        m = Memory(nc, ctx)
        fw, ci, si = FirstWeights(m, io), CompressInputs(m), SampleInputs(m)
        stages = [lambda: load_and_turn_x(nc, m, io, fw), lambda: project_kv(nc, m, io, fw),
                  lambda: project_q(nc, m, io, fw, ci),
                  lambda: compress_keys(nc, m, io, fw, ci, si), lambda: attend_samples(nc, m, fw, si),
                  lambda: attend_prompt(nc, m),
                  lambda: gmlp_values(nc, m, io, fw), lambda: gmlp_gate(nc, m, io, fw),
                  lambda: merge(nc, m, io, fw),
                  lambda: output_and_router(nc, m, io), lambda: route_and_dispatch(nc, m, io),
                  lambda: experts(nc, m, io), lambda: combine(nc, m, io)]
        for stage in stages[:upto]:
            stage()
            if stage is stages[5]:
                m.clear_semaphores()
                fw.second_part()


def kernel(**inputs):
    from concourse import bacc
    from concourse.bass_utils import run_bass_kernel_spmd

    nc = bacc.Bacc("TRN2", target_bir_lowering=False, num_devices=1)
    arrays, io = {}, {}
    for name in _INS:
        a = np.ascontiguousarray(inputs[name])
        arrays[f"in_{name}"] = a
        io[name] = nc.dram_tensor(f"in_{name}", a.shape, mybir.dt.from_np(a.dtype), kind="ExternalInput").ap()
    for name, shape in _OUTS:
        io[name] = nc.dram_tensor(f"out_{name}", shape, F32, kind="ExternalOutput").ap()
    program(nc, io)
    r = run_bass_kernel_spmd(nc, [arrays], core_ids=[0])
    return tuple(r.results[0][f"out_{name}"] for name, _ in _OUTS)
```
